# Optimizing a Trainium2 kernel written in Bass

```python
import math
import jax, jax.numpy as jnp
from jax import lax
import numpy as np
import jax
import jax.numpy as jnp

D_MODEL = 1024
BATCH = 1
SEQ = 256
DEPTH = 1

GRID_W = 64
CTX_LEN = 256
HEAD_DIM = 64
ROPE_THETA = 10000.0
NORM_EPS = 1e-6
Q_BLOCK = 128
DIFF_HEADS = 4
DIFF_V_DIM = 2 * HEAD_DIM
DIFF_WIDTH = DIFF_HEADS * DIFF_V_DIM
GQA_Q_HEADS = 8
GQA_KV_HEADS = 2
GQA_GROUP = GQA_Q_HEADS // GQA_KV_HEADS
GQA_WIDTH = GQA_Q_HEADS * HEAD_DIM
MIX_WIDTH = DIFF_WIDTH + GQA_WIDTH
GQA_KV_WIDTH = GQA_KV_HEADS * HEAD_DIM
IN_COLS = 3 * DIFF_WIDTH + GQA_WIDTH + 2 * GQA_KV_WIDTH
_IN_SPLITS = (DIFF_WIDTH, 2 * DIFF_WIDTH, 3 * DIFF_WIDTH,
              3 * DIFF_WIDTH + GQA_WIDTH, 3 * DIFF_WIDTH + GQA_WIDTH + GQA_KV_WIDTH)
PEER_HEADS = 8
PEER_N_KEYS = 128
PEER_N_EXPERTS = PEER_N_KEYS * PEER_N_KEYS
PEER_QUERY_DIM = 256
PEER_HALF = PEER_QUERY_DIM // 2
PEER_TOPK = 16
PEER_CHUNK = 128


def rmsnorm(x, g):
    xf = x.astype(jnp.float32)
    y = xf * lax.rsqrt(jnp.mean(xf * xf, axis=-1, keepdims=True) + NORM_EPS)
    return (y * g.astype(jnp.float32)).astype(x.dtype)

def modulate(h, shift, scale):
    return h * (1 + scale) + shift

def _rope_axis(x, pos):
    d = x.shape[-1]
    half = d // 2
    freqs = ROPE_THETA ** (-jnp.arange(half, dtype=jnp.float32) / half)
    ang = pos.astype(jnp.float32)[:, None] * freqs[None, :]
    shape = (1, x.shape[1]) + (1,) * (x.ndim - 3) + (half,)
    cos = jnp.cos(ang).reshape(shape).astype(x.dtype)
    sin = jnp.sin(ang).reshape(shape).astype(x.dtype)
    x1, x2 = x[..., :half], x[..., half:]
    return jnp.concatenate([x1 * cos - x2 * sin, x1 * sin + x2 * cos], axis=-1)

def rope2d(x):
    n = x.shape[1]
    rows = n // GRID_W
    row_pos = jnp.broadcast_to(jnp.arange(rows, dtype=jnp.int32)[:, None], (rows, GRID_W)).reshape(-1)
    col_pos = jnp.broadcast_to(jnp.arange(GRID_W, dtype=jnp.int32)[None, :], (rows, GRID_W)).reshape(-1)
    d = x.shape[-1] // 2
    return jnp.concatenate([_rope_axis(x[..., :d], row_pos), _rope_axis(x[..., d:], col_pos)], axis=-1)

def attend(q, k, v):
    B, S, Hk, G, d = q.shape
    nb = S // Q_BLOCK
    qb = q.reshape(B, nb, Q_BLOCK, Hk, G, d).swapaxes(0, 1)
    scale = d ** -0.5

    def one(qblk):
        s = jnp.einsum('bqhgd,bkhd->bhgqk', qblk, k, preferred_element_type=jnp.float32) * scale
        p = jax.nn.softmax(s, axis=-1).astype(v.dtype)
        return jnp.einsum('bhgqk,bkhe->bqhge', p, v)

    o = lax.map(one, qb)
    return o.swapaxes(0, 1).reshape(B, S, Hk, G, v.shape[-1])

def _mixer_heads(p):
    B, S, _ = p.shape
    dq, dk, dv, gq, gk, gv = jnp.split(p, _IN_SPLITS, axis=-1)
    return (dq.reshape(B, S, DIFF_HEADS, 2, HEAD_DIM),
            dk.reshape(B, S, DIFF_HEADS, 2, HEAD_DIM),
            dv.reshape(B, S, DIFF_HEADS, DIFF_V_DIM),
            gq.reshape(B, S, GQA_Q_HEADS, HEAD_DIM),
            gk.reshape(B, S, GQA_KV_HEADS, HEAD_DIM),
            gv.reshape(B, S, GQA_KV_HEADS, HEAD_DIM))

def _mix_queries(dq, gq, dk, dv, gk, gv, lam, lambda_init, subln_g, w_out):
    B, S = dq.shape[:2]
    o1 = attend(dq[:, :, :, 0, None, :], dk[:, :, :, 0, :], dv)
    o2 = attend(dq[:, :, :, 1, None, :], dk[:, :, :, 1, :], dv)
    od = (o1 - lam.astype(o1.dtype) * o2)[:, :, :, 0, :]
    od = rmsnorm(od, subln_g) * (1.0 - lambda_init)
    og = attend(gq.reshape(B, S, GQA_KV_HEADS, GQA_GROUP, HEAD_DIM), gk, gv)
    o = jnp.concatenate([od.reshape(B, S, DIFF_WIDTH), og.reshape(B, S, GQA_WIDTH)], axis=-1)
    return o @ w_out

def peer(h, w_q, subkeys, u, v):
    B, S, D = h.shape
    xs = h.reshape(-1, PEER_CHUNK, D)

    def one(xc):
        C = xc.shape[0]
        q = (xc @ w_q).reshape(C, PEER_HEADS, 2, PEER_HALF)
        s = jnp.einsum('chpd,hpnd->chpn', q, subkeys, preferred_element_type=jnp.float32)
        sv, si = lax.top_k(s, PEER_TOPK)
        cand = sv[:, :, 0, :, None] + sv[:, :, 1, None, :]
        cand_id = si[:, :, 0, :, None] * PEER_N_KEYS + si[:, :, 1, None, :]
        best, pos = lax.top_k(cand.reshape(C, PEER_HEADS, PEER_TOPK * PEER_TOPK), PEER_TOPK)
        ids = jnp.take_along_axis(cand_id.reshape(C, PEER_HEADS, PEER_TOPK * PEER_TOPK), pos, axis=-1)
        g = jax.nn.softmax(best, axis=-1)
        ue = jnp.take(u, ids, axis=0)
        ve = jnp.take(v, ids, axis=0)
        a = jax.nn.gelu(jnp.einsum('cd,chkd->chk', xc, ue), approximate=False)
        return jnp.einsum('chk,chkd->cd', (g * a).astype(xc.dtype), ve)

    return lax.map(one, xs).reshape(B, S, D)

def first_inputs(seed: int = 0) -> dict:
    key = jax.random.key(seed)
    ks = jax.random.split(key, 24)
    D = D_MODEL
    nrm = lambda k, shape, s: jax.random.normal(k, shape, jnp.float32) * s
    return {
        "x": nrm(ks[0], (BATCH, SEQ, D), 1.0),
        "c": nrm(ks[1], (BATCH, D), 1.0),
        "ctx": nrm(ks[2], (BATCH, CTX_LEN, D), 1.0),
        "c_ctx": nrm(ks[3], (D,), 1.0),
        "w_mod": nrm(ks[4], (DEPTH, D, 6 * D), 0.5 * D ** -0.5),
        "b_mod": nrm(ks[5], (DEPTH, 6 * D), 0.01),
        "norm1_g": 1.0 + nrm(ks[6], (DEPTH, D), 0.02),
        "norm2_g": 1.0 + nrm(ks[7], (DEPTH, D), 0.02),
        "w_in": nrm(ks[8], (DEPTH, D, IN_COLS), D ** -0.5),
        "w_out": nrm(ks[9], (DEPTH, MIX_WIDTH, D), MIX_WIDTH ** -0.5),
        "diff_lq1": nrm(ks[10], (DEPTH, HEAD_DIM), 0.1),
        "diff_lk1": nrm(ks[11], (DEPTH, HEAD_DIM), 0.1),
        "diff_lq2": nrm(ks[12], (DEPTH, HEAD_DIM), 0.1),
        "diff_lk2": nrm(ks[13], (DEPTH, HEAD_DIM), 0.1),
        "diff_subln_g": 1.0 + nrm(ks[14], (DEPTH, DIFF_V_DIM), 0.02),
        "gqa_q_norm_g": 1.0 + nrm(ks[15], (DEPTH, HEAD_DIM), 0.02),
        "gqa_k_norm_g": 1.0 + nrm(ks[16], (DEPTH, HEAD_DIM), 0.02),
        "peer_wq": nrm(ks[17], (DEPTH, D, PEER_HEADS * PEER_QUERY_DIM), D ** -0.5),
        "peer_subkeys": nrm(ks[18], (DEPTH, PEER_HEADS, 2, PEER_N_KEYS, PEER_HALF), PEER_HALF ** -0.5),
        "peer_u": nrm(ks[19], (DEPTH, PEER_N_EXPERTS, D), D ** -0.5),
        "peer_v": nrm(ks[20], (DEPTH, PEER_N_EXPERTS, D), (PEER_HEADS * PEER_TOPK) ** -0.5),
        "final_norm_g": 1.0 + nrm(ks[21], (D,), 0.02),
    }

def first_block(x, c, ctx, c_ctx, w_mod, b_mod, norm1_g, norm2_g, w_in, w_out,
              diff_lq1, diff_lk1, diff_lq2, diff_lk2, diff_subln_g,
              gqa_q_norm_g, gqa_k_norm_g, peer_wq, peer_subkeys, peer_u, peer_v,
              final_norm_g):
    for i in range(DEPTH):
        last = i == DEPTH - 1
        lambda_init = 0.8 - 0.6 * math.exp(-0.3 * i)
        mod_x = (jax.nn.silu(c) @ w_mod[i] + b_mod[i])[:, None, :]
        mod_c = jax.nn.silu(c_ctx) @ w_mod[i] + b_mod[i]
        sh1x, sc1x, g1x, sh2x, sc2x, g2x = jnp.split(mod_x, 6, axis=-1)
        sh1c, sc1c, g1c, sh2c, sc2c, g2c = jnp.split(mod_c, 6, axis=-1)

        hx = modulate(rmsnorm(x, norm1_g[i]), sh1x, sc1x)
        hc = modulate(rmsnorm(ctx, norm1_g[i]), sh1c, sc1c)
        c_dq, c_dk, c_dv, c_gq, c_gk, c_gv = _mixer_heads(hc @ w_in[i])
        x_dq, x_dk, x_dv, x_gq, x_gk, x_gv = _mixer_heads(hx @ w_in[i])
        c_gq = rmsnorm(c_gq, gqa_q_norm_g[i])
        c_gk = rmsnorm(c_gk, gqa_k_norm_g[i])
        x_gq = rope2d(rmsnorm(x_gq, gqa_q_norm_g[i]))
        x_gk = rope2d(rmsnorm(x_gk, gqa_k_norm_g[i]))
        x_dq = rope2d(x_dq)
        x_dk = rope2d(x_dk)
        lam = (jnp.exp(jnp.sum(diff_lq1[i].astype(jnp.float32) * diff_lk1[i].astype(jnp.float32)))
               - jnp.exp(jnp.sum(diff_lq2[i].astype(jnp.float32) * diff_lk2[i].astype(jnp.float32)))
               + lambda_init)
        out_x = _mix_queries(x_dq, x_gq,
                             jnp.concatenate([c_dk, x_dk], axis=1),
                             jnp.concatenate([c_dv, x_dv], axis=1),
                             jnp.concatenate([c_gk, x_gk], axis=1),
                             jnp.concatenate([c_gv, x_gv], axis=1),
                             lam, lambda_init, diff_subln_g[i], w_out[i])
        if not last:
            out_c = _mix_queries(c_dq, c_gq, c_dk, c_dv, c_gk, c_gv,
                                 lam, lambda_init, diff_subln_g[i], w_out[i])
            ctx = ctx + g1c * out_c
        x = x + g1x * out_x

        hx2 = modulate(rmsnorm(x, norm2_g[i]), sh2x, sc2x)
        x = x + g2x * peer(hx2, peer_wq[i], peer_subkeys[i], peer_u[i], peer_v[i])
        if not last:
            hc2 = modulate(rmsnorm(ctx, norm2_g[i]), sh2c, sc2c)
            ctx = ctx + g2c * peer(hc2, peer_wq[i], peer_subkeys[i], peer_u[i], peer_v[i])
    return rmsnorm(x, final_norm_g)


CONV_WIDTH = 512
CONV_K = 31
HGRN_HEADS = 4
HGRN_DK = 128
HGRN_DV = 128
HGRN_KW = HGRN_HEADS * HGRN_DK
HGRN_VW = HGRN_HEADS * HGRN_DV
CHUNK = 64
MEM_LEN = 256
XA_HEADS = 4
XA_HEAD_DIM = D_MODEL // XA_HEADS
N_GROUPS = 4
EXPERTS_PER_GROUP = 8
N_EXPERTS = N_GROUPS * EXPERTS_PER_GROUP
TOP_K = 2
D_FF = 512
EPS = 1e-6
ROUTER_BIAS_SCALE = 0.01

_COLS = (CONV_WIDTH, CONV_WIDTH, HGRN_KW, HGRN_KW, HGRN_VW, HGRN_VW, D_MODEL, D_MODEL)
IN_COLS_2 = sum(_COLS)
SPLITS = [sum(_COLS[:i]) for i in range(1, len(_COLS))]


def rms_norm(x, g):
    xf = x.astype(jnp.float32)
    y = xf * lax.rsqrt(jnp.mean(xf * xf, axis=-1, keepdims=True) + EPS)
    return (y * g.astype(jnp.float32)).astype(x.dtype)

def layer_norm(x, g, b):
    xf = x.astype(jnp.float32)
    mu = jnp.mean(xf, axis=-1, keepdims=True)
    var = jnp.mean(jnp.square(xf - mu), axis=-1, keepdims=True)
    y = (xf - mu) * lax.rsqrt(var + EPS)
    return (y * g.astype(jnp.float32) + b.astype(jnp.float32)).astype(x.dtype)

def causal_depthwise_conv(u, w, b):
    y = lax.conv_general_dilated(
        u, w[:, None, :].astype(u.dtype), window_strides=(1,),
        padding=[(CONV_K - 1, 0)], dimension_numbers=('NWC', 'WIO', 'NWC'),
        feature_group_count=u.shape[-1])
    return y + b.astype(u.dtype)

def conformer_conv_branch(a, gate, w_dw, b_dw, ln_g, ln_b, w_proj):
    u = a * jax.nn.sigmoid(gate)
    u = causal_depthwise_conv(u, w_dw, b_dw)
    u = jax.nn.silu(layer_norm(u, ln_g, ln_b))
    return u @ w_proj

def hgrn2_chunkwise(q, k, v, logf):
    b, s, h, dk = q.shape
    dv = v.shape[-1]
    nc = s // CHUNK

    def to_chunks(t):
        return t.reshape(b, nc, CHUNK, h, t.shape[-1]).transpose(1, 0, 3, 2, 4)

    causal = jnp.tril(jnp.ones((CHUNK, CHUNK), dtype=bool))[None, None, :, :, None]

    def step(state, inp):
        qb, kb, vb, fb = inp
        cum = jnp.cumsum(fb, axis=2)
        o_inter = jnp.einsum('bhtk,bhkv->bhtv', qb * jnp.exp(cum), state)
        diff = cum[:, :, :, None, :] - cum[:, :, None, :, :]
        decay = jnp.exp(jnp.where(causal, diff, -jnp.inf))
        scores = jnp.einsum('bhtk,bhtsk,bhsk->bhts', qb, decay, kb)
        o = o_inter + jnp.einsum('bhts,bhsv->bhtv', scores, vb)
        last = cum[:, :, -1:, :]
        state = (jnp.exp(last[:, :, 0, :])[..., None] * state
                 + jnp.einsum('bhsk,bhsv->bhkv', kb * jnp.exp(last - cum), vb))
        return state, o

    s0 = jnp.zeros((b, h, dk, dv), jnp.float32)
    _, o = lax.scan(step, s0, (to_chunks(q), to_chunks(k), to_chunks(v), to_chunks(logf)))
    return o.transpose(1, 0, 3, 2, 4).reshape(b, s, h, dv)

def hgrn2_branch(q_raw, f_raw, i_raw, g_raw, lower_bound, onorm_g, w_o):
    b, s, _ = q_raw.shape

    def heads(t, d):
        return t.reshape(b, s, HGRN_HEADS, d)

    f = lower_bound + (1.0 - lower_bound) * jax.nn.sigmoid(f_raw.astype(jnp.float32))
    q = jax.nn.silu(q_raw.astype(jnp.float32))
    o = hgrn2_chunkwise(heads(q, HGRN_DK), heads(1.0 - f, HGRN_DK),
                        heads(i_raw.astype(jnp.float32), HGRN_DV), heads(jnp.log(f), HGRN_DK))
    o = rms_norm(o, onorm_g) * jax.nn.silu(heads(g_raw.astype(jnp.float32), HGRN_DV))
    return o.reshape(b, s, HGRN_VW).astype(q_raw.dtype) @ w_o

def memory_cross_attention(h, mem_n, w_q, w_k, w_v, w_o):
    b, s, d = h.shape
    m = mem_n.shape[1]
    q = (h @ w_q).reshape(b, s, XA_HEADS, XA_HEAD_DIM)
    k = (mem_n @ w_k).reshape(b, m, XA_HEADS, XA_HEAD_DIM)
    v = (mem_n @ w_v).reshape(b, m, XA_HEADS, XA_HEAD_DIM)
    scores = jnp.einsum('bshd,bmhd->bhsm', q, k).astype(jnp.float32) * (XA_HEAD_DIM ** -0.5)
    p = jax.nn.softmax(scores, axis=-1).astype(v.dtype)
    o = jnp.einsum('bhsm,bmhd->bshd', p, v).reshape(b, s, d)
    return o @ w_o

def hierarchical_moe(h, w_group, b_group, w_expert, b_expert, w_gate, w_up, w_down):
    b, s, d = h.shape
    t = h.reshape(b * s, d)
    n = t.shape[0]
    group_probs = jax.nn.softmax((t @ w_group).astype(jnp.float32) + b_group.astype(jnp.float32), axis=-1)
    g_p, g_idx = lax.top_k(group_probs, 1)
    e_logits = ((t @ w_expert).astype(jnp.float32) + b_expert.astype(jnp.float32))
    e_logits = e_logits.reshape(n, N_GROUPS, EXPERTS_PER_GROUP)
    in_group = jnp.take_along_axis(e_logits, g_idx[:, :, None], axis=1)[:, 0]
    e_p, e_idx = lax.top_k(jax.nn.softmax(in_group, axis=-1), TOP_K)
    e_p = e_p / jnp.sum(e_p, axis=-1, keepdims=True)
    weights = g_p * e_p
    expert_ids = g_idx * EXPERTS_PER_GROUP + e_idx
    combine = jnp.zeros((n, N_EXPERTS), jnp.float32).at[
        jnp.arange(n)[:, None], expert_ids].add(weights).astype(t.dtype)
    y = jnp.zeros_like(t)
    for e in range(N_EXPERTS):
        hid = jax.nn.silu(t @ w_gate[e]) * (t @ w_up[e])
        y = y + combine[:, e:e + 1] * (hid @ w_down[e])
    return y.reshape(b, s, d)

def second_inputs(seed: int = 0) -> dict:
    key = jax.random.key(seed)
    ks = iter(jax.random.split(key, 32))

    def nrm(shape, fan_in):
        return jax.random.normal(next(ks), shape, jnp.float32) * (fan_in ** -0.5)

    def gain(shape):
        return 1.0 + 0.02 * jax.random.normal(next(ks), shape, jnp.float32)

    def small(shape, scale):
        return scale * jax.random.normal(next(ks), shape, jnp.float32)

    L = DEPTH
    return {
        'x': jax.random.normal(next(ks), (BATCH, SEQ, D_MODEL), jnp.float32),
        'mem': jax.random.normal(next(ks), (BATCH, MEM_LEN, D_MODEL), jnp.float32),
        'norm_mix_g': gain((L, D_MODEL)),
        'w_in': nrm((L, D_MODEL, IN_COLS_2), D_MODEL),
        'conv_w': nrm((L, CONV_K, CONV_WIDTH), CONV_K),
        'conv_b': small((L, CONV_WIDTH), 0.02),
        'conv_ln_g': gain((L, CONV_WIDTH)),
        'conv_ln_b': small((L, CONV_WIDTH), 0.02),
        'conv_w_out': nrm((L, CONV_WIDTH, D_MODEL), CONV_WIDTH),
        'hgrn_lb_logits': small((L + 1, HGRN_KW), 0.5),
        'hgrn_onorm_g': gain((L, HGRN_DV)),
        'hgrn_w_out': nrm((L, HGRN_VW, D_MODEL), HGRN_VW),
        'w_mix_out': nrm((L, D_MODEL, D_MODEL), D_MODEL),
        'norm_xa_g': gain((L, D_MODEL)),
        'norm_mem_g': gain((L, D_MODEL)),
        'xa_w_q': nrm((L, D_MODEL, D_MODEL), D_MODEL),
        'xa_w_k': nrm((L, D_MODEL, D_MODEL), D_MODEL),
        'xa_w_v': nrm((L, D_MODEL, D_MODEL), D_MODEL),
        'xa_w_o': nrm((L, D_MODEL, D_MODEL), D_MODEL),
        'norm_ffn_g': gain((L, D_MODEL)),
        'router_group_w': nrm((L, D_MODEL, N_GROUPS), D_MODEL),
        'router_group_b': small((L, N_GROUPS), ROUTER_BIAS_SCALE),
        'router_expert_w': nrm((L, D_MODEL, N_EXPERTS), D_MODEL),
        'router_expert_b': small((L, N_EXPERTS), ROUTER_BIAS_SCALE),
        'moe_w_gate': nrm((L, N_EXPERTS, D_MODEL, D_FF), D_MODEL),
        'moe_w_up': nrm((L, N_EXPERTS, D_MODEL, D_FF), D_MODEL),
        'moe_w_down': nrm((L, N_EXPERTS, D_FF, D_MODEL), D_FF),
        'final_norm_g': gain((D_MODEL,)),
    }

def second_block(x, mem, norm_mix_g, w_in, conv_w, conv_b, conv_ln_g, conv_ln_b, conv_w_out,
              hgrn_lb_logits, hgrn_onorm_g, hgrn_w_out, w_mix_out, norm_xa_g, norm_mem_g,
              xa_w_q, xa_w_k, xa_w_v, xa_w_o, norm_ffn_g, router_group_w, router_group_b,
              router_expert_w, router_expert_b, moe_w_gate, moe_w_up, moe_w_down, final_norm_g):
    lower_bounds = jnp.cumsum(jax.nn.softmax(hgrn_lb_logits.astype(jnp.float32), axis=0), axis=0)
    for l in range(DEPTH):
        h = rms_norm(x, norm_mix_g[l])
        proj = h @ w_in[l]
        c_a, c_g, q_r, f_r, i_r, g_r, gate_c, gate_r = jnp.split(proj, SPLITS, axis=-1)
        y_conv = conformer_conv_branch(c_a, c_g, conv_w[l], conv_b[l], conv_ln_g[l],
                                       conv_ln_b[l], conv_w_out[l])
        y_rec = hgrn2_branch(q_r, f_r, i_r, g_r, lower_bounds[l], hgrn_onorm_g[l], hgrn_w_out[l])
        merged = jax.nn.sigmoid(gate_c) * y_conv + jax.nn.sigmoid(gate_r) * y_rec
        x = x + merged @ w_mix_out[l]
        h = rms_norm(x, norm_xa_g[l])
        mem_n = rms_norm(mem, norm_mem_g[l])
        x = x + memory_cross_attention(h, mem_n, xa_w_q[l], xa_w_k[l], xa_w_v[l], xa_w_o[l])
        h = rms_norm(x, norm_ffn_g[l])
        x = x + hierarchical_moe(h, router_group_w[l], router_group_b[l], router_expert_w[l],
                                 router_expert_b[l], moe_w_gate[l], moe_w_up[l], moe_w_down[l])
    return rms_norm(x, final_norm_g)


def setup_inputs(seed=0):
    out = dict(first_inputs(seed))
    for name, value in second_inputs(seed + 1).items():
        if name != "x":
            out[name + "_2"] = value
    return out


def reference(
    x, c, ctx, c_ctx, w_mod, b_mod, norm1_g, norm2_g, w_in, w_out, diff_lq1, diff_lk1, diff_lq2,
    diff_lk2, diff_subln_g, gqa_q_norm_g, gqa_k_norm_g, peer_wq, peer_subkeys, peer_u, peer_v,
    final_norm_g, mem_2, norm_mix_g_2, w_in_2, conv_w_2, conv_b_2, conv_ln_g_2, conv_ln_b_2,
    conv_w_out_2, hgrn_lb_logits_2, hgrn_onorm_g_2, hgrn_w_out_2, w_mix_out_2, norm_xa_g_2,
    norm_mem_g_2, xa_w_q_2, xa_w_k_2, xa_w_v_2, xa_w_o_2, norm_ffn_g_2, router_group_w_2,
    router_group_b_2, router_expert_w_2, router_expert_b_2, moe_w_gate_2, moe_w_up_2,
    moe_w_down_2, final_norm_g_2,
):
    x = first_block(
        x, c, ctx, c_ctx, w_mod, b_mod, norm1_g, norm2_g, w_in, w_out, diff_lq1, diff_lk1,
        diff_lq2, diff_lk2, diff_subln_g, gqa_q_norm_g, gqa_k_norm_g, peer_wq, peer_subkeys,
        peer_u, peer_v, final_norm_g,
    )
    return second_block(
        x, mem_2, norm_mix_g_2, w_in_2, conv_w_2, conv_b_2, conv_ln_g_2, conv_ln_b_2,
        conv_w_out_2, hgrn_lb_logits_2, hgrn_onorm_g_2, hgrn_w_out_2, w_mix_out_2, norm_xa_g_2,
        norm_mem_g_2, xa_w_q_2, xa_w_k_2, xa_w_v_2, xa_w_o_2, norm_ffn_g_2, router_group_w_2,
        router_group_b_2, router_expert_w_2, router_expert_b_2, moe_w_gate_2, moe_w_up_2,
        moe_w_down_2, final_norm_g_2,
    )


_drawn_inputs = setup_inputs


def setup_inputs(seed=0):
    import zlib

    import numpy as np

    out = dict(_drawn_inputs(seed))
    spreads = {}
    factors = {'norm1_g': 5.014,
     'norm2_g': 5.535,
     'diff_lq1': 8.0,
     'diff_subln_g': 2.946,
     'gqa_q_norm_g': 8.0,
     'gqa_k_norm_g': 8.0,
     'norm_mix_g_2': 3.256,
     'conv_ln_g_2': 25.837,
     'conv_ln_b_2': 28.834,
     'hgrn_onorm_g_2': 7.222,
     'norm_xa_g_2': 8.0,
     'norm_mem_g_2': 4.026,
     'router_group_b_2': 64.0,
     'router_expert_b_2': 29.304,
     'final_norm_g_2': 7.861,
     'diff_lq2': 2.9,
     'conv_b_2': 8.0,
     'norm_ffn_g_2': 8.0,
     'router_group_w_2': 2.99,
     'router_expert_w_2': 2.887,
     'moe_w_gate_2': 2.777}
    for name, (base, spread) in spreads.items():
        noise = np.random.default_rng([zlib.crc32(name.encode()), seed]).standard_normal(out[name].shape)
        drawn = base * np.exp(spread * noise) if base else spread * noise
        out[name] = jnp.asarray(drawn.astype(out[name].dtype))
    for name, factor in factors.items():
        out[name] = (out[name] * factor).astype(out[name].dtype)
    return out
```

```python
import math
from contextlib import ExitStack

import numpy as np
import concourse.bass as bass
from concourse import mybir

F32 = mybir.dt.float32
F32R = mybir.dt.float32r
U32 = mybir.dt.uint32
I32 = mybir.dt.int32
ALU = mybir.AluOpType
ACT = mybir.ActivationFunctionType
AX = mybir.AxisListType.X

P = 128
D = 1024
KT = D // P
T = 256
TT = T // P
HD = 64
NH_DIFF = 4
EPS = 1e-6
LAMBDA_INIT = 0.8 - 0.6 * math.exp(-0.3 * 0)
UNIT = 1024
RING = 4
PH, PKEYS, PTOP = 8, 128, 16
CONV_K, CC = 31, 512
GROUPS, PER_GROUP, EXPERTS = 4, 8, 32
FF = 512
TOP_K = 2
CAP = 64
LEVELS = 7

W_IN_UNITS = [("dk", i) for i in range(4)] + [("gk", 0)] + [("dq", i) for i in range(4)] \
    + [("gq", i) for i in range(4)] + [("gv", 0)] + [("dv", i) for i in range(4)]


def plan_first():
    units = [("mod", n) for n in range(16)]
    rest = [("mod", n) for n in range(16, 48)]
    for i in range(0, 18, 2):
        units += W_IN_UNITS[i:i + 2]
        take = 4 if i < 14 else 2
        units += rest[:take]
        rest = rest[take:]
    assert not rest
    units += [("out", n) for n in range(8)]
    units += [("wq", n) for n in range(16)]
    return units


def plan_second():
    units = []
    for what, n in (("f", 4), ("q", 4), ("i", 4), ("ca", 4), ("cg", 4), ("g", 4), ("gc", 8), ("gr", 8),
                    ("xk", 8), ("xv", 8), ("ho", 4), ("co", 4), ("mix", 8), ("xq", 8), ("xo", 8)):
        units += [(what, i) for i in range(n)]
    return units


FIRST, SECOND = plan_first(), plan_second()
FIRST_DVE = [u for u in FIRST if u[0] == "mod" and u[1] >= 16]
FIRST_PE = [u for u in FIRST if u not in FIRST_DVE]
SECOND_ACT = [u for u in SECOND if u[0] not in ("co", "ho", "mix", "xo")]
BETWEEN = [u for u in SECOND if u[0] in ("ca", "cg", "g", "gc")][:2 * (LEVELS + 1)]
PAIRS1, PAIRS_PEER, PAIRS2 = len(FIRST) // 2, PKEYS, len(SECOND) // 2

CONST = {}
_at = 0
for _n, _w in (("ident", 128), ("ones", 128), ("halves", 128), ("swap", 128), ("cos", 256), ("sin", 256),
               ("iota", 128), ("before", 128)):
    CONST[_n] = (_at, _w)
    _at += _w
NCONST = _at
VEC = {}
_at = 0
for _n, _w in (("b_mod", 48), ("norm1_g", 8), ("norm2_g", 8), ("final_norm_g", 8), ("norm_mix_g", 8),
               ("norm_xa_g", 8), ("norm_mem_g", 8), ("norm_ffn_g", 8), ("conv_b", 4), ("conv_ln_g", 4),
               ("conv_ln_b", 4), ("lb", 8), ("onorm_g", 1), ("subln_g", 1), ("gq_g", 1), ("gk_g", 1),
               ("lam_q", 2), ("lam_k", 2), ("conv_w", 4 * CONV_K)):
    VEC[_n] = (_at, _w)
    _at += _w
NVEC = _at


FAMILIES = {
    "squares_ready": (("sq1_ready", 2), ("sqg_ready", 5), ("sqo_ready", 2), ("sq2_ready", 8), ("sqx_ready", 8), ("sqm_ready", 1), ("sqh_ready", 2), ("sqc_ready", 1), ("sqn_ready", 8), ("sq5_ready", 8)),
    "deviation_ready": (("std1_ready", 1), ("stdg_ready", 3), ("stdo_ready", 2), ("std2_ready", 1), ("stdx_ready", 2), ("stdm_ready", 1), ("stdh_ready", 2), ("stdc_ready", 1), ("stdn_ready", 1), ("std5_ready", 1), ("std6_ready", 2)),
    "sums_ready": (("ss1_ready", 1), ("ssg_ready", 3), ("sso_ready", 2), ("ss2_ready", 1), ("ssx_ready", 1), ("ssm_ready", 1), ("ssh_ready", 2), ("meanc_ready", 1), ("varc_ready", 1), ("ssn_ready", 1), ("ss5_mm", 1)),
    "h_ready": (("h_x_ready", 8), ("h2_ready", 8), ("H3_ready", 8), ("H4_ready", 8), ("H5_ready", 8)),
    "x_ready": (("x1_ready", 8), ("x2_ready", 8), ("x2n_ready", 8), ("x3_ready", 8), ("x4_ready", 8)),
}
FAMILY, BASE = {}, {}
for _f, _stages in FAMILIES.items():
    _at = 0
    for _n, _w in _stages:
        FAMILY[_n], BASE[_n] = _f, _at
        _at += _w


def base(name):
    return BASE[name]


def build(nc, t):
    ctx = ExitStack()
    with ctx:
        place_of = {}

        def sb(name, cols, dt=F32):
            tensor = ctx.enter_context(nc.sbuf_tensor(name, [P, cols], dt))
            place_of[name] = nc.sbuf_base - 4 * cols
            return tensor

        sems = {}

        def S(name):
            name = FAMILY.get(name, name)
            if name not in sems:
                sems[name] = ctx.enter_context(nc.semaphore(name))
            return sems[name]

        def three(ap, n):
            return ap.rearrange("p (a b) -> p a b", a=n)

        def wide(ap, n):
            return ap.unsqueeze(1).broadcast_to([P, n, ap.shape[1]])

        def each(ap, n):
            return ap.unsqueeze(2).broadcast_to([P, ap.shape[1], n])

        const = sb("const", NCONST)
        vec = sb("vec", NVEC)
        modT = sb("modT", 96)
        X = sb("X", KT * T)
        H = sb("H", KT * T)
        ring = sb("ring", RING * 2 * UNIT)
        big = sb("big", P * T)
        misc = sb("misc", 2300 + 4096)
        small, work = misc[:, 0:2300], misc[:, 2300:6396]
        bank = [ctx.enter_context(nc.psum_tensor(f"bank{i}", [P, 512], F32)) for i in range(8)]

        def cst(name):
            a, w = CONST[name]
            return const[:, a:a + w]

        def v(name, i=0, n=1):
            a, _ = VEC[name]
            return vec[:, a + i:a + i + n]

        def area(start, cols):
            return big[:, start:start + cols]

        ident, ones, halves, swap = cst("ident"), cst("ones"), cst("halves"), cst("swap")
        Xv, Hv = three(X[:], KT), three(H[:], KT)
        mod3 = three(modT[:], 48)
        eps = small[:, 0:1]
        cT = small[:, 8:24]
        csT = small[:, 24:40]
        gs_x, gs_c = small[:, 40:48], small[:, 48:56]
        gain_dv = small[:, 56:57]
        lam = small[:, 57:58]
        lam_e = small[:, 60:62]
        lprod = small[:, 62:64]
        gs2 = small[:, 64:72]
        g_tmp = small[:, 72:80]
        mx, nmx, rsum, rinv = (small[:, 80 + 6 * i:86 + 6 * i] for i in range(4))

        ctxT = three(area(0, 2048), KT)
        hAll = three(area(2048, 4096), KT)
        sq = three(area(6144, 4096), KT)
        dkT = three(area(10240, 2048), 4)
        gkT = area(12288, 512)
        dqT = three(area(12800, 1024), 4)
        gqT = three(area(13824, 1024), 4)
        dvs = three(area(14848, 2048), 4)
        gvs = three(area(16896, 512), 4)
        Pb = area(17408, 3072).rearrange("p (i r k) -> p i r k", i=3, r=2)
        PTb = area(0, 2048).rearrange("p (i r k q) -> p i r k q", i=2, r=2, k=4)
        oT = three(area(21504, 2048), 8)
        rt = area(23552, 2048).rearrange("p (a b c) -> p a b c", a=4, b=2)
        rs1 = area(25600, 512)
        rsg = area(26112, 1024)
        rsk = area(27136, 512)
        mod_acc = three(area(27648, 4096), 32)
        mod_rows4 = area(17408, 2048)

        qh = area(0, 512).rearrange("p (s t) -> p s t", s=2)
        sc = area(512, 512).rearrange("p (s t n) -> p s t n", s=2, t=TT)
        sc2 = area(1024, 512).rearrange("p (s t n) -> p s t n", s=2, t=TT)
        sv = area(1536, 512).rearrange("p (t h n) -> p t h n", t=TT, h=16)
        si = area(2048, 512).bitcast(U32).rearrange("p (t h n) -> p t h n", t=TT, h=16)
        sif = area(2560, 512).rearrange("p (t h n) -> p t h n", t=TT, h=16)
        cand = area(3072, 1024).rearrange("p (s t n) -> p s t n", s=2, t=TT)
        cand2 = area(4096, 1024).rearrange("p (s t n) -> p s t n", s=2, t=TT)
        best = area(5120, 256).rearrange("p (t h n) -> p t h n", t=TT, h=PH)
        pos = area(5376, 256).bitcast(U32).rearrange("p (t h n) -> p t h n", t=TT, h=PH)
        digit_u = area(5632, 512).bitcast(U32).rearrange("p (d t k) -> p d t k", d=2, t=TT)
        digit = area(6144, 512).rearrange("p (d t k) -> p d t k", d=2, t=TT)
        gate = area(6656, 256).rearrange("p (t h n) -> p t h n", t=TT, h=PH)
        ids = area(6912, 512).rearrange("p (d t k) -> p d t k", d=2, t=TT)
        pick = area(8192, 4096).rearrange("p (s h n a) -> p s h n a", s=2, h=PH, n=PTOP)
        gsum, grec = small[:, 104:120], small[:, 120:136]
        GIJ = three(work[:, 2048:2816], 3)
        left, right = three(work[:, 0:1024], 8), three(work[:, 1024:2048], 8)
        H_parts, ring_parts, misc_parts = (
            nc.alloc_sbuf_tensor_at(f"{name}_parts", [P, cols], F32R, offset=place_of[name]).ap()
            for name, cols in (("H", KT * T), ("ring", RING * 2 * UNIT), ("misc", 6396)))
        x_hi, x_lo = three(misc_parts[:, 2748:4796], KT), three(H_parts, KT)
        wgt_hi, wgt_lo = three(misc_parts[:, 4796:5308], 2), three(misc_parts[:, 5308:5820], 2)
        act_e = three(misc[:, 5820:6332], 2)
        u_hi, v_hi = misc_parts[:, 700:1724], misc_parts[:, 1724:2748]
        G = three(big[:], PKEYS)
        zeros = small[:, 136:648]

        sqx = three(area(0, 4096), KT)
        rsx = area(13440, 512)
        up = area(0, 4 * (CONV_K - 1 + T)).rearrange("p (c t) -> p c t", c=4)
        cv = area(1152, 1024).rearrange("p (c t) -> p c t", c=4)
        caT = three(area(2176, 1024), 4)
        vi = three(area(3200, 1024), TT)
        ff = three(area(4224, 1024), 4)
        kk = three(area(5248, 1024), 4)
        qq = three(area(6272, 1024), 4)
        gg = three(area(7296, 1024), 4)
        cum = area(8320, 1024)
        DE = area(9344, 1024)
        QE, KE = area(10368, 1024), area(11392, 1024)
        scT = area(12416, 1024).rearrange("p (h t n) -> p h t n", h=4, t=TT)
        cross = three(area(13440, 512), 4)
        xv = three(area(13952, 2048), TT)
        xkT = three(area(16000, 2048), KT)
        memn = three(area(18048, 2048), KT)
        sqm = three(area(13952, 2048), KT)
        rsm = area(20096, 256)
        gcs, grs = three(work[:, 0:2048], KT), three(work[:, 2048:4096], KT)
        masks = three(small[:, 136:136 + 896], LEVELS)
        lb, lb1, lbd = small[:, 1512:1516], small[:, 1516:1520], small[:, 1520:1524]
        fg_mix = small[:, 1524:1532]
        sqc = three(area(8320, 1024), 4)
        sgate = cv
        mean, rstdc = area(9344, 256), area(9600, 256)
        och = three(area(5248, 1024), 4)
        sqh = three(area(6272, 1024), 4)
        rsh = area(10368, 1024)
        xaq = three(area(0, 2048), KT)
        xP = area(2048, 2048).rearrange("p (i t k) -> p i t k", i=4, t=TT)
        xPT = area(4096, 2048).rearrange("p (i k q) -> p i k q", i=4, k=TT)
        xo = three(area(6144, 2048), KT)
        sqn = three(area(8192, 2048), KT)
        rsn = area(10240, 256)
        xmx, xnmx, xrs, xri = (small[:, 1532 + 8 * i:1540 + 8 * i] for i in range(4))

        w_exp = [area(20480, 12288), area(8192, 12288)]
        w_gate, w_up = ([w[:, 4096 * i:4096 * (i + 1)].rearrange("p (k n) -> p k n", k=KT) for w in w_exp] for i in range(2))
        w_down = [w[:, 8192:12288].rearrange("p (k n) -> p k n", k=4) for w in w_exp]
        h_tok, x_tok = three(area(0, 2048), TT), three(area(2048, 2048), TT)
        sq5, rs5 = three(area(4096, 2048), KT), area(6144, 256)
        hg = three(area(4096, 1024), KT)
        y_slot = area(6144, 1024)
        sel, selw = three(area(7168, 256), TT), three(area(7424, 256), TT)
        selwT = area(7680, 256)
        silu, hid = area(5120, 512), area(5632, 512)
        hidT = three(work[:, 0:512], 4)
        fin_g = work[:, 1024:2048]
        x5 = three(work[:, 2048:4096], TT)
        chosen, weight, place = (three(small[:, 1700 + 64 * i:1764 + 64 * i], TT) for i in range(3))
        r_w = three(small[:, 1892:2180], KT)
        r_b = small[:, 2180:2216]
        scr = area(7936, 256)
        logit = three(scr[:, 0:72], TT)
        g8, gm8, i8, em8 = (three(scr[:, 72 + 16 * i:88 + 16 * i], TT) for i in range(4))
        gi8, ei8 = (three(scr[:, 136 + 16 * i:152 + 16 * i].bitcast(U32), TT) for i in range(2))
        grp, gex = three(scr[:, 168:176], TT), three(scr[:, 176:184], TT)
        prod = scr[:, 184:248].rearrange("p (t g e) -> p t g e", t=TT, g=GROUPS)
        rr = small[:, 2216:2300]
        gif, eif, eid = three(rr[:, 0:2], TT), three(rr[:, 2:6], TT), three(rr[:, 6:10], TT)
        gsm, e21, den, w12 = rr[:, 10:12], rr[:, 12:14], rr[:, 14:16], three(rr[:, 16:20], TT)
        most, rnd = rr[:, 20:21], rr[:, 21:22]
        rounds = rr[:, 22:23].bitcast(I32)
        ss5, ri5 = rr[:, 24:26], rr[:, 26:28]
        cmp4 = rr[:, 28:32]
        fin_part = rr[:, 32:36]

        def unit(n):
            s = (n // 2) % RING
            a = (2 * s + n % 2) * UNIT
            return ring[:, a:a + UNIT].rearrange("p (k n) -> p k n", k=KT)

        def pair_landed(eng, n):
            eng.wait_ge(S(f"ring_full{n % RING}"), 16 * (n // RING + 1))

        def peer_unit(q, i, ring=ring):
            s = (PAIRS1 + q) % RING
            return ring[:, (2 * s + i) * UNIT:(2 * s + i + 1) * UNIT]

        def PT_bank(i, r):
            return 4 + i % 2 if i < 8 else 4 + r

        def second_done(eng, what, i):
            eng.wait_ge(S("second_unit_done"), SECOND.index((what, i)) + 1)

        def second_bank(what, i):
            return bank[SECOND.index((what, i)) % 4]

        def first_done(eng, what, i):
            eng.wait_ge(S("first_unit_done"), FIRST_PE.index((what, i)) + 1)

        block = ctx.enter_context(nc.Block())

        @block.sync
        def _(sp):
            def load_pair(n, src):
                s = n % RING
                sp.dma_start(ring[:, s * 2 * UNIT:(s + 1) * 2 * UNIT], src).then_inc(S(f"ring_full{s}"), 16)

            for n in range(PAIRS1):
                if n >= RING:
                    what, i = FIRST[2 * (n - RING) + 1]
                    if (what, i) in FIRST_DVE:
                        sp.wait_ge(S("mod_pair_done"), (FIRST_DVE.index((what, i)) + 1) // 2)
                    else:
                        first_done(sp, what, i)
                load_pair(n, t["first"][n])
            for j in range(RING):
                first_done(sp, *FIRST[2 * (PAIRS1 - RING + j) + 1])
                load_pair(PAIRS1 + j, t["peer"][j])
            with sp.Fori(0, PKEYS // RING - 1) as i:
                for q in range(RING):
                    sp.wait_ge(S("peer_pair_done"), i * RING + (q + 1))
                    s = (PAIRS1 + q) % RING
                    sp.dma_start(ring[:, s * 2 * UNIT:(s + 1) * 2 * UNIT], t["peer"].rearrange("j p c -> (j p) c")[bass.ds((i * RING + (RING + q)) * P, P), :]).then_inc(S(f"ring_full{s}"), 16)
            sp.wait_ge(S("x2_ready"), base("x2_ready") + 1)
            sp.dma_start(area(18048, 2048), t["memT"]).then_inc(S("mem_in"), 16)
            sp.dma_start(small[:, 136:136 + 128 * LEVELS], t["masks"]).then_inc(S("masks_in"), 16)
            for m in range(PAIRS2):
                n = PAIRS1 + PAIRS_PEER + m
                if m < RING:
                    sp.wait_ge(S("peer_pair_done"), PAIRS_PEER - RING + m + 1)
                else:
                    second_done(sp, *SECOND[2 * (m - RING) + 1])
                load_pair(n, t["second"][m])
                if m in (6, 8, 10):
                    i = (m - 6) // 2
                    sp.dma_start(w_exp[0][:, 4096 * i:4096 * (i + 1)], t[("moe_gate", "moe_up", "moe_down")[i]][0]).then_inc(
                        S(("gates_in", "ups_in", "downs_in")[i]), 16)
                if m == 12:
                    sp.dma_start(r_w.rearrange("p k n -> p (k n)"), t["router_w"]).then_inc(S("router_in"), 16)
                    sp.dma_start(r_b, t["router_b"].broadcast_to([P, 36])).then_inc(S("router_in"), 16)
            sp.wait_ge(S("xpv_ready"), 4)
            flat = {n: t[n].rearrange("e p c -> (e p) c") for n in ("moe_gate", "moe_up", "moe_down")}

            def load_part(a, e, i):
                name = ("moe_gate", "moe_up", "moe_down")[i]
                src = t[name][e] if isinstance(e, int) else flat[name][bass.ds(e * P, P), :]
                sp.dma_start(w_exp[a][:, 4096 * i:4096 * (i + 1)], src).then_inc(S(("gates_in", "ups_in", "downs_in")[i]), 16)

            for i in range(3):
                load_part(1, 1, i)
            sp.wait_ge(S("x4_ready"), base("x4_ready") + 8)
            sp.dma_start(fin_g, t["final_g"].broadcast_to([P, D])).then_inc(S("final_in"), 16)

            def load_experts(q, p):
                for i, done in enumerate(("gate_mm", "up_mm", "down_mm")):
                    sp.wait_ge(S(done), q)
                    for a in range(2):
                        load_part(a, p * 2 + a, i)

            with sp.Fori(0, EXPERTS // 2 - 1) as i:
                load_experts(i + 1, i + 1)
            sp.wait_ge(S("rounds_ready"), 1)
            n = sp.value_load(rounds[0:1, :], min_val=1, max_val=4)
            with sp.If(n > 1):
                with sp.Fori(1, n) as r:
                    with sp.Fori(0, EXPERTS // 2) as i:
                        load_experts(r * 16 + i, i)
            for tt in range(TT):
                sp.wait_ge(S("out_ready"), tt + 1)
                sp.dma_start(t["out"][tt * P:(tt + 1) * P, :], x5[:, tt, :]).then_inc(S("out_written"), 16)
            sp.wait_ge(S("out_written"), 16 * TT)

        @block.scalar
        def _(act):
            chain = [0]

            def link(ins):
                chain[0] += 1
                ins.then_inc(S("act_own"), 1)
                act.wait_ge(S("act_own"), chain[0])

            act.dma_start(X[:], t["xT"]).then_inc(S("x_in"), 16)
            act.dma_start(cT, t["cT"]).then_inc(S("c_in"), 16)
            act.dma_start(const[:], t["const"]).then_inc(S("const_in"), 16)
            act.dma_start(area(0, 2048), t["ctxT"]).then_inc(S("ctx_in"), 16)
            act.dma_start(vec[:], t["vec"]).then_inc(S("vec_in"), 16)
            act.dma_start(work[:, 0:2048], t["subkeys"]).then_inc(S("subkeys_in"), 16)

            act.wait_ge(S("c_in"), 16)
            act.activation(csT, cT, ACT.Silu).then_inc(S("cs_ready"), 1)
            act.wait_ge(S("x_in"), 16)
            act.activation(sq[:, :, T:2 * T], Xv, ACT.Square).then_inc(S("sq1_ready"), 1)
            act.wait_ge(S("ctx_in"), 16)
            act.activation(sq[:, :, 0:T], ctxT, ACT.Square).then_inc(S("sq1_ready"), 1)
            act.wait_ge(S("ss1_ready"), base("ss1_ready") + 1)
            act.wait_ge(S("eps_ready"), 1)
            act.activation(rs1, bank[6][:], ACT.Sqrt, scale=1.0 / D, bias=eps).then_inc(S("std1_ready"), 1)
            act.wait_ge(S("lam_sums"), 1)
            act.activation(lam_e, bank[5][:, 0:2], ACT.Exp).then_inc(S("lam_exp"), 1)
            for n in range(4):
                first_done(act, "mod", 4 * n + 3)
                act.activation(mod_rows4[0:2, n * 512:(n + 1) * 512], bank[n][0:2, :], ACT.Copy).then_inc(S("mod_rows_taken"), 1)
            act.wait_ge(S("gs1_ready"), 1)
            for k in range(KT):
                act.wait_ge(S("normed1"), k + 1)
                act.activation(hAll[:, k, 0:T], hAll[:, k, 0:T], ACT.Identity, scale=gs_c[:, k:k + 1],
                               bias=mod3[:, k, 1:2]).then_inc(S("h_ctx_ready"), 1)
            dst = {"dk": lambda i: dkT[:, i, :], "gk": lambda i: gkT, "dq": lambda i: dqT[:, i, :],
                   "gq": lambda i: gqT[:, i, :], "gv": lambda i: gvs, "dv": lambda i: dvs[:, :, i * P:(i + 1) * P]}
            for n, (what, i) in enumerate(W_IN_UNITS):
                first_done(act, what, i)
                src = bank[n % 4][:, 0:T] if what in ("dq", "gq") else bank[n % 4][:]
                if what in ("gv", "dv"):
                    src = three(src, 4)
                act.activation(dst[what](i), src, ACT.Copy).then_inc(S("win_taken"), 1)
                if (what, i) == ("gk", 0):
                    act.wait_ge(S("win_taken"), n + 1)
                    act.activation(sq[:, 0, :], gkT, ACT.Square).then_inc(S("sqg_ready"), 1)
                if what == "gq":
                    act.wait_ge(S("win_taken"), n + 1)
                    act.activation(sq[:, 2 + i // 2, (i % 2) * T:(i % 2 + 1) * T], gqT[:, i, :], ACT.Square).then_inc(S("sqg_ready"), 1)
                if n in (8, 14, 15):
                    j = (8, 14, 15).index(n)
                    act.wait_ge(S("ssg_ready"), base("ssg_ready") + j + 1)
                    act.activation((rsk, rsg[:, 0:512], rsg[:, 512:1024])[j], bank[6][:], ACT.Sqrt, scale=1.0 / HD,
                                   bias=eps).then_inc(S("stdg_ready"), 1)
            def exps(i):
                for r in range(2):
                    act.wait_ge(S("nmax_ready"), 2 * i + r + 1)
                    c = 2 * (i % 3) + r
                    if i >= 3:
                        act.wait_ge(S("PT_ready"), i - 2)
                    act.activation(Pb[:, i % 3, r, :], bank[2 * (i % 2) + r][:], ACT.Exp, scale=HD ** -0.5,
                                   bias=nmx[:, c:c + 1], accum_out=rsum[:, c:c + 1]).then_inc(S("exp_ready"), 1)

            def take_PT(i):
                act.wait_ge(S("PT_ready"), i + 1)
                if i >= 2:
                    act.wait_ge(S("pv_ready"), i - 1)
                for r in range(1 if i < 8 else 2):
                    ins = act.activation(PTb[:, i % 2, r, :, :].rearrange("p k q -> p (k q)"), bank[PT_bank(i, r)][:], ACT.Copy)
                ins.then_inc(S("PT_taken"), 1)

            for i in range(16 + 2):
                if i < 16:
                    exps(i)
                if i >= 2:
                    take_PT(i - 2)
            act.wait_ge(S("o_taken"), 8)
            for n in range(2):
                act.activation(sq[:, n, :], oT[:, 2 * n:2 * n + 2, :].rearrange("p a b -> p (a b)"), ACT.Square).then_inc(S("sqo_ready"), 1)
            for n in range(2):
                act.wait_ge(S("sso_ready"), base("sso_ready") + n + 1)
                act.activation(rsg[:, n * 512:(n + 1) * 512], bank[n][:], ACT.Sqrt, scale=1.0 / P, bias=eps).then_inc(S("stdo_ready"), 1)
            for k in range(KT):
                act.wait_ge(S("x1_ready"), base("x1_ready") + k + 1)
                act.activation(sq[:, k, 0:T], Xv[:, k, :], ACT.Square).then_inc(S("sq2_ready"), 1)
            act.wait_ge(S("ss2_ready"), base("ss2_ready") + 1)
            act.activation(rs1[:, 0:T], bank[6][:, 0:T], ACT.Sqrt, scale=1.0 / D, bias=eps).then_inc(S("std2_ready"), 1)
            for n in range(16):
                first_done(act, "wq", n)
                if n >= 2:
                    act.wait_ge(S("keys_scored"), n - 1)
                act.activation(qh[:, n % 2, :], bank[n % 2][:, 0:T], ACT.Copy).then_inc(S("qh_ready"), 1)
                act.wait_ge(S("keys_scored"), n + 1)
                if n >= 2:
                    act.wait_ge(S("sc_used"), n - 1)
                act.activation(sc[:, n % 2, :, :].rearrange("p t n -> p (t n)"), bank[2 + n % 2][:, 0:T], ACT.Copy).then_inc(S("sc_ready"), 1)
            act.wait_ge(S("best_shifted"), 1)
            act.activation(gate.rearrange("p t h n -> p (t h n)"), gate.rearrange("p t h n -> p (t h n)"), ACT.Exp).then_inc(S("gate_exp"), 1)
            for tt in range(TT):
                act.wait_ge(S("GIJ_turned"), tt + 1)
                act.activation(GIJ[:, :, tt * P:(tt + 1) * P], three(bank[4 + tt][:, 0:384], 3), ACT.Copy).then_inc(S("GIJ_ready"), 1)
            act.sem_inc(S("gates_taken"), 4)
            with act.Fori(0, T // 16) as i:
                g = i * 4
                for q in range(4):
                    act.wait_ge(S("gates_mm"), g * 4 + (12 + 4 * q))
                    nc.scalar.activation(G[:, :, bass.ds(g * 4 + 4 * q, 4)], three(bank[4 + q][:], 4).rearrange("p t j -> p j t"),
                                         ACT.Copy).then_inc(S("gates_taken"), 1)
            act.activation(x_hi, Hv, ACT.Copy).then_inc(S("x_hi_ready"), 1)

            def lead_u(q, j):
                s = (PAIRS1 + q) % RING
                act.wait_ge(S(f"ring_full{s}"), j * (16 // RING) + (16 * ((PAIRS1 + q) // RING + 1) - q * (16 // RING)))
                act.wait_ge(S("ux_ready"), j)
                nc.scalar.activation(u_hi, peer_unit(q, 0), ACT.Copy).then_inc(S("u_hi_ready"), 1)

            def lead_v(q, j):
                act.wait_ge(S("peer_pair_done"), j)
                nc.scalar.activation(v_hi, peer_unit(q, 1), ACT.Copy).then_inc(S("v_hi_ready"), 1)

            def gelu(q, j, first=False):
                act.wait_ge(S("ux_ready"), j + 1)
                if not first:
                    act.wait_ge(S("wgt_ready"), j - 1)
                nc.scalar.activation(act_e[:, q % 2, :], bank[4 + q % 2][:, 0:T], ACT.Gelu).then_inc(S("gelu_ready"), 1)

            lead_u(0, 0)
            lead_u(1, 1)
            gelu(0, 0, True)
            lead_v(0, 0)
            lead_u(2, 2)
            gelu(1, 1, True)
            lead_v(1, 1)
            with act.Fori(0, PKEYS // RING - 1) as i:
                for q in range(1, RING + 1):
                    lead_u((q + 2) % RING, i * RING + (q + 2))
                    gelu((q + 1) % RING, i * RING + (q + 1))
                    lead_v((q + 1) % RING, i * RING + (q + 1))
            lead_u(3, PKEYS - 1)
            for q in (2, 3):
                gelu(q, PKEYS - RING + q)
                lead_v(q, PKEYS - RING + q)
            for k in range(KT):
                act.wait_ge(S("x2_ready"), base("x2_ready") + k + 1)
                act.activation(sqx[:, k, 0:T], Xv[:, k, :], ACT.Square)
                act.activation(sqx[:, k, T:2 * T], Xv[:, k, :], ACT.Square, scale=v("final_norm_g", k)).then_inc(S("sqx_ready"), 1)
            act.wait_ge(S("mem_in"), 16)
            act.activation(sqm, memn, ACT.Square).then_inc(S("sqm_ready"), 1)
            act.wait_ge(S("ssx_ready"), base("ssx_ready") + 1)
            act.activation(rsx[:, 0:T], bank[6][:, 0:T], ACT.Sqrt, scale=1.0 / D, bias=eps).then_inc(S("stdx_ready"), 1)
            act.wait_ge(S("ms_mix_ready"), 1)
            act.activation(rsx[:, T:2 * T], rsx[:, T:2 * T], ACT.Sqrt, bias=eps).then_inc(S("stdx_ready"), 1)

            out2 = {"f": lambda i: (ff[:, i, :], ACT.Sigmoid), "q": lambda i: (qq[:, i, :], ACT.Silu),
                    "i": lambda i: (vi[:, :, i * P:(i + 1) * P], ACT.Copy), "ca": lambda i: (caT[:, i, :], ACT.Copy),
                    "cg": lambda i: (sgate[:, i, :], ACT.Sigmoid), "g": lambda i: (gg[:, i, :], ACT.Silu),
                    "gc": lambda i: (gcs[:, i, :], ACT.Sigmoid), "gr": lambda i: (grs[:, i, :], ACT.Sigmoid),
                    "xk": lambda i: (xkT[:, i, :], ACT.Copy), "xv": lambda i: (xv[:, :, i * P:(i + 1) * P], ACT.Copy),
                    "xq": lambda i: (xaq[:, i, :], ACT.Copy)}

            def take2(units):
                for what, i in units:
                    second_done(act, what, i)
                    src = second_bank(what, i)[:, 0:T]
                    out, func = out2[what](i)
                    act.activation(out, three(src, TT) if what in ("i", "xv") else src, func).then_inc(S("taken2"), 1)

            act.wait_ge(S("H3_ready"), base("H3_ready") + KT)
            take2([("f", i) for i in range(4)])
            act.wait_ge(S("lbd_ready"), 1)
            act.activation(lb, lbd, ACT.Sigmoid).then_inc(S("lb_ready"), 1)
            take2([("q", i) for i in range(4)])
            act.wait_ge(S("ssm_ready"), base("ssm_ready") + 1)
            act.activation(rsm, bank[6][:, 0:T], ACT.Sqrt, scale=1.0 / D, bias=eps).then_inc(S("stdm_ready"), 1)
            take2([("i", i) for i in range(4)])
            act.wait_ge(S("f_ready"), 1)
            act.activation(DE, ff.rearrange("p c t -> p (c t)"), ACT.Ln).then_inc(S("logf_ready"), 1)
            for lev in range(LEVELS + 1):
                act.wait_ge(S("dist_ready"), lev + 1)
                act.activation(DE, DE, ACT.Exp).then_inc(S("decay_ready"), 1)
                take2(BETWEEN[2 * lev:2 * lev + 2])
            act.wait_ge(S("cross_mm"), 1)
            act.activation(cross, three(bank[7][:], 4), ACT.Copy).then_inc(S("cross_ready"), 1)
            take2([("gc", 4), ("gc", 5)])
            for n in range(2):
                act.wait_ge(S("rec_ready"), n + 1)
                o_ = och[:, 2 * n:2 * n + 2, :].rearrange("p h t -> p (h t)")
                act.activation(o_, bank[6 + n][:], ACT.Copy)
                act.activation(sqh[:, 2 * n:2 * n + 2, :].rearrange("p h t -> p (h t)"), bank[6 + n][:], ACT.Square).then_inc(S("sqh_ready"), 1)
            take2([("gc", 6), ("gc", 7)])
            for n in range(2):
                act.wait_ge(S("ssh_ready"), base("ssh_ready") + n + 1)
                act.activation(rsh[:, n * 512:(n + 1) * 512], bank[4 + n][:], ACT.Sqrt, scale=1.0 / P, bias=eps).then_inc(S("stdh_ready"), 1)
            take2([(w, i) for w in ("gr", "xk") for i in range(8)])
            act.wait_ge(S("conv_centred"), 1)
            act.activation(sqc, cv, ACT.Square).then_inc(S("sqc_ready"), 1)
            take2([("xv", i) for i in range(4)])
            act.wait_ge(S("varc_ready"), base("varc_ready") + 1)
            act.activation(rstdc, bank[7][:, 0:T], ACT.Sqrt, scale=1.0 / CC, bias=eps).then_inc(S("stdc_ready"), 1)
            take2([("xv", i) for i in range(4, 8)])
            act.wait_ge(S("conv_normed"), 1)
            for i in range(4):
                act.activation(cv[:, i, :], cv[:, i, :], ACT.Silu, scale=v("conv_ln_g", i), bias=v("conv_ln_b", i)).then_inc(S("conv_act"), 1)
            for k in range(KT):
                act.wait_ge(S("x3_ready"), base("x3_ready") + k + 1)
                act.activation(sqn[:, k, :], Xv[:, k, :], ACT.Square).then_inc(S("sqn_ready"), 1)
            act.wait_ge(S("ssn_ready"), base("ssn_ready") + 1)
            act.activation(rsn, bank[6][:, 0:T], ACT.Sqrt, scale=1.0 / D, bias=eps).then_inc(S("stdn_ready"), 1)
            take2([("xq", i) for i in range(8)])
            for h in range(4):
                act.wait_ge(S("xmax_ready"), h + 1)
                for qt in range(TT):
                    c = 2 * h + qt
                    ins = act.activation(xP[:, h, qt, :], bank[4 + h % 2][:, qt * T:(qt + 1) * T], ACT.Exp, scale=1.0 / 16.0,
                                         bias=xnmx[:, c:c + 1], accum_out=xrs[:, c:c + 1])
                ins.then_inc(S("xexp_ready"), 1)
            for h in range(4):
                act.wait_ge(S("xPT_mm"), h + 1)
                act.activation(xPT[:, h, :, :].rearrange("p k q -> p (k q)"), bank[6 + h % 2][:], ACT.Copy).then_inc(S("xPT_ready"), 1)
            for k in range(KT):
                act.wait_ge(S("x4_ready"), base("x4_ready") + k + 1)
                act.activation(sq5[:, k, :], Xv[:, k, :], ACT.Square).then_inc(S("sq5_ready"), 1)
            act.wait_ge(S("ss5_mm"), base("ss5_mm") + 1)
            act.activation(rs5, bank[6][:, 0:T], ACT.Sqrt, scale=1.0 / D, bias=eps).then_inc(S("std5_ready"), 1)
            for n in range(4):
                act.wait_ge(S("x_turned"), n + 1)
                act.activation(x_tok[:, n // 2, (n % 2) * 512:(n % 2 + 1) * 512], bank[n][:], ACT.Copy).then_inc(S("x_tok_ready"), 1)
            for n in range(4):
                act.wait_ge(S("h_turned"), n + 1)
                act.activation(h_tok[:, n // 2, (n % 2) * 512:(n % 2 + 1) * 512], bank[n][:], ACT.Copy).then_inc(S("h_tok_ready"), 1)
            act.wait_ge(S("shifted5"), 2)
            act.activation(gex, gex, ACT.Exp)
            act.activation(e21, e21, ACT.Exp).then_inc(S("exp5_ready"), 1)
            act.wait_ge(S("rounds_ready"), 1)
            n = act.value_load(rounds[0:1, :], min_val=1, max_val=4)

            def silu_of(q):
                act.wait_ge(S("gate_mm"), q + 1)
                nc.scalar.activation(silu, bank[4][:], ACT.Silu).then_inc(S("silu_ready"), 1)

            def take_gathered(q):
                act.wait_ge(S("gather_mm"), q + 1)
                for b in range(2):
                    ins = nc.scalar.activation(hg[:, 4 * b:4 * b + 4, :].rearrange("p k n -> p (k n)"), bank[6 + b][:], ACT.Copy)
                ins.then_inc(S("hg_ready"), 1)

            def take_y(q):
                act.wait_ge(S("down_mm"), q + 1)
                for b in range(2):
                    ins = nc.scalar.activation(y_slot[:, 512 * b:512 * (b + 1)], bank[6 + b][:], ACT.Copy)
                ins.then_inc(S("y_slot_ready"), 1)

            with act.Fori(0, n) as r:
                take_gathered(r * 16)
                with act.Fori(0, EXPERTS // 2 - 1) as i:
                    silu_of(r * 16 + i)
                    take_gathered(r * 16 + i + 1)
                    take_y(r * 16 + i)
                silu_of(r * 16 + 15)
                take_y(r * 16 + 15)
            for tt in range(TT):
                act.wait_ge(S("x5_ready"), 2 * tt + 2)
                act.activation(y_slot, x5[:, tt, :], ACT.Square, accum_out=ss5[:, tt:tt + 1]).then_inc(S("ss5_ready"), 1)
                act.wait_ge(S("ss5_ready"), tt + 1)
                act.activation(ss5[:, tt:tt + 1], ss5[:, tt:tt + 1], ACT.Sqrt, scale=1.0 / D, bias=eps).then_inc(S("std6_ready"), 1)

        @block.tensor
        def _(pe):
            pair = [0]
            at = [0]

            def take():
                n = FIRST.index(FIRST_PE[at[0]])
                at[0] += 1
                if n % 2 == 0:
                    pair_landed(pe, n // 2)
                return unit(n)

            pe.wait_ge(S("const_in"), 16)
            pe.wait_ge(S("lprod_ready"), 1)
            nc.tensor.matmul(bank[5][:, 0:2], ones, lprod, start=True, stop=True).then_inc(S("lam_sums"), 1)
            pe.wait_ge(S("sq1_ready"), base("sq1_ready") + 2)
            for k in range(KT):
                last = nc.tensor.matmul(bank[6][:], ones, sq[:, k, :], start=(k == 0), stop=(k == KT - 1))
            last.then_inc(S("ss1_ready"), 1)
            cs = csT.rearrange("p (k two) -> p k two", two=2)
            pe.wait_ge(S("cs_ready"), 1)
            for n in range(16):
                w = take()
                for k in range(KT):
                    last = nc.tensor.matmul(bank[n // 4][0:2, (n % 4) * P:(n % 4 + 1) * P], cs[:, k, :], w[:, k, :],
                                            start=(k == 0), stop=(k == KT - 1))
                last.then_inc(S("first_unit_done"), 1)
            for n in range(16):
                pe.wait_ge(S("mod_rows_taken"), n // 4 + 1)
                last = nc.tensor.transpose(bank[7][:, 2 * n:2 * n + 2], mod_rows4[0:2, n * P:(n + 1) * P], ident[0:2, 0:2])
            last.then_inc(S("mod1_ready"), 1)
            pe.wait_ge(S("lam_exp"), 1)
            aux = [0]

            def rope_mm(src2):
                b = 4 + aux[0] % 2
                if aux[0] >= 2:
                    pe.wait_ge(S("rope_taken"), aux[0] - 1)
                for j, s in enumerate(src2):
                    last = nc.tensor.matmul(bank[b][:, j * T:(j + 1) * T], swap, s, start=True, stop=True)
                last.then_inc(S("rope_ready"), 1)
                aux[0] += 1

            n_win = 0
            pe.wait_ge(S("h_x_ready"), base("h_x_ready") + KT)
            pe.wait_ge(S("h_ctx_ready"), KT)
            for what, i in W_IN_UNITS:
                w = take()
                b = bank[n_win % 4]
                if n_win >= 4:
                    pe.wait_ge(S("win_taken"), n_win - 3)
                if what in ("dk", "gk", "dq", "gq"):
                    a, n = (0, 2 * T) if what in ("dk", "gk") else (T, T)
                    for k in range(KT):
                        last = nc.tensor.matmul(b[:, 0:n], w[:, k, :], hAll[:, k, a:a + n], start=(k == 0), stop=(k == KT - 1))
                else:
                    for tt in range(4):
                        for k in range(KT):
                            last = nc.tensor.matmul(b[:, tt * P:(tt + 1) * P], hAll[:, k, tt * P:(tt + 1) * P], w[:, k, :],
                                                    start=(k == 0), stop=(k == KT - 1))
                last.then_inc(S("first_unit_done"), 1)
                n_win += 1
                if n_win == 7:
                    pe.wait_ge(S("win_taken"), 5)
                    for j in range(2):
                        rope_mm([dkT[:, 2 * j, T:], dkT[:, 2 * j + 1, T:]])
                    pe.wait_ge(S("sqg_ready"), base("sqg_ready") + 1)
                    nc.tensor.matmul(bank[6][:], halves, sq[:, 0, :], start=True, stop=True).then_inc(S("ssg_ready"), 1)
                if n_win == 11:
                    pe.wait_ge(S("win_taken"), 9)
                    for j in range(2):
                        rope_mm([dqT[:, 2 * j, :], dqT[:, 2 * j + 1, :]])
                if n_win in (14, 15):
                    g = n_win - 14
                    pe.wait_ge(S("sqg_ready"), base("sqg_ready") + 3 + 2 * g)
                    pe.wait_ge(S("stdg_ready"), base("stdg_ready") + 1 + g)
                    nc.tensor.matmul(bank[6][:], halves, sq[:, 2 + g, :], start=True, stop=True).then_inc(S("ssg_ready"), 1)
                if n_win == 16:
                    pe.wait_ge(S("gk_normed"), 1)
                    rope_mm([gkT[:, T:]])
            for j in range(2):
                pe.wait_ge(S("gq_normed"), j + 1)
                rope_mm([gqT[:, 2 * j, :], gqT[:, 2 * j + 1, :]])

            def scores(i):
                t_, qt = (i % 8) // 2, i % 2
                q = dqT if i < 8 else gqT
                if i == 0:
                    pe.wait_ge(S("rope_done"), 4)
                    pe.wait_ge(S("win_taken"), 18)
                if i == 8:
                    pe.wait_ge(S("rope_done"), 7)
                for r in range(2):
                    k = dkT[:, t_, :] if i < 8 else gkT
                    if i >= 2:
                        pe.wait_ge(S("exp_ready"), 2 * (i - 2) + r + 1)
                    a = HD * r
                    nc.tensor.matmul(bank[2 * (i % 2) + r][:], q[a:a + HD, t_, qt * P:(qt + 1) * P], k[a:a + HD, :],
                                     start=True, stop=True).then_inc(S("scores_ready"), 1)

            def transposes(i):
                pe.wait_ge(S("P_ready"), i + 1)
                if i >= 2:
                    pe.wait_ge(S("PT_taken"), i - 1 if i < 8 else i)
                for r in range(1 if i < 8 else 2):
                    for k in range(4):
                        last = nc.tensor.transpose(bank[PT_bank(i, r)][:, k * P:(k + 1) * P], Pb[:, i % 3, r, k * P:(k + 1) * P], ident)
                last.then_inc(S("PT_ready"), 1)

            def pv(i):
                t_ = (i % 8) // 2
                pe.wait_ge(S("PT_taken"), i + 1)
                if i >= 2:
                    pe.wait_ge(S("o_taken"), i - 1)
                o = bank[6 + i % 2]
                for k in range(4):
                    if i < 8:
                        last = nc.tensor.matmul(o[:, 0:P], dvs[:, k, t_ * P:(t_ + 1) * P], PTb[:, i % 2, 0, k, :], start=(k == 0), stop=(k == 3))
                if i >= 8:
                    for r in range(2):
                        for k in range(4):
                            last = nc.tensor.matmul(o[HD * r:HD * (r + 1), 0:P], gvs[:, k, HD * r:HD * (r + 1)], PTb[:, i % 2, r, k, :],
                                                    start=(k == 0), stop=(k == 3))
                last.then_inc(S("pv_ready"), 1)

            for i in range(19):
                if i < 16:
                    scores(i)
                if 2 <= i < 18:
                    transposes(i - 2)
                if i >= 3:
                    pv(i - 3)
            pe.wait_ge(S("mod_pair_done"), 16)
            pe.wait_ge(S("o_taken"), 16)
            for n in range(32):
                last = nc.tensor.matmul(bank[7][:, n:n + 1], mod_acc[:, n, :], ones[:, 0:1], start=True, stop=True)
            last.then_inc(S("mod2_ready"), 1)
            for n in range(2):
                pe.wait_ge(S("sqo_ready"), base("sqo_ready") + n + 1)
                nc.tensor.matmul(bank[n][:], ones, sq[:, n, :], start=True, stop=True).then_inc(S("sso_ready"), 1)
            pe.wait_ge(S("o_taken"), 16)
            pe.wait_ge(S("od_normed"), 2)
            for n in range(8):
                w = take()
                b = bank[2 + n % 4]
                if n >= 4:
                    pe.wait_ge(S("x1_ready"), base("x1_ready") + n - 3)
                for k in range(KT):
                    last = nc.tensor.matmul(b[:, 0:T], w[:, k, :], oT[:, k, :], start=(k == 0), stop=(k == KT - 1))
                last.then_inc(S("first_unit_done"), 1)
            for k in range(KT):
                pe.wait_ge(S("sq2_ready"), base("sq2_ready") + k + 1)
                last = nc.tensor.matmul(bank[6][:, 0:T], ones, sq[:, k, 0:T], start=(k == 0), stop=(k == KT - 1))
            last.then_inc(S("ss2_ready"), 1)
            pe.wait_ge(S("h2_ready"), base("h2_ready") + KT)
            pe.wait_ge(S("subkeys_in"), 16)
            subkeys = three(work[:, 0:2048], 16)

            def key_scores(n):
                pe.wait_ge(S("qh_ready"), n + 1)
                if n >= 2:
                    pe.wait_ge(S("sc_ready"), n - 1)
                for tt in range(TT):
                    last = nc.tensor.matmul(bank[2 + n % 2][:, tt * P:(tt + 1) * P], qh[:, n % 2, tt * P:(tt + 1) * P],
                                            subkeys[:, n, :], start=True, stop=True)
                last.then_inc(S("keys_scored"), 1)

            for n in range(16):
                w = take()
                if n >= 2:
                    pe.wait_ge(S("qh_ready"), n - 1)
                for k in range(KT):
                    last = nc.tensor.matmul(bank[n % 2][:, 0:T], w[:, k, :], Hv[:, k, :], start=(k == 0), stop=(k == KT - 1))
                last.then_inc(S("first_unit_done"), 1)
                if n >= 1:
                    key_scores(n - 1)
            key_scores(15)
            pe.wait_ge(S("ids_ready"), 1)
            for tt in range(TT):
                for i, a in enumerate((gate[:, tt, :, :].rearrange("p h n -> p (h n)"), ids[:, 0, tt, :], ids[:, 1, tt, :])):
                    last = nc.tensor.transpose(bank[4 + tt][:, i * P:(i + 1) * P], a, ident)
                last.then_inc(S("GIJ_turned"), 1)
            pe.wait_ge(S("GIJ_ready"), 2)
            pe.sem_inc(S("gates_mm"), 8)
            with pe.Fori(0, T // 16) as i:
                g = i * 4
                for q in range(16):
                    if q % 4 == 0:
                        pe.wait_ge(S("gates_taken"), g + (q // 4 + 1))
                    pe.wait_ge(S("left_ready"), g * 4 + (q + 1))
                    if q % 4 == 0:
                        pe.wait_ge(S("right_ready"), g + (q // 4 + 1))
                    nc.tensor.matmul(bank[4 + q // 4][:, (q % 4) * P:(q % 4 + 1) * P], left[:, q % 8, :], right[:, q % 8, :],
                                     start=True, stop=True).then_inc(S("gates_mm"), 1)
            pe.wait_ge(S("zeros_ready"), 1)
            for b in range(4):
                nc.tensor.matmul(bank[b][:], zeros[:, 0:P], zeros, start=True, stop=False, skip_group_check=True)

            def ux(q, j, first=False):
                pe.wait_ge(S("u_hi_ready"), j + 1)
                if not first:
                    pe.wait_ge(S("gelu_ready"), j - 1)
                hi, lo, out = three(u_hi, KT), three(peer_unit(q, 0, ring_parts), KT), bank[4 + q % 2][:, 0:T]
                for k in range(KT):
                    nc.tensor.matmul(out, hi[:, k, :], x_hi[:, k, :], start=(k == 0), stop=False)
                    nc.tensor.matmul(out, hi[:, k, :], x_lo[:, k, :], start=False, stop=False)
                pe.wait_ge(S("u_lo_ready"), j + 1)
                for k in range(KT):
                    last = nc.tensor.matmul(out, lo[:, k, :], x_hi[:, k, :], start=False, stop=(k == KT - 1))
                last.then_inc(S("ux_ready"), 1)

            def wv(q, j):
                pe.wait_ge(S("v_hi_ready"), j + 1)
                pe.wait_ge(S("wgt_ready"), j + 1)
                lo = peer_unit(q, 1, ring_parts)
                for b_ in ((v_hi, wgt_hi), (v_hi, wgt_lo), (lo, wgt_hi)):
                    if b_[0] is lo:
                        pe.wait_ge(S("v_lo_ready"), j + 1)
                    for k in range(KT):
                        last = nc.tensor.matmul(bank[k // 2][:, (k % 2) * T:(k % 2 + 1) * T], b_[0][:, k * P:(k + 1) * P],
                                                b_[1][:, q % 2, :], start=False, stop=False, skip_group_check=True)
                last.then_inc(S("peer_pair_done"), 1)

            pe.wait_ge(S("x_lo_ready"), 1)
            ux(0, 0, True)
            ux(1, 1, True)
            wv(0, 0)
            with pe.Fori(0, PKEYS // RING - 1) as i:
                for q in range(RING):
                    ux((q + 2) % RING, i * RING + (q + 2))
                    wv((q + 1) % RING, i * RING + (q + 1))
            for q in (2, 3):
                ux(q, PKEYS - RING + q)
                wv(q - 1, PKEYS - RING + q - 1)
            wv(3, PKEYS - 1)
            for b in range(4):
                last = nc.tensor.matmul(bank[b][:], zeros[:, 0:P], zeros, start=False, stop=True, skip_group_check=True)
            last.then_inc(S("peer_ready"), 1)
            for k in range(KT):
                pe.wait_ge(S("sqx_ready"), base("sqx_ready") + k + 1)
                last = nc.tensor.matmul(bank[6][:], ones, sqx[:, k, :], start=(k == 0), stop=(k == KT - 1))
            last.then_inc(S("ssx_ready"), 1)
            at2 = [0]

            def take2(what, i):
                n = at2[0]
                assert SECOND[n] == (what, i)
                at2[0] += 1
                if n % 2 == 0:
                    pair_landed(pe, PAIRS1 + PAIRS_PEER + n // 2)
                if n >= 4:
                    prior = SECOND[n - 4]
                    if prior in SECOND_ACT:
                        pe.wait_ge(S("taken2"), SECOND_ACT.index(prior) + 1)
                    elif prior[0] in ("co", "ho"):
                        pe.wait_ge(S("merge_taken"), prior[1] + (1 if prior[0] == "ho" else 5))
                    elif prior[0] == "mix":
                        pe.wait_ge(S("x3_ready"), base("x3_ready") + prior[1] + 1)
                    else:
                        pe.wait_ge(S("x4_ready"), base("x4_ready") + prior[1] + 1)
                s = (PAIRS1 + PAIRS_PEER + n // 2) % RING
                return ring[:, (2 * s + n % 2) * UNIT:(2 * s + n % 2 + 1) * UNIT]

            def project(units, rhs):
                for what, i in units:
                    w, b = three(take2(what, i), KT), second_bank(what, i)
                    if what in ("i", "xv"):
                        for tt in range(TT):
                            for k in range(KT):
                                last = nc.tensor.matmul(b[:, tt * P:(tt + 1) * P], rhs[:, k, tt * P:(tt + 1) * P], w[:, k, :],
                                                        start=(k == 0), stop=(k == KT - 1))
                    else:
                        for k in range(KT):
                            last = nc.tensor.matmul(b[:, 0:T], w[:, k, :], rhs[:, k, :], start=(k == 0), stop=(k == KT - 1))
                    last.then_inc(S("second_unit_done"), 1)

            pe.wait_ge(S("H3_ready"), base("H3_ready") + KT)
            project([("f", i) for i in range(4)], Hv)
            pe.wait_ge(S("stdx_ready"), base("stdx_ready") + 2)
            pe.wait_ge(S("sqm_ready"), base("sqm_ready") + 1)
            for k in range(KT):
                last = nc.tensor.matmul(bank[6][:, 0:T], ones, sqm[:, k, :], start=(k == 0), stop=(k == KT - 1))
            last.then_inc(S("ssm_ready"), 1)
            project([(w, i) for w in ("q", "i") for i in range(4)], Hv)
            qe, ke = (x.rearrange("p (h t n) -> p h t n", h=4, t=TT) for x in (QE, KE))
            for lev in range(LEVELS + 2):
                if lev <= LEVELS:
                    pe.wait_ge(S("qke_ready"), lev + 1)
                if lev == LEVELS:
                    for h in range(4):
                        last = nc.tensor.matmul(bank[7][:, h * P:(h + 1) * P], ke[:, h, 0, :], qe[:, h, 1, :], start=True, stop=True)
                    last.then_inc(S("cross_mm"), 1)
                else:
                    n_level = min(lev, LEVELS)
                    if n_level >= 1:
                        pe.wait_ge(S("level_taken"), n_level)
                    for h in range(4):
                        for tt in range(TT):
                            i = 2 * h + tt
                            a, b = (ke[:, h, tt, :], qe[:, h, tt, :]) if lev < LEVELS else \
                                (kk[:, h, tt * P:(tt + 1) * P], qq[:, h, tt * P:(tt + 1) * P])
                            last = nc.tensor.matmul(bank[4 + i // 4][:, (i % 4) * P:(i % 4 + 1) * P], a, b, start=True, stop=True)
                    last.then_inc(S("level_mm"), 1)
                if lev <= LEVELS:
                    project(BETWEEN[2 * lev:2 * lev + 2], Hv)
            project([("gc", 4), ("gc", 5)], Hv)
            pe.wait_ge(S("cross_ready"), 1)
            pe.wait_ge(S("level_taken"), LEVELS + 1)
            for h in range(4):
                o_ = bank[6 + h // 2][:, (h % 2) * T:(h % 2 + 1) * T]
                v0, v1 = vi[:, 0, h * P:(h + 1) * P], vi[:, 1, h * P:(h + 1) * P]
                nc.tensor.matmul(o_[:, 0:P], v0, scT[:, h, 0, :], start=True, stop=True)
                nc.tensor.matmul(o_[:, P:T], v0, cross[:, h, :], start=True, stop=False)
                last = nc.tensor.matmul(o_[:, P:T], v1, scT[:, h, 1, :], start=False, stop=True)
                if h % 2 == 1:
                    last.then_inc(S("rec_ready"), 1)
            project([("gc", 6), ("gc", 7)], Hv)
            for n in range(2):
                pe.wait_ge(S("sqh_ready"), base("sqh_ready") + n + 1)
                nc.tensor.matmul(bank[4 + n][:], ones, sqh[:, 2 * n:2 * n + 2, :].rearrange("p h t -> p (h t)"),
                                 start=True, stop=True).then_inc(S("ssh_ready"), 1)
            project([("gr", i) for i in range(8)], Hv)
            pe.wait_ge(S("memn_ready"), 1)
            project([("xk", i) for i in range(8)], memn)
            pe.wait_ge(S("conv_ready"), 1)
            for i in range(4):
                last = nc.tensor.matmul(bank[6][:, 0:T], ones, cv[:, i, :], start=(i == 0), stop=(i == 3))
            last.then_inc(S("meanc_ready"), 1)
            project([("xv", i) for i in range(4)], memn)
            pe.wait_ge(S("sqc_ready"), base("sqc_ready") + 1)
            for i in range(4):
                last = nc.tensor.matmul(bank[7][:, 0:T], ones, sqc[:, i, :], start=(i == 0), stop=(i == 3))
            last.then_inc(S("varc_ready"), 1)
            project([("xv", i) for i in range(4, 8)], memn)
            for what, rhs in (("ho", och), ("co", cv)):
                for i in range(4):
                    pe.wait_ge(S("conv_act" if what == "co" else "och_normed"), 4)
                    w, b = three(take2(what, i), 4), second_bank(what, i)
                    for n in range(2):
                        for k in range(4):
                            last = nc.tensor.matmul(b[:, n * T:(n + 1) * T], w[:, k, n * P:(n + 1) * P], rhs[:, k, :],
                                                    start=(k == 0), stop=(k == 3))
                    last.then_inc(S("second_unit_done"), 1)
            pe.wait_ge(S("merged"), 4)
            project([("mix", i) for i in range(8)], gcs)
            for k in range(KT):
                pe.wait_ge(S("sqn_ready"), base("sqn_ready") + k + 1)
                last = nc.tensor.matmul(bank[6][:, 0:T], ones, sqn[:, k, :], start=(k == 0), stop=(k == KT - 1))
            last.then_inc(S("ssn_ready"), 1)
            pe.wait_ge(S("H4_ready"), base("H4_ready") + KT)
            project([("xq", i) for i in range(8)], Hv)
            pe.wait_ge(S("taken2"), len(SECOND_ACT))
            for h in range(4):
                if h >= 2:
                    pe.wait_ge(S("xexp_ready"), h - 1)
                for qt in range(TT):
                    for k in range(2):
                        last = nc.tensor.matmul(bank[4 + h % 2][:, qt * T:(qt + 1) * T], xaq[:, 2 * h + k, qt * P:(qt + 1) * P],
                                                xkT[:, 2 * h + k, :], start=(k == 0), stop=(k == 1))
                last.then_inc(S("xscores_ready"), 1)
            for h in range(4):
                pe.wait_ge(S("xP_ready"), h + 1)
                if h >= 2:
                    pe.wait_ge(S("xPT_ready"), h - 1)
                for kt in range(TT):
                    for qt in range(TT):
                        last = nc.tensor.transpose(bank[6 + h % 2][:, (2 * kt + qt) * P:(2 * kt + qt + 1) * P],
                                                   xP[:, h, qt, kt * P:(kt + 1) * P], ident)
                last.then_inc(S("xPT_mm"), 1)
            for h in range(4):
                pe.wait_ge(S("xPT_ready"), h + 1)
                if h >= 2:
                    pe.wait_ge(S("xo_taken"), h - 1)
                for d in range(2):
                    for kt in range(TT):
                        last = nc.tensor.matmul(bank[4 + h % 2][:, d * T:(d + 1) * T], xv[:, kt, (2 * h + d) * P:(2 * h + d + 1) * P],
                                                xPT[:, h, kt, :], start=(kt == 0), stop=(kt == 1))
                last.then_inc(S("xpv_ready"), 1)
            pe.wait_ge(S("xo_taken"), 4)
            project([("xo", i) for i in range(8)], xo)
            for k in range(KT):
                pe.wait_ge(S("sq5_ready"), base("sq5_ready") + k + 1)
                last = nc.tensor.matmul(bank[6][:, 0:T], ones, sq5[:, k, :], start=(k == 0), stop=(k == KT - 1))
            last.then_inc(S("ss5_mm"), 1)
            pe.wait_ge(S("x4_ready"), base("x4_ready") + 8)
            for src, ready in ((Xv, "x_turned"), (Hv, "h_turned")):
                if src is Hv:
                    pe.wait_ge(S("H5_ready"), base("H5_ready") + KT)
                    pe.wait_ge(S("router_in"), 32)
                    for tt in range(TT):
                        for k in range(KT):
                            last = nc.tensor.matmul(bank[7][:, 36 * tt:36 * tt + 36], Hv[:, k, tt * P:(tt + 1) * P], r_w[:, k, :],
                                                    start=(k == 0), stop=(k == KT - 1))
                    last.then_inc(S("logits_mm"), 1)
                for n in range(4):
                    if src is Hv:
                        pe.wait_ge(S("x_tok_ready"), n + 1)
                    for j in range(4):
                        k = 4 * (n % 2) + j
                        last = nc.tensor.transpose(bank[n][:, j * P:(j + 1) * P], src[:, k, (n // 2) * P:(n // 2 + 1) * P], ident)
                    last.then_inc(S(ready), 1)
            pe.wait_ge(S("chosen_ready"), 1)
            before = cst("before")
            nc.tensor.matmul(bank[6][:, 0:32], before, chosen[:, 0, :], start=True, stop=True)
            nc.tensor.matmul(bank[6][:, 32:64], ones, chosen[:, 0, :], start=True, stop=False)
            nc.tensor.matmul(bank[6][:, 32:64], before, chosen[:, 1, :], start=False, stop=True)
            nc.tensor.matmul(bank[6][:, 64:96], ones, chosen[:, 0, :], start=True, stop=False)
            nc.tensor.matmul(bank[6][:, 64:96], ones, chosen[:, 1, :], start=False, stop=True).then_inc(S("places_mm"), 1)
            pe.wait_ge(S("h_tok_ready"), 4)
            pe.wait_ge(S("zeros5_ready"), 1)
            for b in range(4):
                nc.tensor.matmul(bank[b][:], zeros[:, 0:P], zeros, start=True, stop=False, skip_group_check=True)
            pe.wait_ge(S("rounds_ready"), 1)
            n = pe.value_load(rounds[0:1, :], min_val=1, max_val=4)

            def gather(q):
                pe.wait_ge(S("sel_ready"), q + 1)
                for k in range(KT):
                    for tt in range(TT):
                        last = nc.tensor.matmul(bank[6 + k // 4][:, (k % 4) * P:(k % 4 + 1) * P], h_tok[:, tt, k * P:(k + 1) * P],
                                                sel[:, tt, :], start=(tt == 0), stop=(tt == TT - 1))
                last.then_inc(S("gather_mm"), 1)

            def both(out, slots, weights, k, n):
                for a in range(2):
                    c = slice(a * CAP, (a + 1) * CAP)
                    last = nc.tensor.matmul(out[c, :], slots[:, c], weights[a], start=(k == 0), stop=(k == n - 1))
                return last

            def gate_up(q):
                pe.wait_ge(S("hg_ready"), q + 1)
                for w, b, loaded, done in ((w_gate, 4, "gates_in", "gate_mm"), (w_up, 5, "ups_in", "up_mm")):
                    pe.wait_ge(S(loaded), q * 32 + 32)
                    for k in range(KT):
                        last = both(bank[b], hg[:, k, :], [x[:, k, :] for x in w], k, KT)
                    last.then_inc(S(done), 1)

            def scatter(q):
                pe.wait_ge(S("y_slot_ready"), q + 1)
                for tt in range(TT):
                    for b in range(2):
                        nc.tensor.matmul(bank[2 * tt + b][:], selwT[:, tt * P:(tt + 1) * P], y_slot[:, 512 * b:512 * (b + 1)],
                                         start=False, stop=False, skip_group_check=True)

            def turn(q):
                pe.wait_ge(S("hid_ready"), q + 1)
                for k in range(4):
                    last = nc.tensor.transpose(bank[4][:, k * P:(k + 1) * P], hid[:, k * P:(k + 1) * P], ident)
                last.then_inc(S("turn_mm"), 1)
                pe.wait_ge(S("selw_ready"), q + 1)
                for tt in range(TT):
                    last = nc.tensor.transpose(bank[5][:, tt * P:(tt + 1) * P], selw[:, tt, :], ident)
                last.then_inc(S("selT_mm"), 1)

            def down(q):
                pe.wait_ge(S("hidT_ready"), q + 1)
                pe.wait_ge(S("downs_in"), q * 32 + 32)
                for k in range(4):
                    for b in range(2):
                        last = both(bank[6 + b], hidT[:, k, :], [w[:, k, 512 * b:512 * (b + 1)] for w in w_down], k, 4)
                last.then_inc(S("down_mm"), 1)

            with pe.Fori(0, n) as r:
                q0 = r * 16
                gather(q0)
                gate_up(q0)
                gather(q0 + 1)
                turn(q0)
                pe.wait_ge(S("hg_ready"), q0 + 2)
                down(q0)
                with pe.Fori(0, EXPERTS // 2 - 2) as i:
                    q = q0 + i + 1
                    pe.wait_ge(S("selwT_ready"), q)
                    gate_up(q)
                    scatter(q - 1)
                    gather(q + 1)
                    turn(q)
                    pe.wait_ge(S("hg_ready"), q + 2)
                    down(q)
                pe.wait_ge(S("selwT_ready"), q0 + 15)
                gate_up(q0 + 15)
                scatter(q0 + 14)
                turn(q0 + 15)
                down(q0 + 15)
                pe.wait_ge(S("selwT_ready"), q0 + 16)
                scatter(q0 + 15)
            for b in range(4):
                last = nc.tensor.matmul(bank[b][:], zeros[:, 0:P], zeros, start=False, stop=True, skip_group_check=True)
            last.then_inc(S("moe_mm"), 1)

        @block.vector
        def _(dve):
            chain = [0]

            def link(ins):
                chain[0] += 1
                ins.then_inc(S("dve_own"), 1)
                dve.wait_ge(S("dve_own"), chain[0])

            dve.memset(eps, EPS).then_inc(S("eps_ready"), 1)
            dve.wait_ge(S("vec_in"), 16)
            dve.tensor_tensor(lprod, v("lam_q", 0, 2), v("lam_k", 0, 2), ALU.mult).then_inc(S("lprod_ready"), 1)
            dve.wait_ge(S("std1_ready"), base("std1_ready") + 1)
            link(dve.reciprocal(rs1, rs1))
            dve.wait_ge(S("ctx_in"), 16)
            for k in range(KT):
                dve.tensor_tensor(hAll[:, k, 0:T], ctxT[:, k, :], rs1[:, 0:T], ALU.mult).then_inc(S("normed1"), 1)
            dve.wait_ge(S("x_in"), 16)
            link(dve.tensor_tensor(hAll[:, :, T:2 * T], Xv, wide(rs1[:, T:2 * T], KT), ALU.mult))
            dve.wait_ge(S("mod1_ready"), 1)
            link(dve.tensor_tensor(mod3[:, 0:16, :], three(bank[7][:, 0:32], 16), each(v("b_mod", 0, 16), 2), ALU.add))
            link(dve.tensor_scalar(gs_x, mod3[:, 8:16, 0], 1.0, None, ALU.add))
            link(dve.tensor_scalar(gs_c, mod3[:, 8:16, 1], 1.0, None, ALU.add))
            dve.tensor_tensor(gs_x, gs_x, v("norm1_g", 0, 8), ALU.mult)
            dve.tensor_tensor(gs_c, gs_c, v("norm1_g", 0, 8), ALU.mult).then_inc(S("gs1_ready"), 1)
            dve.wait_ge(S("gs1_ready"), 1)
            for k in range(KT):
                dve.tensor_scalar(hAll[:, k, T:2 * T], hAll[:, k, T:2 * T], gs_x[:, k:k + 1], mod3[:, k, 0:1],
                                  ALU.mult, ALU.add).then_inc(S("h_x_ready"), 1)
            dve.wait_ge(S("lam_exp"), 1)
            link(dve.tensor_tensor(lam, lam_e[:, 0:1], lam_e[:, 1:2], ALU.subtract))
            link(dve.tensor_scalar(lam, lam, LAMBDA_INIT, -1.0, ALU.add, ALU.mult))
            dve.tensor_scalar(gain_dv, v("subln_g"), 1.0 - LAMBDA_INIT, None, ALU.mult)

            cs = csT.rearrange("p (k two) -> p k two", two=2)
            nmod = [0]

            def mod_pair():
                m = nmod[0]
                nmod[0] += 1
                n = FIRST.index(FIRST_DVE[2 * m])
                pair_landed(dve, n // 2)
                s = (n // 2) % RING
                w = ring[:, 2 * s * UNIT:(2 * s + 2) * UNIT].rearrange("p (u k n) -> p u k n", u=2, k=KT)
                acc = mod_acc[:, 2 * m:2 * m + 2, :]
                link(dve.tensor_scalar(acc, w[:, :, 0, :], cs[:, 0, 0:1], None, ALU.mult))
                for k in range(1, KT):
                    ins = dve.scalar_tensor_tensor(acc, w[:, :, k, :], cs[:, k, 0:1], acc, ALU.mult, ALU.add)
                    if k < KT - 1:
                        link(ins)
                ins.then_inc(S("mod_pair_done"), 1)

            nrope = [0]

            def rope(x, n):
                i = nrope[0]
                nrope[0] += 1
                b = three(bank[4 + i % 2][:, 0:n * T], n)
                dve.wait_ge(S("rope_ready"), i + 1)
                link(dve.tensor_tensor(rt[:, 0, 0:n, :], x, wide(cst("cos"), n), ALU.mult))
                ins = dve.tensor_tensor(rt[:, 1, 0:n, :], b, wide(cst("sin"), n), ALU.mult)
                ins.then_inc(S("rope_taken"), 1)
                dve.wait_ge(S("rope_taken"), i + 1)
                dve.tensor_tensor(x, rt[:, 0, 0:n, :], rt[:, 1, 0:n, :], ALU.add).then_inc(S("rope_done"), 1)
                dve.wait_ge(S("rope_done"), i + 1)

            for _ in range(4):
                mod_pair()
            dve.wait_ge(S("win_taken"), 5)
            for j in range(2):
                rope(dkT[:, 2 * j:2 * j + 2, T:2 * T], 2)
            for _ in range(2):
                mod_pair()
            dve.wait_ge(S("stdg_ready"), base("stdg_ready") + 1)
            link(dve.reciprocal(rsk, rsk))
            dve.scalar_tensor_tensor(gkT, gkT, v("gk_g"), rsk, ALU.mult, ALU.mult).then_inc(S("gk_normed"), 1)
            for _ in range(2):
                mod_pair()
            for j in range(2):
                rope(dqT[:, 2 * j:2 * j + 2, :], 2)
            for _ in range(4):
                mod_pair()
            for j in range(2):
                dve.wait_ge(S("stdg_ready"), base("stdg_ready") + 2 + j)
                link(dve.reciprocal(rsg[:, j * 512:(j + 1) * 512], rsg[:, j * 512:(j + 1) * 512]))
                dve.scalar_tensor_tensor(gqT[:, 2 * j:2 * j + 2, :], gqT[:, 2 * j:2 * j + 2, :], v("gq_g"),
                                         three(rsg[:, j * 512:(j + 1) * 512], 2), ALU.mult, ALU.mult).then_inc(S("gq_normed"), 1)
            mod_pair()
            dve.wait_ge(S("gk_normed"), 1)
            rope(gkT[:, T:].unsqueeze(1), 1)
            dve.wait_ge(S("gq_normed"), 2)
            for j in range(2):
                rope(gqT[:, 2 * j:2 * j + 2, :], 2)

            while nmod[0] < 16:
                mod_pair()

            def maxima(i):
                for r in range(2):
                    c = 2 * (i % 3) + r
                    dve.wait_ge(S("scores_ready"), 2 * i + r + 1)
                    link(dve.reduce_max(mx[:, c:c + 1], bank[2 * (i % 2) + r][:], AX))
                    dve.tensor_scalar(nmx[:, c:c + 1], mx[:, c:c + 1], -HD ** -0.5, None, ALU.mult).then_inc(S("nmax_ready"), 1)

            def normalise(i):
                c = 2 * (i % 3)
                dve.wait_ge(S("exp_ready"), 2 * i + 2)
                link(dve.reciprocal(rinv[:, c:c + 2], rsum[:, c:c + 2]))
                a, b = Pb[:, i % 3, 0, :], Pb[:, i % 3, 1, :]
                if i < 8:
                    dve.tensor_scalar(b, b, rinv[:, c + 1:c + 2], lam, ALU.mult, ALU.mult).then_inc(S("P2_scaled"), 1)
                    dve.wait_ge(S("P2_scaled"), i + 1)
                    dve.scalar_tensor_tensor(a, a, rinv[:, c:c + 1], b, ALU.mult, ALU.add).then_inc(S("P_ready"), 1)
                else:
                    dve.tensor_scalar(a, a, rinv[:, c:c + 1], None, ALU.mult)
                    dve.tensor_scalar(b, b, rinv[:, c + 1:c + 2], None, ALU.mult).then_inc(S("P_ready"), 1)

            def take_o(i):
                dve.wait_ge(S("pv_ready"), i + 1)
                tile = (i % 8) // 2 + (0 if i < 8 else 4)
                dve.tensor_copy(oT[:, tile, (i % 2) * P:(i % 2 + 1) * P], bank[6 + i % 2][:, 0:P]).then_inc(S("o_taken"), 1)

            for i in range(20):
                if i < 16:
                    maxima(i)
                if 1 <= i < 17:
                    normalise(i - 1)
                if i >= 4:
                    take_o(i - 4)
            for n in range(2):
                dve.wait_ge(S("stdo_ready"), base("stdo_ready") + n + 1)
                r = rsg[:, n * 512:(n + 1) * 512]
                link(dve.reciprocal(r, r))
                dve.scalar_tensor_tensor(oT[:, 2 * n:2 * n + 2, :], oT[:, 2 * n:2 * n + 2, :], gain_dv, three(r, 2),
                                         ALU.mult, ALU.mult).then_inc(S("od_normed"), 1)
            dve.wait_ge(S("mod2_ready"), 1)
            link(dve.tensor_tensor(mod3[:, 16:48, 0], bank[7][:, 0:32], v("b_mod", 16, 32), ALU.add))
            link(dve.tensor_scalar(gs2, mod3[:, 32:40, 0], 1.0, None, ALU.add))
            dve.tensor_tensor(gs2, gs2, v("norm2_g", 0, 8), ALU.mult).then_inc(S("mod_taken"), 1)
            for n in range(8):
                first_done(dve, "out", n)
                dve.scalar_tensor_tensor(Xv[:, n, :], bank[2 + n % 4][:, 0:T], mod3[:, 16 + n, 0:1], Xv[:, n, :],
                                         ALU.mult, ALU.add).then_inc(S("x1_ready"), 1)
            dve.wait_ge(S("std2_ready"), base("std2_ready") + 1)
            dve.wait_ge(S("mod_taken"), 1)
            dve.wait_ge(S("x1_ready"), base("x1_ready") + 8)
            link(dve.reciprocal(rs1[:, 0:T], rs1[:, 0:T]))
            link(dve.tensor_tensor(Hv, Xv, wide(rs1[:, 0:T], KT), ALU.mult))
            for k in range(KT):
                dve.tensor_scalar(Hv[:, k, :], Hv[:, k, :], gs2[:, k:k + 1], mod3[:, 24 + k, 0:1], ALU.mult, ALU.add).then_inc(S("h2_ready"), 1)
            dve.memset(zeros, 0.0).then_inc(S("zeros_ready"), 1)

            def top16(values, spare, out_v, out_i):
                for tt in range(TT):
                    ins = dve.max(out_v[tt][:, 0:8], values[tt])
                link(ins)
                for tt in range(TT):
                    dve.max_index(out_i[tt][:, 0:8], out_v[tt][:, 0:8], values[tt])
                for tt in range(TT):
                    ins = dve.match_replace(spare[tt], out_v[tt][:, 0:8], values[tt], -3.0e38)
                link(ins)
                for tt in range(TT):
                    ins = dve.max(out_v[tt][:, 8:16], spare[tt])
                link(ins)
                for tt in range(TT):
                    ins = dve.max_index(out_i[tt][:, 8:16], out_v[tt][:, 8:16], spare[tt])
                return ins

            for n in range(16):
                dve.wait_ge(S("sc_ready"), n + 1)
                top16([sc[:, n % 2, tt, :] for tt in range(TT)], [sc2[:, n % 2, tt, :] for tt in range(TT)],
                      [sv[:, tt, n, :] for tt in range(TT)], [si[:, tt, n, :] for tt in range(TT)]).then_inc(S("sc_used"), 1)
                if n % 2 == 0:
                    continue
                h = n // 2
                dve.wait_ge(S("sc_used"), n + 1)
                for tt in range(TT):
                    ins = dve.tensor_tensor(three(cand[:, h % 2, tt, :], PTOP), each(sv[:, tt, n - 1, :], PTOP),
                                            wide(sv[:, tt, n, :], PTOP), ALU.add)
                link(ins)
                link(top16([cand[:, h % 2, tt, :] for tt in range(TT)], [cand2[:, h % 2, tt, :] for tt in range(TT)],
                           [best[:, tt, h, :] for tt in range(TT)], [pos[:, tt, h, :] for tt in range(TT)]))
            dve.tensor_tensor(gate, best, best[:, :, :, 0:1].broadcast_to([P, TT, PH, PTOP]), ALU.subtract).then_inc(S("best_shifted"), 1)
            posf = pos.rearrange("p t h n -> p t (h n)")
            dve.tensor_scalar(digit_u[:, 0, :, :], posf, 4, None, ALU.logical_shift_right)
            link(dve.tensor_scalar(digit_u[:, 1, :, :], posf, 15, None, ALU.bitwise_and))
            dve.tensor_copy(digit.rearrange("p d t k -> p (d t k)"), digit_u.rearrange("p d t k -> p (d t k)"))
            link(dve.tensor_copy(sif.rearrange("p t h n -> p (t h n)"), si.rearrange("p t h n -> p (t h n)")))
            iota16 = cst("iota")[:, 0:PTOP].unsqueeze(1).broadcast_to([P, P, PTOP])
            for tt in range(TT):
                for d in range(2):
                    eq = pick[:, d, :, :, :]
                    link(dve.tensor_tensor(eq.rearrange("p h n a -> p (h n) a"), each(digit[:, d, tt, :], PTOP), iota16, ALU.is_equal))
                    key = sif[:, tt, :, :].rearrange("p (h d) a -> p h d a", d=2)[:, :, d, :]
                    link(dve.tensor_tensor(eq, eq, key.unsqueeze(2).broadcast_to([P, PH, PTOP, PTOP]), ALU.mult))
                    link(dve.reduce_sum(ids[:, d, tt, :], eq.rearrange("p h n a -> p (h n) a"), AX))
            dve.wait_ge(S("gate_exp"), 1)
            gs = gsum.rearrange("p (t h) -> p t h", t=TT)
            gr = grec.rearrange("p (t h) -> p t h", t=TT)
            link(dve.reduce_sum(gs, gate, AX))
            link(dve.reciprocal(grec, gsum))
            dve.tensor_tensor(gate, gate, gr.unsqueeze(3).broadcast_to([P, TT, PH, PTOP]), ALU.mult).then_inc(S("ids_ready"), 1)
            dve.wait_ge(S("GIJ_ready"), 2)
            with dve.Fori(0, T // 8) as i:
                t0 = i * 8
                for q in range(8):
                    if q % 4 == 0:
                        dve.wait_ge(S("gates_mm"), t0 + (q + 4))
                        nc.vector.tensor_tensor(right[:, q:q + 4, :], wide(cst("iota"), 4), each(GIJ[:, 2, bass.ds(t0 + q, 4)], P),
                                                ALU.is_equal).then_inc(S("right_ready"), 1)
                    nc.vector.tensor_scalar(left[:, q, :], cst("iota"), GIJ[:, 1, bass.ds(t0 + q, 1)], GIJ[:, 0, bass.ds(t0 + q, 1)],
                                            ALU.is_equal, ALU.mult).then_inc(S("left_ready"), 1)

            dve.wait_ge(S("x_hi_ready"), 1)
            dve.tensor_tensor(x_lo, Hv, x_hi, ALU.subtract).then_inc(S("x_lo_ready"), 1)

            def rest_u(q, j):
                dve.wait_ge(S("u_hi_ready"), j + 1)
                nc.vector.tensor_tensor(peer_unit(q, 0, ring_parts), peer_unit(q, 0), u_hi, ALU.subtract).then_inc(S("u_lo_ready"), 1)

            def rest_v(q, j):
                dve.wait_ge(S("v_hi_ready"), j + 1)
                nc.vector.tensor_tensor(peer_unit(q, 1, ring_parts), peer_unit(q, 1), v_hi, ALU.subtract).then_inc(S("v_lo_ready"), 1)

            def weigh(q, j, first=False):
                w = act_e[:, q % 2, :]
                dve.wait_ge(S("gelu_ready"), j + 1)
                nc.vector.tensor_tensor(w.unsqueeze(1), w.unsqueeze(1), G[:, bass.ds(j, 1), :], ALU.mult).then_inc(S("weighed"), 1)
                if not first:
                    dve.wait_ge(S("peer_pair_done"), j - 1)
                dve.wait_ge(S("weighed"), j + 1)
                nc.vector.tensor_copy(wgt_hi[:, q % 2, :], w).then_inc(S("wgt_hi_ready"), 1)
                dve.wait_ge(S("wgt_hi_ready"), j + 1)
                nc.vector.tensor_tensor(wgt_lo[:, q % 2, :], w, wgt_hi[:, q % 2, :], ALU.subtract).then_inc(S("wgt_ready"), 1)

            rest_u(0, 0)
            rest_u(1, 1)
            weigh(0, 0, True)
            rest_v(0, 0)
            rest_u(2, 2)
            weigh(1, 1, True)
            rest_v(1, 1)
            with dve.Fori(0, PKEYS // RING - 1) as i:
                for q in range(1, RING + 1):
                    rest_u((q + 2) % RING, i * RING + (q + 2))
                    weigh((q + 1) % RING, i * RING + (q + 1))
                    rest_v((q + 1) % RING, i * RING + (q + 1))
            rest_u(3, PKEYS - 1)
            for q in (2, 3):
                weigh(q, PKEYS - RING + q)
                rest_v(q, PKEYS - RING + q)
            dve.wait_ge(S("peer_ready"), 1)
            for n in range(8):
                dve.scalar_tensor_tensor(Xv[:, n, :], bank[n // 2][:, (n % 2) * T:(n % 2 + 1) * T], mod3[:, 40 + n, 0:1], Xv[:, n, :],
                                         ALU.mult, ALU.add).then_inc(S("x2_ready"), 1)
            dve.wait_ge(S("stdx_ready"), base("stdx_ready") + 1)
            dve.wait_ge(S("x2_ready"), base("x2_ready") + 8)
            link(dve.reciprocal(rsx[:, 0:T], rsx[:, 0:T]))
            link(dve.scalar_tensor_tensor(rsx[:, T:2 * T], bank[6][:, T:2 * T], 1.0 / D, rsx[:, 0:T], ALU.mult, ALU.mult))
            dve.tensor_tensor(rsx[:, T:2 * T], rsx[:, T:2 * T], rsx[:, 0:T], ALU.mult).then_inc(S("ms_mix_ready"), 1)
            dve.tensor_tensor(fg_mix, v("final_norm_g", 0, 8), v("norm_mix_g", 0, 8), ALU.mult).then_inc(S("fg_mix_ready"), 1)
            dve.tensor_tensor(lbd, v("lb", 0, 4), v("lb", 4, 4), ALU.subtract).then_inc(S("lbd_ready"), 1)
            dve.wait_ge(S("stdx_ready"), base("stdx_ready") + 2)
            dve.wait_ge(S("fg_mix_ready"), 1)
            link(dve.reciprocal(rsx[:, T:2 * T], rsx[:, T:2 * T]))
            link(dve.tensor_tensor(rsx[:, T:2 * T], rsx[:, T:2 * T], rsx[:, 0:T], ALU.mult))
            for k in range(KT):
                dve.scalar_tensor_tensor(Hv[:, k, :], Xv[:, k, :], fg_mix[:, k:k + 1], rsx[:, T:2 * T], ALU.mult, ALU.mult).then_inc(S("H3_ready"), 1)
            dve.wait_ge(S("H3_ready"), base("H3_ready") + KT)
            for k in range(KT):
                dve.scalar_tensor_tensor(Xv[:, k, :], Xv[:, k, :], v("final_norm_g", k), rsx[:, 0:T], ALU.mult, ALU.mult).then_inc(S("x2n_ready"), 1)
            dve.wait_ge(S("lb_ready"), 1)
            link(dve.tensor_scalar(lb1, lb, -1.0, 1.0, ALU.mult, ALU.add))
            for i in range(4):
                ins = dve.tensor_scalar(ff[:, i, :], ff[:, i, :], lb1[:, i:i + 1], lb[:, i:i + 1], ALU.mult, ALU.add)
            ins.then_inc(S("f_ready"), 1)
            dve.wait_ge(S("f_ready"), 1)
            dve.tensor_scalar(kk, ff, -1.0, 1.0, ALU.mult, ALU.add).then_inc(S("kk_ready"), 1)
            dve.wait_ge(S("stdm_ready"), base("stdm_ready") + 1)
            link(dve.reciprocal(rsm, rsm))
            for k in range(KT):
                ins = dve.scalar_tensor_tensor(memn[:, k, :], memn[:, k, :], v("norm_mem_g", k), rsm, ALU.mult, ALU.mult)
            ins.then_inc(S("memn_ready"), 1)
            dve.wait_ge(S("logf_ready"), 1)
            for i in range(4 * TT):
                ins = dve.tensor_tensor_scan(cum[:, i * P:(i + 1) * P], ones, DE[:, i * P:(i + 1) * P], 0.0, ALU.mult, ALU.add)
            link(ins)
            dve.memset(QE, 0.0)
            dve.memset(KE, 0.0)
            link(dve.memset(scT, 0.0))
            dve.wait_ge(S("masks_in"), 16)
            dve.wait_ge(S("kk_ready"), 1)
            dve.wait_ge(S("taken2"), 8)
            kkf, qqf = (x.rearrange("p c t -> p (c t)") for x in (kk, qq))
            sc8 = scT.rearrange("p h t n -> p (h t) n")

            def take_level(n, mask):
                dve.wait_ge(S("level_mm"), n + 1)
                for b in range(2):
                    ins = dve.copy_predicated(sc8[:, 4 * b:4 * b + 4, :], wide(mask, 4).bitcast(U32), three(bank[4 + b][:], 4))
                ins.then_inc(S("level_taken"), 1)

            for lev in range(LEVELS + 1):
                half = 1 << lev
                a, b = ([x.rearrange("p (m z n) -> p m z n", z=2, n=half)[:, :, z, :] for x in (cum, DE, QE, KE, kkf, qqf)]
                        for z in range(2))
                cum0, D0, _, K0, k0, _ = a
                cum1, D1, Q1, _, _, q1 = b
                ref = cum0[:, :, half - 1:half].broadcast_to([P, 4 * T // (2 * half), half])
                if lev >= 1:
                    dve.wait_ge(S("qke_ready"), lev)
                dve.tensor_tensor(D0, ref, cum0, ALU.subtract)
                if lev < LEVELS:
                    ins = dve.tensor_tensor(D1, cum1, ref, ALU.subtract)
                else:
                    ins = dve.tensor_copy(D1, cum1)
                ins.then_inc(S("dist_ready"), 1)
                if lev >= 1:
                    take_level(lev - 1, masks[:, lev - 1, :])
                dve.wait_ge(S("decay_ready"), lev + 1)
                dve.tensor_tensor(K0, k0, D0, ALU.mult)
                dve.tensor_tensor(Q1, q1, D1, ALU.mult).then_inc(S("qke_ready"), 1)
            take_level(LEVELS, ident)
            dve.wait_ge(S("taken2"), SECOND_ACT.index(("cg", 3)) + 1)
            dve.memset(up[:, :, 0:CONV_K - 1], 0.0)
            link(dve.tensor_tensor(up[:, :, CONV_K - 1:], caT, sgate, ALU.mult))
            n_tap = [0]
            for j in range(CONV_K):
                for i in range(4):
                    w = v("conv_w", i * CONV_K + j)
                    if j == 0:
                        ins = dve.tensor_scalar(cv[:, i, :], up[:, i, 0:T], w, v("conv_b", i), ALU.mult, ALU.add)
                    else:
                        dve.wait_ge(S("taps"), 4 * (j - 1) + i + 1)
                        ins = dve.scalar_tensor_tensor(cv[:, i, :], up[:, i, j:j + T], w, cv[:, i, :], ALU.mult, ALU.add)
                    ins.then_inc(S("taps"), 1)
            dve.wait_ge(S("taps"), 4 * CONV_K)
            dve.tensor_copy(mean[:, 0:1], cv[:, 0, 0:1]).then_inc(S("conv_ready"), 1)
            for n in range(2):
                dve.wait_ge(S("stdh_ready"), base("stdh_ready") + n + 1)
                link(dve.reciprocal(rsh[:, n * 512:(n + 1) * 512], rsh[:, n * 512:(n + 1) * 512]))
                o_ = och[:, 2 * n:2 * n + 2, :]
                link(dve.scalar_tensor_tensor(o_, o_, v("onorm_g"), three(rsh[:, n * 512:(n + 1) * 512], 2), ALU.mult, ALU.mult))
                ins = dve.tensor_tensor(o_, o_, gg[:, 2 * n:2 * n + 2, :], ALU.mult)
                ins.then_inc(S("och_normed"), 2)
            dve.wait_ge(S("meanc_ready"), base("meanc_ready") + 1)
            link(dve.tensor_scalar(mean, bank[6][:, 0:T], 1.0 / CC, None, ALU.mult))
            dve.tensor_tensor(cv, cv, wide(mean, 4), ALU.subtract).then_inc(S("conv_centred"), 1)
            dve.wait_ge(S("stdc_ready"), base("stdc_ready") + 1)
            link(dve.reciprocal(rstdc, rstdc))
            dve.wait_ge(S("conv_centred"), 1)
            dve.tensor_tensor(cv, cv, wide(rstdc, 4), ALU.mult).then_inc(S("conv_normed"), 1)
            for i in range(4):
                second_done(dve, "ho", i)
                dve.tensor_tensor(grs[:, 2 * i:2 * i + 2, :], grs[:, 2 * i:2 * i + 2, :], three(second_bank("ho", i)[:], 2), ALU.mult).then_inc(S("merge_taken"), 1)
            for i in range(4):
                second_done(dve, "co", i)
                dve.tensor_tensor(gcs[:, 2 * i:2 * i + 2, :], gcs[:, 2 * i:2 * i + 2, :], three(second_bank("co", i)[:], 2), ALU.mult).then_inc(S("merge_taken"), 1)
                dve.wait_ge(S("merge_taken"), 5 + i)
                dve.tensor_tensor(gcs[:, 2 * i:2 * i + 2, :], gcs[:, 2 * i:2 * i + 2, :], grs[:, 2 * i:2 * i + 2, :], ALU.add).then_inc(S("merged"), 1)
            dve.wait_ge(S("x2n_ready"), base("x2n_ready") + KT)
            for i in range(8):
                second_done(dve, "mix", i)
                dve.tensor_tensor(Xv[:, i, :], second_bank("mix", i)[:, 0:T], Xv[:, i, :], ALU.add).then_inc(S("x3_ready"), 1)
            dve.wait_ge(S("stdn_ready"), base("stdn_ready") + 1)
            link(dve.reciprocal(rsn, rsn))
            dve.wait_ge(S("x3_ready"), base("x3_ready") + 8)
            for k in range(KT):
                dve.scalar_tensor_tensor(Hv[:, k, :], Xv[:, k, :], v("norm_xa_g", k), rsn, ALU.mult, ALU.mult).then_inc(S("H4_ready"), 1)
            for h in range(4):
                c = slice(2 * h, 2 * h + 2)
                dve.wait_ge(S("xscores_ready"), h + 1)
                link(dve.reduce_max(xmx[:, c], three(bank[4 + h % 2][:], 2), AX))
                dve.tensor_scalar(xnmx[:, c], xmx[:, c], -1.0 / 16.0, None, ALU.mult).then_inc(S("xmax_ready"), 1)
            for h in range(4):
                c = slice(2 * h, 2 * h + 2)
                dve.wait_ge(S("xexp_ready"), h + 1)
                link(dve.reciprocal(xri[:, c], xrs[:, c]))
                dve.tensor_tensor(xP[:, h, :, :], xP[:, h, :, :], each(xri[:, c], T), ALU.mult).then_inc(S("xP_ready"), 1)
            for h in range(4):
                dve.wait_ge(S("xpv_ready"), h + 1)
                dve.tensor_copy(xo[:, 2 * h:2 * h + 2, :], three(bank[4 + h % 2][:], 2)).then_inc(S("xo_taken"), 1)
            for i in range(8):
                second_done(dve, "xo", i)
                dve.tensor_tensor(Xv[:, i, :], second_bank("xo", i)[:, 0:T], Xv[:, i, :], ALU.add).then_inc(S("x4_ready"), 1)
            dve.memset(zeros, 0.0).then_inc(S("zeros5_ready"), 1)
            dve.wait_ge(S("std5_ready"), base("std5_ready") + 1)
            link(dve.reciprocal(rs5, rs5))
            dve.wait_ge(S("x4_ready"), base("x4_ready") + 8)
            for k in range(KT):
                dve.scalar_tensor_tensor(Hv[:, k, :], Xv[:, k, :], v("norm_ffn_g", k), rs5, ALU.mult, ALU.mult).then_inc(S("H5_ready"), 1)
            link(dve.memset(g8, -3.0e38))
            dve.wait_ge(S("logits_mm"), 1)
            dve.wait_ge(S("router_in"), 32)
            link(dve.tensor_tensor(logit, three(bank[7][:, 0:72], TT), wide(r_b, TT), ALU.add))
            link(dve.tensor_copy(g8[:, :, 0:GROUPS], logit[:, :, 0:GROUPS]))
            for tt in range(TT):
                ins = dve.max(gm8[:, tt, :], g8[:, tt, :])
            link(ins)
            for tt in range(TT):
                dve.max_index(gi8[:, tt, :], gm8[:, tt, :], g8[:, tt, :])
            link(dve.tensor_tensor(gex, logit[:, :, 0:GROUPS], gm8[:, :, 0:1].broadcast_to([P, TT, GROUPS]), ALU.subtract))
            ins = dve.tensor_copy(gif, gi8[:, :, 0:1])
            ins.then_inc(S("shifted5"), 1)
            dve.wait_ge(S("shifted5"), 1)
            link(dve.tensor_tensor(grp, wide(cst("iota")[:, 0:GROUPS], TT), gif.broadcast_to([P, TT, GROUPS]), ALU.is_equal))
            el = logit[:, :, GROUPS:].rearrange("p t (g e) -> p t g e", g=GROUPS)
            link(dve.tensor_tensor(prod, el, grp.unsqueeze(3).broadcast_to([P, TT, GROUPS, PER_GROUP]), ALU.mult))
            for tt in range(TT):
                ins = dve.reduce_sum(i8[:, tt, :], prod[:, tt, :, :].rearrange("p g e -> p e g"), AX)
            link(ins)
            for tt in range(TT):
                ins = dve.max(em8[:, tt, :], i8[:, tt, :])
            link(ins)
            for tt in range(TT):
                ins = dve.max_index(ei8[:, tt, :], em8[:, tt, :], i8[:, tt, :])
            link(ins)
            dve.tensor_tensor(e21.unsqueeze(2), em8[:, :, 1:2], em8[:, :, 0:1], ALU.subtract).then_inc(S("shifted5"), 1)
            link(dve.tensor_copy(eif, ei8[:, :, 0:2]))
            dve.scalar_tensor_tensor(eid, gif.broadcast_to([P, TT, TOP_K]), float(PER_GROUP), eif, ALU.mult, ALU.add).then_inc(S("eid_ready"), 1)
            dve.wait_ge(S("exp5_ready"), 1)
            dve.wait_ge(S("eid_ready"), 1)
            link(dve.reduce_sum(gsm, gex, AX))
            link(dve.scalar_tensor_tensor(den, e21, 1.0, gsm, ALU.add, ALU.mult))
            link(dve.reciprocal(w12[:, :, 0], den))
            link(dve.tensor_tensor(w12[:, :, 1], w12[:, :, 0], e21, ALU.mult))
            for tt in range(TT):
                ins = dve.tensor_scalar(chosen[:, tt, :], cst("iota")[:, 0:EXPERTS], eid[:, tt, 0:1], None, ALU.is_equal)
                dve.tensor_scalar(weight[:, tt, :], cst("iota")[:, 0:EXPERTS], eid[:, tt, 0:1], w12[:, tt, 0:1], ALU.is_equal, ALU.mult)
            oh, ohw = three(scr[:, 0:64], TT), three(scr[:, 72:136], TT)
            for tt in range(TT):
                dve.tensor_scalar(oh[:, tt, :], cst("iota")[:, 0:EXPERTS], eid[:, tt, 1:2], None, ALU.is_equal)
                ins = dve.tensor_scalar(ohw[:, tt, :], cst("iota")[:, 0:EXPERTS], eid[:, tt, 1:2], w12[:, tt, 1:2], ALU.is_equal, ALU.mult)
            link(ins)
            dve.tensor_tensor(chosen, chosen, oh, ALU.add).then_inc(S("chosen_ready"), 1)
            dve.tensor_tensor(weight, weight, ohw, ALU.add).then_inc(S("weight_ready"), 1)
            dve.wait_ge(S("places_mm"), 1)
            dve.tensor_scalar(cmp4, cst("iota")[:, 0:4], float(CAP), None, ALU.mult)
            dve.tensor_copy(place, three(bank[6][:, 0:64], TT))
            link(dve.reduce_max(most, bank[6][:, 64:96], AX))
            link(dve.tensor_scalar(cmp4, cmp4, most, None, ALU.is_lt))
            link(dve.reduce_sum(rnd, cmp4, AX))
            dve.tensor_copy(rounds, rnd).then_inc(S("rounds_ready"), 1)
            dve.wait_ge(S("rounds_ready"), 1)
            dve.wait_ge(S("weight_ready"), 1)
            n = dve.value_load(rounds[0:1, :], min_val=1, max_val=4)
            iota_cap = cst("iota")[:, 0:CAP]

            def one_hot(out, scale, p):
                for tt in range(TT):
                    for a in range(2):
                        e = slice(2 * p + a, 2 * p + a + 1) if isinstance(p, int) else bass.ds(p * 2 + a, 1)
                        ins = nc.vector.tensor_scalar(out[:, tt, a * CAP:(a + 1) * CAP], iota_cap, place[:, tt, e], scale[:, tt, e],
                                                      ALU.is_equal, ALU.mult)
                return ins

            def select(q, p):
                dve.wait_ge(S("gather_mm"), q)
                one_hot(sel, chosen, p).then_inc(S("sel_ready"), 1)

            def middle(q, p):
                one_hot(selw, weight, p).then_inc(S("selw_ready"), 1)
                dve.wait_ge(S("silu_ready"), q + 1)
                dve.wait_ge(S("up_mm"), q + 1)
                nc.vector.tensor_tensor(hid, silu, bank[5][:], ALU.mult).then_inc(S("hid_ready"), 1)
                dve.wait_ge(S("turn_mm"), q + 1)
                nc.vector.tensor_copy(hidT.rearrange("p k n -> p (k n)"), bank[4][:]).then_inc(S("hidT_ready"), 1)
                dve.wait_ge(S("selT_mm"), q + 1)
                nc.vector.tensor_copy(selwT, bank[5][:, 0:T]).then_inc(S("selwT_ready"), 1)

            with dve.Fori(0, n) as r:
                q0 = r * 16
                one_hot(sel, chosen, 0).then_inc(S("sel_ready"), 1)
                with dve.Fori(0, EXPERTS // 2 - 1) as i:
                    select(q0 + i + 1, i + 1)
                    middle(q0 + i, i)
                middle(q0 + 15, 15)
                nc.vector.tensor_scalar(place, place, -float(CAP), None, ALU.add).then_inc(S("place_moved"), 1)
                dve.wait_ge(S("place_moved"), r + 1)
            dve.wait_ge(S("moe_mm"), 1)
            for m in range(4):
                h_ = slice((m % 2) * 512, (m % 2 + 1) * 512)
                dve.tensor_tensor(x5[:, m // 2, h_], bank[m][:], x_tok[:, m // 2, h_], ALU.add).then_inc(S("x5_ready"), 1)
            dve.wait_ge(S("final_in"), 16)
            for tt in range(TT):
                dve.wait_ge(S("std6_ready"), base("std6_ready") + tt + 1)
                link(dve.reciprocal(ri5[:, tt:tt + 1], ss5[:, tt:tt + 1]))
                dve.scalar_tensor_tensor(x5[:, tt, :], x5[:, tt, :], ri5[:, tt:tt + 1], fin_g, ALU.mult, ALU.mult).then_inc(S("out_ready"), 1)


def lay_out(inputs):
    g = {k: np.asarray(a) for k, a in inputs.items()}

    def features(a):
        a = a.T
        return np.ascontiguousarray(a.reshape(-1, P, a.shape[1]).transpose(1, 0, 2)).reshape(P, -1)

    def tiles(w, width=P):
        k, n = w.shape
        return np.ascontiguousarray(w.reshape(k // P, P, n // width, width).transpose(2, 1, 0, 3)).reshape(n // width, P, -1)

    def rows(w):
        e, k, n = w.shape
        return np.ascontiguousarray(w.reshape(e, k // P, P, n).transpose(0, 2, 1, 3)).reshape(e, P, -1)

    def col(a):
        return a.reshape(-1, P).T

    o = {}
    o["xT"], o["ctxT"], o["memT"] = features(g["x"][0]), features(g["ctx"][0]), features(g["mem_2"][0])
    o["cT"] = np.ascontiguousarray(np.stack([col(g["c"][0]), col(g["c_ctx"])], 2)).reshape(P, 16)
    vec = {"b_mod": col(g["b_mod"][0])}
    for n in ("norm1_g", "norm2_g"):
        vec[n] = col(g[n][0])
    vec["final_norm_g"] = col(g["final_norm_g"])
    for n in ("norm_mix_g", "norm_xa_g", "norm_mem_g", "norm_ffn_g", "conv_b", "conv_ln_g", "conv_ln_b"):
        vec[n] = col(g[n + "_2"][0])
    vec["lb"] = np.concatenate([col(g["hgrn_lb_logits_2"][0]), col(g["hgrn_lb_logits_2"][1])], 1)
    vec["onorm_g"], vec["subln_g"] = col(g["hgrn_onorm_g_2"][0]), col(g["diff_subln_g"][0])
    vec["gq_g"] = np.tile(g["gqa_q_norm_g"][0], 2)[:, None]
    vec["gk_g"] = np.tile(g["gqa_k_norm_g"][0], 2)[:, None]
    for n, k in (("lam_q", "q"), ("lam_k", "k")):
        vec[n] = np.zeros((P, 2), np.float32)
        vec[n][:HD, 0], vec[n][:HD, 1] = g[f"diff_l{k}1"][0], g[f"diff_l{k}2"][0]
    vec["conv_w"] = np.ascontiguousarray(g["conv_w_2"][0].reshape(CONV_K, 4, P).transpose(2, 1, 0)).reshape(P, -1)
    o["vec"] = np.concatenate([vec[n] for n in VEC], 1)
    heads = [0, 4, 1, 5, 2, 6, 3, 7]
    w_in = tiles(g["w_in"][0])
    gq = g["w_in"][0][:, 1536:2048].reshape(D, 8, HD)[:, heads].reshape(D, 512)
    first = {"mod": tiles(g["w_mod"][0]), "dq": w_in[0:4], "dk": w_in[4:8], "dv": w_in[8:12], "gq": tiles(gq),
             "gk": w_in[16:17], "gv": w_in[17:18]}
    w_out = g["w_out"][0]
    w_out = np.concatenate([w_out[:512], w_out[512:].reshape(8, HD, D)[heads].reshape(512, D)])
    first["out"], first["wq"] = tiles(w_out), tiles(g["peer_wq"][0])
    o["first"] = pairs([first[what][i] for what, i in FIRST])
    o["subkeys"] = np.ascontiguousarray(g["peer_subkeys"][0].reshape(16, PKEYS, P).transpose(2, 0, 1)).reshape(P, 2048)
    u = g["peer_u"][0].reshape(PKEYS, PKEYS, KT, P).transpose(1, 3, 2, 0).reshape(PKEYS, P, 1, UNIT)
    w = g["peer_v"][0].reshape(PKEYS, PKEYS, 1, D).transpose(1, 0, 2, 3)
    o["peer"] = np.concatenate([u, w], 2).reshape(PKEYS, P, 2 * UNIT)
    s, at = g["w_in_2"][0], 0
    second = {}
    for n, w in (("ca", 512), ("cg", 512), ("q", 512), ("f", 512), ("i", 512), ("g", 512), ("gc", 1024), ("gr", 1024)):
        second[n] = tiles(s[:, at:at + w])
        at += w
    second["co"], second["ho"] = tiles(g["conv_w_out_2"][0], 256), tiles(g["hgrn_w_out_2"][0], 256)
    for n, k in (("mix", "w_mix_out_2"), ("xq", "xa_w_q_2"), ("xk", "xa_w_k_2"), ("xv", "xa_w_v_2"), ("xo", "xa_w_o_2")):
        second[n] = tiles(g[k][0])
    o["second"] = pairs([second[what][i] for what, i in SECOND])
    o["moe_gate"] = rows(g["moe_w_gate_2"][0])
    o["moe_up"] = rows(g["moe_w_up_2"][0])
    o["moe_down"] = rows(g["moe_w_down_2"][0])
    o["router_w"] = np.ascontiguousarray(np.concatenate([g["router_group_w_2"][0], g["router_expert_w_2"][0]], 1)
                                         .reshape(KT, P, 36).transpose(1, 0, 2)).reshape(P, -1)
    o["router_b"] = np.concatenate([g["router_group_b_2"][0], g["router_expert_b_2"][0]])[None]
    o["final_g"] = g["final_norm_g_2"][None]
    c = {"ident": np.eye(P), "ones": np.ones((P, P)), "halves": np.kron(np.eye(2), np.ones((HD, HD)))}
    r = np.arange(P)
    swap = np.zeros((P, P))
    first_half = r % 32 < 16
    swap[r[first_half] + 16, r[first_half]] = -1.0
    swap[r[~first_half] - 16, r[~first_half]] = 1.0
    c["swap"] = swap
    freq = (np.float32(10000.0) ** (-np.arange(16, dtype=np.float32) / np.float32(16))).astype(np.float32)
    tok = np.arange(T)
    grid = np.where(((r // 32) % 2 == 0)[:, None], (tok // 64)[None], (tok % 64)[None]).astype(np.float32)
    ang = (grid * freq[r % 16][:, None]).astype(np.float32)
    c["cos"], c["sin"] = np.cos(ang), np.sin(ang)
    c["iota"] = np.tile(np.arange(P), (P, 1))
    c["before"] = (r[:, None] < r[None]) * 1.0
    o["const"] = np.concatenate([c[n] for n in CONST], 1).astype(np.float32)
    masks = []
    for lev in range(LEVELS):
        half = 1 << lev
        same = (r[:, None] // (2 * half)) == (r[None] // (2 * half))
        masks.append(same & (r[:, None] % (2 * half) < half) & (r[None] % (2 * half) >= half))
    o["masks"] = np.concatenate(masks, 1).astype(np.float32)
    return o


def pairs(units):
    a = np.stack(units).reshape(len(units) // 2, 2, P, UNIT).transpose(0, 2, 1, 3)
    return np.ascontiguousarray(a).reshape(len(units) // 2, P, 2 * UNIT)


def kernel(**inputs):
    import concourse.bacc as bacc
    from concourse.bass_utils import run_bass_kernel_spmd
    nc = bacc.Bacc("TRN2", target_bir_lowering=False, num_devices=1)
    arrays, dram = {}, {}
    for name, a in lay_out(inputs).items():
        arrays[f"in_{name}_dram"] = a
        dram[name] = nc.dram_tensor(f"in_{name}_dram", a.shape, F32, kind="ExternalInput").ap()
    dram["out"] = nc.dram_tensor("out_dram", (T, D), F32, kind="ExternalOutput").ap()
    build(nc, dram)
    r = run_bass_kernel_spmd(nc, [arrays], core_ids=[0])
    return r.results[0]["out_dram"].reshape(1, T, D)
```

```python
import math
from contextlib import ExitStack

import numpy as np
import concourse.bass as bass
from concourse import mybir

F32 = mybir.dt.float32
F32R = mybir.dt.float32r
U32 = mybir.dt.uint32
I32 = mybir.dt.int32
ALU = mybir.AluOpType
ACT = mybir.ActivationFunctionType
AX = mybir.AxisListType.X

P = 128
D = 1024
KT = D // P
T = 256
TT = T // P
HD = 64
NH_DIFF = 4
EPS = 1e-6
LAMBDA_INIT = 0.8 - 0.6 * math.exp(-0.3 * 0)
UNIT = 1024
RING = 4
PH, PKEYS, PTOP = 8, 128, 16
CONV_K, CC = 31, 512
GROUPS, PER_GROUP, EXPERTS = 4, 8, 32
FF = 512
TOP_K = 2
CAP = 64
POOL_TOKENS = (3, 6, 7)
CONV_DVE = 3
LEVELS = 7

W_IN_UNITS = [("dk", i) for i in range(4)] + [("gk", 0)] + [("dq", i) for i in range(4)] \
    + [("gq", i) for i in range(4)] + [("gv", 0)] + [("dv", i) for i in range(4)]


def plan_first():
    return [("mod", n) for n in range(16)] + W_IN_UNITS + [("out", n) for n in range(8)] + [("wq", n) for n in range(16)]


def plan_second():
    units = []
    for what, a, b in (("f", 0, 4), ("q", 0, 4), ("i", 0, 4), ("gr", 0, 4), ("ca", 0, 4), ("cg", 0, 4), ("g", 0, 4), ("gc", 0, 8),
                       ("gr", 4, 8), ("xk", 0, 8), ("xv", 0, 8), ("ho", 0, 4), ("co", 0, 4), ("mix", 0, 8), ("xq", 0, 8), ("xo", 0, 8)):
        units += [(what, i) for i in range(a, b)]
    return units


FIRST, SECOND = plan_first(), plan_second()
MOD_REST = 32
SECOND_ACT = [u for u in SECOND if u[0] not in ("co", "ho", "mix", "xo")]
BETWEEN = SECOND[SECOND.index(("ca", 0)):][:3 * (LEVELS + 1)]
PAIRS1, PAIRS_PEER, PAIRS2 = len(FIRST) // 2, PKEYS, len(SECOND) // 2

CONST = {}
_at = 0
for _n, _w in (("ident", 128), ("ones", 128), ("halves", 128), ("swap", 128), ("cos", 256), ("sin", 256),
               ("iota", 128), ("before", 128)):
    CONST[_n] = (_at, _w)
    _at += _w
NCONST = _at
VEC = {}
_at = 0
for _n, _w in (("b_mod", 48), ("norm1_g", 8), ("norm2_g", 8), ("final_norm_g", 8), ("norm_mix_g", 8),
               ("norm_xa_g", 8), ("norm_mem_g", 8), ("norm_ffn_g", 8), ("conv_b", 4), ("conv_ln_g", 4),
               ("conv_ln_b", 4), ("lb", 8), ("onorm_g", 1), ("subln_g", 1), ("gq_g", 1), ("gk_g", 1),
               ("lam_q", 2), ("lam_k", 2), ("conv_w", 4 * CONV_K)):
    VEC[_n] = (_at, _w)
    _at += _w
NVEC = _at


FAMILIES = {
    "score_products_done": (("scores_ready", 32), ("xscores_ready", 4)),
    "value_products_done": (("pv_ready", 16), ("xpv_ready", 4)),
    "probabilities_ready": (("P_ready", 16), ("xP_ready", 4)),
    "maxima_ready": (("nmax_ready", 32), ("xmax_ready", 4)),
    "exponentials_ready": (("exp_ready", 32), ("xexp_ready", 4)),
    "squares_ready": (("sq1_ready", 2), ("sqg_ready", 5), ("sqo_ready", 2), ("sq2_ready", 8), ("sqx_ready", 8), ("sqm_ready", 1), ("sqh_ready", 2), ("sqc_ready", 1), ("sqn_ready", 8), ("sq5_ready", 8)),
    "deviation_ready": (("std1_ready", 1), ("stdg_ready", 3), ("stdo_ready", 2), ("std2_ready", 1), ("stdx_ready", 2), ("stdm_ready", 1), ("stdh_ready", 2), ("stdc_ready", 1), ("stdn_ready", 1), ("std5_ready", 1), ("std6_ready", 2)),
    "sums_ready": (("ss1_ready", 1), ("ssg_ready", 3), ("sso_ready", 2), ("ss2_ready", 1), ("ssx_ready", 1), ("ssm_ready", 1), ("ssh_ready", 2), ("meanc_ready", 1), ("varc_ready", 1), ("ssn_ready", 1), ("ss5_mm", 1)),
    "h_ready": (("h_x_ready", 8), ("H3_ready", 8), ("H4_ready", 8), ("H5_ready", 8)),
    "x_ready": (("x1_ready", 8), ("x2_ready", 8), ("x2n_ready", 8), ("x3_ready", 8), ("x4_ready", 8)),
}
FAMILY, BASE = {}, {}
for _f, _stages in FAMILIES.items():
    _at = 0
    for _n, _w in _stages:
        FAMILY[_n], BASE[_n] = _f, _at
        _at += _w


def base(name):
    return BASE[name]


def build(nc, t):
    ctx = ExitStack()
    with ctx:
        place_of = {}

        def sb(name, cols, dt=F32):
            tensor = ctx.enter_context(nc.sbuf_tensor(name, [P, cols], dt))
            place_of[name] = nc.sbuf_base - 4 * cols
            return tensor

        sems = {}

        def S(name):
            name = FAMILY.get(name, name)
            if name not in sems:
                sems[name] = ctx.enter_context(nc.semaphore(name))
            return sems[name]

        def three(ap, n):
            return ap.rearrange("p (a b) -> p a b", a=n)

        def wide(ap, n):
            return ap.unsqueeze(1).broadcast_to([P, n, ap.shape[1]])

        def each(ap, n):
            return ap.unsqueeze(2).broadcast_to([P, ap.shape[1], n])

        const = sb("const", NCONST)
        vec = sb("vec", NVEC)
        modT = sb("modT", 96)
        X = sb("X", KT * T)
        H = sb("H", KT * T)
        ring = sb("ring", RING * 2 * UNIT)
        big = sb("big", P * T)
        misc = sb("misc", 2300 + 4096)
        small, work = misc[:, 0:2300], misc[:, 2300:6396]
        bank = [ctx.enter_context(nc.psum_tensor(f"bank{i}", [P, 512], F32)) for i in range(8)]

        def cst(name):
            a, w = CONST[name]
            return const[:, a:a + w]

        def v(name, i=0, n=1):
            a, _ = VEC[name]
            return vec[:, a + i:a + i + n]

        def area(start, cols):
            return big[:, start:start + cols]

        ident, ones, halves, swap = cst("ident"), cst("ones"), cst("halves"), cst("swap")
        Xv, Hv = three(X[:], KT), three(H[:], KT)
        mod3 = three(modT[:], 48)
        eps = small[:, 0:1]
        cT = small[:, 8:24]
        csT = small[:, 24:40]
        gs_x, gs_c = small[:, 40:48], small[:, 48:56]
        gain_dv = small[:, 56:57]
        lam = small[:, 57:58]
        lam_e = small[:, 60:62]
        lprod = small[:, 62:64]
        gs2 = small[:, 64:72]
        g_tmp = small[:, 72:80]
        mx, nmx, rsum, rinv = (small[:, 80 + 6 * i:86 + 6 * i] for i in range(4))

        ctxT = three(area(0, 2048), KT)
        hAll = three(area(2048, 4096), KT)
        sq = three(area(6144, 4096), KT)
        dkT = three(area(10240, 2048), 4)
        gkT = area(12288, 512)
        dqT = three(area(12800, 1024), 4)
        gqT = three(area(13824, 1024), 4)
        dvs = three(area(14848, 2048), 4)
        gvs = three(area(16896, 512), 4)
        Pb = area(17408, 3072).rearrange("p (i r k) -> p i r k", i=3, r=2)
        PTb = area(0, 2048).rearrange("p (i r k q) -> p i r k q", i=2, r=2, k=4)
        oT = three(area(21504, 2048), 8)
        rt = area(23552, 2048).rearrange("p (a b c) -> p a b c", a=4, b=2)
        rs1 = area(25600, 512)
        rsg = area(26112, 1024)
        rsk = area(27136, 512)
        mod_acc = three(area(27648, 4096), 32)
        mod_in = (misc[:, 252:2300], misc[:, 4348:6396])
        mod_rows4 = area(17408, 2048)

        qh = area(0, 512).rearrange("p (s t) -> p s t", s=2)
        sc = area(512, 512).rearrange("p (s t n) -> p s t n", s=2, t=TT)
        sc2 = area(1024, 512).rearrange("p (s t n) -> p s t n", s=2, t=TT)
        sv = area(1536, 512).rearrange("p (t h n) -> p t h n", t=TT, h=16)
        si = area(2048, 512).bitcast(U32).rearrange("p (t h n) -> p t h n", t=TT, h=16)
        sif = area(2560, 512).rearrange("p (t h n) -> p t h n", t=TT, h=16)
        cand = area(3072, 1024).rearrange("p (s t n) -> p s t n", s=2, t=TT)
        cand2 = area(4096, 1024).rearrange("p (s t n) -> p s t n", s=2, t=TT)
        best = area(5120, 256).rearrange("p (t h n) -> p t h n", t=TT, h=PH)
        pos = area(5376, 256).bitcast(U32).rearrange("p (t h n) -> p t h n", t=TT, h=PH)
        digit_u = area(5632, 512).bitcast(U32).rearrange("p (d t k) -> p d t k", d=2, t=TT)
        digit = area(6144, 512).rearrange("p (d t k) -> p d t k", d=2, t=TT)
        gate = area(6656, 256).rearrange("p (t h n) -> p t h n", t=TT, h=PH)
        ids = area(6912, 512).rearrange("p (d t k) -> p d t k", d=2, t=TT)
        pick = area(8192, 4096).rearrange("p (t h n a) -> p t h n a", t=TT, h=PH, n=PTOP)
        gsum, grec = small[:, 104:120], small[:, 120:136]
        GIJ = three(work[:, 2048:2816], 3)
        left, right = three(work[:, 0:1024], 8), three(work[:, 1024:2048], 8)
        H_parts, ring_parts, misc_parts, big_parts = (
            nc.alloc_sbuf_tensor_at(f"{name}_parts", [P, cols], F32R, offset=place_of[name]).ap()
            for name, cols in (("H", KT * T), ("ring", RING * 2 * UNIT), ("misc", 6396), ("big", P * T)))
        x_hi, x_lo = three(misc_parts[:, 2748:4796], KT), three(H_parts, KT)
        wgt_hi, wgt_lo = three(misc_parts[:, 4796:5308], 2), three(misc_parts[:, 5308:5820], 2)
        act_e = three(misc[:, 5820:6332], 2)
        fg2, gain2 = three(misc[:, 700:1724], KT), small[:, 650:658]
        u_hi, v_hi = misc_parts[:, 700:1724], misc_parts[:, 1724:2748]
        G = three(big[:], PKEYS)
        pool_ids = small[:, 660:668]
        zeros = small[:, 136:648]

        sqx = three(area(0, 2048), KT)
        rsx = area(13440, 512)
        up = area(0, 4 * (CONV_K - 1 + T)).rearrange("p (c t) -> p c t", c=4)
        cv = area(1152, 1024).rearrange("p (c t) -> p c t", c=4)
        caT = three(area(2176, 1024), 4)
        vi = three(area(3200, 1024), TT)
        ff = three(area(4224, 1024), 4)
        kk = three(area(5248, 1024), 4)
        qq = three(area(6272, 1024), 4)
        gg = three(area(7296, 1024), 4)
        cum = area(8320, 1024)
        DE = area(9344, 1024)
        QE, KE = area(10368, 1024), area(11392, 1024)
        scT = area(12416, 1024).rearrange("p (h t n) -> p h t n", h=4, t=TT)
        cross = three(area(13440, 512), 4)
        xv = three(area(13952, 2048), TT)
        xkT = three(area(16000, 2048), KT)
        memn = three(area(18048, 2048), KT)
        h_hi, h_lo = (three(big_parts[:, a:a + 2048], KT) for a in (20480, 22528))
        w_hi = [big_parts[:, a:a + UNIT] for a in (24576, 25600)]
        sqm = three(area(13952, 2048), KT)
        rsm = area(20096, 256)
        gcs, grs = three(work[:, 0:2048], KT), three(work[:, 2048:4096], KT)
        masks = three(small[:, 136:136 + 896], LEVELS)
        pool_product = small[:, 1040:1296]
        lb, lb1, lbd = small[:, 1512:1516], small[:, 1516:1520], small[:, 1520:1524]
        fg_mix = small[:, 1524:1532]
        sqc = three(area(8320, 1024), 4)
        sgate = cv
        mean, rstdc = area(9344, 256), area(9600, 256)
        och = three(area(5248, 1024), 4)
        sqh = three(area(6272, 1024), 4)
        rsh = area(10368, 1024)
        xaq = three(area(0, 2048), KT)
        xP = area(2048, 2048).rearrange("p (i t k) -> p i t k", i=4, t=TT)
        xPT = area(4096, 2048).rearrange("p (i k q) -> p i k q", i=4, k=TT)
        xo = three(area(6144, 2048), KT)
        sqn = three(area(8192, 2048), KT)
        rsn = area(10240, 256)
        xmx, xnmx, xrs, xri = (small[:, 1532 + 8 * i:1540 + 8 * i] for i in range(4))

        w_exp = [area(20480, 12288), area(8192, 12288)]
        gate_at = [[w[:, 0:4096] for w in w_exp], [ring[:, 4096 * a:4096 * (a + 1)] for a in range(2)]]
        w_gate = [[three(w, KT) for w in pair] for pair in gate_at]
        w_up = [three(w[:, 4096:8192], KT) for w in w_exp]
        w_down = [w[:, 8192:12288].rearrange("p (k n) -> p k n", k=4) for w in w_exp]
        h_tok, x_tok = three(area(0, 2048), TT), three(area(2048, 2048), TT)
        sq5, rs5 = three(area(4096, 2048), KT), area(6144, 256)
        hg = three(area(4096, 1024), KT)
        y_slot = area(6144, 1024)
        sel, selw = three(area(7168, 256), TT), three(area(7424, 256), TT)
        selwT = area(7680, 256)
        silu, hid = area(5120, 512), area(5632, 512)
        hidT = three(work[:, 0:512], 4)
        fin_g = work[:, 1024:2048]
        x5 = three(work[:, 2048:4096], TT)
        chosen, weight, place = (three(small[:, 1700 + 64 * i:1764 + 64 * i], TT) for i in range(3))
        r_w = three(small[:, 1892:2180], KT)
        r_b = small[:, 2180:2216]
        scr = area(7936, 256)
        logit = three(scr[:, 0:72], TT)
        g8, gm8, i8, em8 = (three(scr[:, 72 + 16 * i:88 + 16 * i], TT) for i in range(4))
        gi8, ei8 = (three(scr[:, 136 + 16 * i:152 + 16 * i].bitcast(U32), TT) for i in range(2))
        grp, gex = three(scr[:, 168:176], TT), three(scr[:, 176:184], TT)
        prod = scr[:, 184:248].rearrange("p (t g e) -> p t g e", t=TT, g=GROUPS)
        rr = small[:, 2216:2300]
        gif, eif, eid = three(rr[:, 0:2], TT), three(rr[:, 2:6], TT), three(rr[:, 6:10], TT)
        gsm, e21, den, w12 = rr[:, 10:12], rr[:, 12:14], rr[:, 14:16], three(rr[:, 16:20], TT)
        most, rnd = rr[:, 20:21], rr[:, 21:22]
        rounds = rr[:, 22:23].bitcast(I32)
        ss5, ri5 = rr[:, 24:26], rr[:, 26:28]
        cmp4 = rr[:, 28:32]
        fin_part = rr[:, 32:36]

        def unit(n):
            s = (n // 2) % RING
            a = (2 * s + n % 2) * UNIT
            return ring[:, a:a + UNIT].rearrange("p (k n) -> p k n", k=KT)

        def pair_landed(eng, n):
            eng.wait_ge(S(f"ring_full{n % RING}"), 16 * (n // RING + 1))

        def peer_unit(q, i, ring=ring):
            s = (PAIRS1 + q) % RING
            return ring[:, (2 * s + i) * UNIT:(2 * s + i + 1) * UNIT]

        def PT_bank(i, r):
            return 4 + i % 2 if i < 8 else 4 + r

        def second_done(eng, what, i):
            eng.wait_ge(S("second_unit_done"), SECOND.index((what, i)) + 1)

        def second_unit(n, ring=ring):
            s = (PAIRS1 + PAIRS_PEER + n // 2) % RING
            return ring[:, (2 * s + n % 2) * UNIT:(2 * s + n % 2 + 1) * UNIT]

        def second_bank(what, i):
            return bank[SECOND.index((what, i)) % 4]

        def first_done(eng, what, i):
            eng.wait_ge(S("first_unit_done"), FIRST.index((what, i)) + 1)

        def convolve(eng, tiles, taps):
            for j in range(CONV_K):
                for n, i in enumerate(tiles):
                    w = v("conv_w", i * CONV_K + j)
                    if j == 0:
                        ins = eng.tensor_scalar(cv[:, i, :], up[:, i, 0:T], w, v("conv_b", i), ALU.mult, ALU.add)
                    else:
                        eng.wait_ge(S(taps), len(tiles) * (j - 1) + n + 1)
                        ins = eng.scalar_tensor_tensor(cv[:, i, :], up[:, i, j:j + T], w, cv[:, i, :], ALU.mult, ALU.add)
                    ins.then_inc(S(taps), 1)

        block = ctx.enter_context(nc.Block())

        @block.sync
        def _(sp):
            def load_pair(n, src):
                s = n % RING
                sp.dma_start(ring[:, s * 2 * UNIT:(s + 1) * 2 * UNIT], src).then_inc(S(f"ring_full{s}"), 16)

            for n in range(PAIRS1):
                if n >= RING:
                    first_done(sp, *FIRST[2 * (n - RING) + 1])
                load_pair(n, t["first"][n])
            for j in range(RING):
                first_done(sp, *FIRST[2 * (PAIRS1 - RING + j) + 1])
                load_pair(PAIRS1 + j, t["peer"][j])
            with sp.Fori(0, PKEYS // RING - 1) as i:
                for q in range(RING):
                    sp.wait_ge(S("peer_pair_done"), i * RING + (q + 1))
                    s = (PAIRS1 + q) % RING
                    sp.dma_start(ring[:, s * 2 * UNIT:(s + 1) * 2 * UNIT], t["peer"].rearrange("j p c -> (j p) c")[bass.ds((i * RING + (RING + q)) * P, P), :]).then_inc(S(f"ring_full{s}"), 16)
            sp.wait_ge(S("x2_ready"), base("x2_ready") + 1)
            sp.dma_start(area(18048, 2048), t["memT"]).then_inc(S("mem_in"), 16)
            for m in range(PAIRS2):
                n = PAIRS1 + PAIRS_PEER + m
                if m < RING:
                    sp.wait_ge(S("peer_pair_done"), PAIRS_PEER - RING + m + 1)
                else:
                    second_done(sp, *SECOND[2 * (m - RING) + 1])
                load_pair(n, t["second"][m])
                if m == RING:
                    sp.dma_start(small[:, 136:136 + 128 * LEVELS], t["masks"]).then_inc(S("masks_in"), 16)
                if m in (6, 24, 26):
                    i = {6: 2, 24: 0, 26: 1}[m]
                    if m == 24:
                        second_done(sp, *BETWEEN[-1])
                    sp.dma_start(w_exp[0][:, 4096 * i:4096 * (i + 1)], t[("moe_gate", "moe_up", "moe_down")[i]][0]).then_inc(
                        S(("gates_in0", "ups_in", "downs_in")[i]), 16)
                if m == 12:
                    sp.dma_start(r_w.rearrange("p k n -> p (k n)"), t["router_w"]).then_inc(S("router_in"), 16)
                    sp.dma_start(r_b, t["router_b"].broadcast_to([P, 36])).then_inc(S("router_in"), 16)
            sp.wait_ge(S("xpv_ready"), base("xpv_ready") + 4)
            flat = {n: t[n].rearrange("e p c -> (e p) c") for n in ("moe_gate", "moe_up", "moe_down")}

            def load_gates(a, e, parity):
                src = t["moe_gate"][e] if isinstance(e, int) else flat["moe_gate"][bass.ds(e * P, P), :]
                sp.dma_start(gate_at[parity][a], src).then_inc(S(f"gates_in{parity}"), 16)

            def load_part(a, e, i):
                name = ("moe_gate", "moe_up", "moe_down")[i]
                src = t[name][e] if isinstance(e, int) else flat[name][bass.ds(e * P, P), :]
                sp.dma_start(w_exp[a][:, 4096 * i:4096 * (i + 1)], src).then_inc(S(("", "ups_in", "downs_in")[i]), 16)

            def load_ups_downs(q, p):
                for i, done in ((1, "up_mm"), (2, "down_mm")):
                    sp.wait_ge(S(done), q)
                    for a in range(2):
                        load_part(a, p * 2 + a, i)

            load_gates(1, 1, 0)
            load_part(1, 1, 1)
            load_part(1, 1, 2)
            second_done(sp, *SECOND[-1])
            for a in range(2):
                load_gates(a, 2 + a, 1)
            sp.wait_ge(S("x4_ready"), base("x4_ready") + 8)
            sp.dma_start(fin_g, t["final_g"].broadcast_to([P, D])).then_inc(S("final_in"), 16)
            with sp.Fori(0, EXPERTS // 4 - 1) as i:
                for odd in range(2):
                    q = i * 2 + (1 + odd)
                    sp.wait_ge(S("gate_mm"), q)
                    for a in range(2):
                        load_gates(a, q * 2 + (2 + a), odd)
                    load_ups_downs(q, q)
            load_ups_downs(EXPERTS // 2 - 1, EXPERTS // 2 - 1)
            sp.wait_ge(S("rounds_ready"), 1)
            n = sp.value_load(rounds[0:1, :], min_val=1, max_val=4)
            with sp.If(n > 1):
                with sp.Fori(1, n) as r:
                    with sp.Fori(0, EXPERTS // 4) as i:
                        for odd in range(2):
                            q, p = r * 16 + i * 2 + odd, i * 2 + odd
                            sp.wait_ge(S("gate_mm"), q - 1)
                            for a in range(2):
                                load_gates(a, p * 2 + a, odd)
                            load_ups_downs(q, p)
            for tt in range(TT):
                sp.wait_ge(S("out_ready"), tt + 1)
                sp.dma_start(t["out"][tt * P:(tt + 1) * P, :], x5[:, tt, :]).then_inc(S("out_written"), 16)
            sp.wait_ge(S("out_written"), 16 * TT)

        @block.gpsimd
        def _(pool):
            first_done(pool, "mod", 9)
            for m in range(MOD_REST // 2):
                if m >= 2:
                    pool.wait_ge(S("mod_pair_done"), m - 1)
                pool.dma_start(mod_in[m % 2], t["mod_rest"][m]).then_inc(S(f"mod_in{m % 2}"), 16)
            pool.dma_start(work[:, 0:2048], t["subkeys"]).then_inc(S("subkeys_in"), 16)
            pool.wait_ge(S("GIJ_ready"), 2)
            pool.sem_inc(S("pool_rows_ready"), 3)
            with pool.Fori(0, T // 8) as i:
                pool.wait_ge(S("pool_rows_ready"), i * 3 + 3)
                nc.gpsimd.sem_inc(S("pool_steps"), 1)
                nc.gpsimd.tensor_copy(pool_ids, GIJ[:, 2, bass.ds(i * 8, 8)]).then_inc(S("pool_ids_ready"), 1)
                pool.wait_ge(S("pool_ids_ready"), i + 1)
                for q in POOL_TOKENS:
                    if q in (3, 6):
                        pool.wait_ge(S("gates_mm"), i * 8 + (q - q % 4 + 4))
                        nc.gpsimd.sem_inc(S("pool_steps"), 1)
                    nc.gpsimd.tensor_scalar(right[:, q, :], cst("iota"), pool_ids[:, q:q + 1], None,
                                            ALU.is_equal).then_inc(S("pool_rows_ready"), 1)
            pool.wait_ge(S("up_ready"), 1)
            steps = 0
            for j in range(CONV_K):
                for i in range(CONV_DVE, 4):
                    w = v("conv_w", i * CONV_K + j)
                    if j == 0:
                        pool.tensor_scalar(cv[:, i, :], up[:, i, 0:T], w, v("conv_b", i), ALU.mult, ALU.add).then_inc(S("pool_taps"), 1)
                    else:
                        pool.wait_ge(S("pool_taps"), steps)
                        pool.tensor_scalar(pool_product, up[:, i, j:j + T], w, None, ALU.mult).then_inc(S("pool_taps"), 1)
                        steps += 1
                        pool.wait_ge(S("pool_taps"), steps)
                        pool.tensor_tensor(cv[:, i, :], cv[:, i, :], pool_product, ALU.add).then_inc(S("pool_taps"), 1)
                    steps += 1

        @block.scalar
        def _(act):
            chain = [0]

            def link(ins):
                chain[0] += 1
                ins.then_inc(S("act_own"), 1)
                act.wait_ge(S("act_own"), chain[0])

            act.dma_start(cT, t["cT"]).then_inc(S("c_in"), 16)
            act.dma_start(X[:], t["xT"]).then_inc(S("x_in"), 16)
            act.dma_start(const[:], t["const"]).then_inc(S("const_in"), 16)
            act.dma_start(area(0, 2048), t["ctxT"]).then_inc(S("ctx_in"), 16)
            act.dma_start(vec[:], t["vec"]).then_inc(S("vec_in"), 16)

            act.wait_ge(S("c_in"), 16)
            act.activation(csT, cT, ACT.Silu).then_inc(S("cs_ready"), 1)
            act.wait_ge(S("x_in"), 16)
            act.activation(sq[:, :, T:2 * T], Xv, ACT.Square).then_inc(S("sq1_ready"), 1)
            act.wait_ge(S("ctx_in"), 16)
            act.activation(sq[:, :, 0:T], ctxT, ACT.Square).then_inc(S("sq1_ready"), 1)
            act.wait_ge(S("ss1_ready"), base("ss1_ready") + 1)
            act.wait_ge(S("eps_ready"), 1)
            act.activation(rs1, bank[6][:], ACT.Sqrt, scale=1.0 / D, bias=eps).then_inc(S("std1_ready"), 1)
            for n in range(4):
                first_done(act, "mod", 4 * n + 3)
                act.activation(mod_rows4[0:2, n * 512:(n + 1) * 512], bank[n][0:2, :], ACT.Copy).then_inc(S("mod_rows_taken"), 1)
            act.wait_ge(S("lam_sums"), 1)
            act.activation(lam_e, bank[5][:, 0:2], ACT.Exp).then_inc(S("lam_exp"), 1)
            act.wait_ge(S("gs1_ready"), 1)
            for k in range(KT):
                act.wait_ge(S("normed1"), k + 1)
                act.activation(hAll[:, k, 0:T], hAll[:, k, 0:T], ACT.Identity, scale=gs_c[:, k:k + 1],
                               bias=mod3[:, k, 1:2]).then_inc(S("h_ctx_ready"), 1)
            dst = {"dk": lambda i: dkT[:, i, :], "gk": lambda i: gkT, "dq": lambda i: dqT[:, i, :],
                   "gq": lambda i: gqT[:, i, :], "gv": lambda i: gvs, "dv": lambda i: dvs[:, :, i * P:(i + 1) * P]}
            for n, (what, i) in enumerate(W_IN_UNITS):
                first_done(act, what, i)
                src = bank[n % 4][:, 0:T] if what in ("dq", "gq") else bank[n % 4][:]
                if what in ("gv", "dv"):
                    src = three(src, 4)
                act.activation(dst[what](i), src, ACT.Copy).then_inc(S("win_taken"), 1)
                if (what, i) == ("gk", 0):
                    act.wait_ge(S("win_taken"), n + 1)
                    act.activation(sq[:, 0, :], gkT, ACT.Square).then_inc(S("sqg_ready"), 1)
                if what == "gq":
                    act.wait_ge(S("win_taken"), n + 1)
                    act.activation(sq[:, 2 + i // 2, (i % 2) * T:(i % 2 + 1) * T], gqT[:, i, :], ACT.Square).then_inc(S("sqg_ready"), 1)
                if n in (8, 14, 15):
                    j = (8, 14, 15).index(n)
                    act.wait_ge(S("ssg_ready"), base("ssg_ready") + j + 1)
                    act.activation((rsk, rsg[:, 0:512], rsg[:, 512:1024])[j], bank[6][:], ACT.Sqrt, scale=1.0 / HD,
                                   bias=eps).then_inc(S("stdg_ready"), 1)
            def exps(i):
                for r in range(2):
                    act.wait_ge(S("nmax_ready"), base("nmax_ready") + 2 * i + r + 1)
                    c = 2 * (i % 3) + r
                    if i >= 3:
                        act.wait_ge(S("PT_ready"), i - 2)
                    act.activation(Pb[:, i % 3, r, :], bank[2 * (i % 2) + r][:], ACT.Exp, scale=HD ** -0.5,
                                   bias=nmx[:, c:c + 1], accum_out=rsum[:, c:c + 1]).then_inc(S("exp_ready"), 1)

            def take_PT(i):
                act.wait_ge(S("PT_ready"), i + 1)
                if i >= 2:
                    act.wait_ge(S("pv_ready"), base("pv_ready") + i - 1)
                for r in range(1 if i < 8 else 2):
                    ins = act.activation(PTb[:, i % 2, r, :, :].rearrange("p k q -> p (k q)"), bank[PT_bank(i, r)][:], ACT.Copy)
                ins.then_inc(S("PT_taken"), 1)

            for i in range(16 + 2):
                if i < 16:
                    exps(i)
                if i >= 2:
                    take_PT(i - 2)
                if i == 14:
                    act.wait_ge(S("o_taken"), 8)
                    for n in range(2):
                        act.activation(sq[:, n, :], oT[:, 2 * n:2 * n + 2, :].rearrange("p a b -> p (a b)"), ACT.Square).then_inc(S("sqo_ready"), 1)
            for n in range(2):
                act.wait_ge(S("sso_ready"), base("sso_ready") + n + 1)
                act.activation(rsg[:, n * 512:(n + 1) * 512], bank[n][:], ACT.Sqrt, scale=1.0 / P, bias=eps).then_inc(S("stdo_ready"), 1)
            for k in range(KT):
                act.wait_ge(S("x1_ready"), base("x1_ready") + k + 1)
                act.activation(sq[:, k, 0:T], Xv[:, k, :], ACT.Square).then_inc(S("sq2_ready"), 1)
            act.wait_ge(S("ss2_ready"), base("ss2_ready") + 1)
            act.activation(rs1[:, 0:T], bank[6][:, 0:T], ACT.Sqrt, scale=1.0 / D, bias=eps).then_inc(S("std2_ready"), 1)
            for k in range(KT):
                act.wait_ge(S("h2_scaled"), k + 1)
                act.activation(Hv[:, k, :], Hv[:, k, :], ACT.Identity, bias=mod3[:, 24 + k, 0:1]).then_inc(S("h2_ready"), 1)
            for n in range(16):
                first_done(act, "wq", n)
                if n >= 2:
                    act.wait_ge(S("keys_scored"), n - 1)
                act.activation(qh[:, n % 2, :], bank[n % 2][:, 0:T], ACT.Copy).then_inc(S("qh_ready"), 1)
                act.wait_ge(S("keys_scored"), n + 1)
                if n >= 2:
                    act.wait_ge(S("sc_used"), n - 1)
                act.activation(sc[:, n % 2, :, :].rearrange("p t n -> p (t n)"), bank[2 + n % 2][:, 0:T], ACT.Copy).then_inc(S("sc_ready"), 1)
            act.wait_ge(S("best_shifted"), 1)
            act.activation(gate.rearrange("p t h n -> p (t h n)"), gate.rearrange("p t h n -> p (t h n)"), ACT.Exp).then_inc(S("gate_exp"), 1)
            for tt in range(TT):
                act.wait_ge(S("GIJ_turned"), tt + 1)
                act.activation(GIJ[:, :, tt * P:(tt + 1) * P], three(bank[4 + tt][:, 0:384], 3), ACT.Copy).then_inc(S("GIJ_ready"), 1)
            act.sem_inc(S("gates_taken"), 4)
            with act.Fori(0, T // 16) as i:
                g = i * 4
                for q in range(4):
                    act.wait_ge(S("gates_mm"), g * 4 + (12 + 4 * q))
                    nc.scalar.activation(G[:, :, bass.ds(g * 4 + 4 * q, 4)], three(bank[4 + q][:], 4).rearrange("p t j -> p j t"),
                                         ACT.Copy).then_inc(S("gates_taken"), 1)
            act.activation(x_hi, Hv, ACT.Copy).then_inc(S("x_hi_ready"), 1)

            def lead_u(q, j, first=False):
                s = (PAIRS1 + q) % RING
                act.wait_ge(S(f"ring_full{s}"), j * (16 // RING) + (16 * ((PAIRS1 + q) // RING + 1) - q * (16 // RING)))
                if not first:
                    act.wait_ge(S("ux_ready"), j)
                nc.scalar.activation(u_hi, peer_unit(q, 0), ACT.Copy).then_inc(S("u_hi_ready"), 1)

            def lead_v(q, j, first=False):
                if not first:
                    act.wait_ge(S("peer_pair_done"), j)
                nc.scalar.activation(v_hi, peer_unit(q, 1), ACT.Copy).then_inc(S("v_hi_ready"), 1)

            def gelu(q, j, first=False):
                act.wait_ge(S("ux_ready"), j + 1)
                if not first:
                    act.wait_ge(S("wgt_ready"), j - 1)
                nc.scalar.activation(act_e[:, q % 2, :], bank[4 + q % 2][:, 0:T], ACT.Gelu).then_inc(S("gelu_ready"), 1)

            lead_u(0, 0, True)
            lead_u(1, 1)
            gelu(0, 0, True)
            lead_v(0, 0, True)
            lead_u(2, 2)
            gelu(1, 1, True)
            lead_v(1, 1)
            with act.Fori(0, PKEYS // RING - 1) as i:
                for q in range(1, RING + 1):
                    lead_u((q + 2) % RING, i * RING + (q + 2))
                    gelu((q + 1) % RING, i * RING + (q + 1))
                    lead_v((q + 1) % RING, i * RING + (q + 1))
            lead_u(3, PKEYS - 1)
            for q in (2, 3):
                gelu(q, PKEYS - RING + q)
                lead_v(q, PKEYS - RING + q)
            for k in range(KT):
                act.wait_ge(S("x2_ready"), base("x2_ready") + k + 1)
                act.activation(sqx[:, k, :], Xv[:, k, :], ACT.Square).then_inc(S("sqx_ready"), 1)
            act.wait_ge(S("mem_in"), 16)
            act.activation(sqm, memn, ACT.Square).then_inc(S("sqm_ready"), 1)
            act.wait_ge(S("ssx_ready"), base("ssx_ready") + 1)
            act.activation(rsx[:, 0:T], bank[6][:, 0:T], ACT.Sqrt, scale=1.0 / D, bias=eps).then_inc(S("stdx_ready"), 1)
            act.wait_ge(S("ms_mix_ready"), 1)
            act.activation(rsx[:, T:2 * T], rsx[:, T:2 * T], ACT.Sqrt, bias=eps).then_inc(S("stdx_ready"), 1)

            out2 = {"f": lambda i: (ff[:, i, :], ACT.Sigmoid), "q": lambda i: (qq[:, i, :], ACT.Silu),
                    "i": lambda i: (vi[:, :, i * P:(i + 1) * P], ACT.Copy), "ca": lambda i: (caT[:, i, :], ACT.Copy),
                    "cg": lambda i: (sgate[:, i, :], ACT.Sigmoid), "g": lambda i: (gg[:, i, :], ACT.Silu),
                    "gc": lambda i: (gcs[:, i, :], ACT.Sigmoid), "gr": lambda i: (grs[:, i, :], ACT.Sigmoid),
                    "xk": lambda i: (xkT[:, i, :], ACT.Copy), "xv": lambda i: (xv[:, :, i * P:(i + 1) * P], ACT.Copy),
                    "xq": lambda i: (xaq[:, i, :], ACT.Copy)}

            def take2(units):
                for what, i in units:
                    second_done(act, what, i)
                    src = second_bank(what, i)[:, 0:T]
                    out, func = out2[what](i)
                    act.activation(out, three(src, TT) if what in ("i", "xv") else src, func).then_inc(S("taken2"), 1)

            act.wait_ge(S("H3_ready"), base("H3_ready") + KT)
            act.activation(h_hi, Hv, ACT.Copy).then_inc(S("h3_hi_ready"), 1)

            def lead2(m):
                n = SECOND.index(BETWEEN[m])
                pair_landed(act, PAIRS1 + PAIRS_PEER + n // 2)
                if m >= 2:
                    second_done(act, *BETWEEN[m - 2])
                act.activation(w_hi[m % 2], second_unit(n), ACT.Copy).then_inc(S("w2_hi_ready"), 1)

            take2([("f", i) for i in range(4)])
            act.wait_ge(S("lbd_ready"), 1)
            act.activation(lb, lbd, ACT.Sigmoid).then_inc(S("lb_ready"), 1)
            take2([("q", i) for i in range(4)])
            act.wait_ge(S("ssm_ready"), base("ssm_ready") + 1)
            act.activation(rsm, bank[6][:, 0:T], ACT.Sqrt, scale=1.0 / D, bias=eps).then_inc(S("stdm_ready"), 1)
            take2([("i", i) for i in range(4)])
            act.wait_ge(S("f_ready"), 1)
            act.activation(DE, ff.rearrange("p c t -> p (c t)"), ACT.Ln).then_inc(S("logf_ready"), 1)
            take2([("gr", 0), ("gr", 1)])
            lead2(0)
            for lev in range(LEVELS + 2):
                m = 3 * lev - 3
                if lev >= 1:
                    lead2(m + 1)
                if lev <= LEVELS:
                    act.wait_ge(S("dist_ready"), lev + 1)
                    act.activation(DE, DE, ACT.Exp).then_inc(S("decay_ready"), 1)
                if lev == 0:
                    take2([("gr", 2), ("gr", 3)])
                if lev >= 1:
                    take2(BETWEEN[m:m + 1])
                    lead2(m + 2)
                    take2(BETWEEN[m + 1:m + 2])
                    if m + 3 < len(BETWEEN):
                        lead2(m + 3)
                    take2(BETWEEN[m + 2:m + 3])
            act.wait_ge(S("cross_mm"), 1)
            act.activation(cross, three(bank[7][:], 4), ACT.Copy).then_inc(S("cross_ready"), 1)
            take2([("xk", 0), ("xk", 1)])
            for n in range(2):
                act.wait_ge(S("rec_ready"), n + 1)
                o_ = och[:, 2 * n:2 * n + 2, :].rearrange("p h t -> p (h t)")
                act.activation(o_, bank[6 + n][:], ACT.Copy)
                act.activation(sqh[:, 2 * n:2 * n + 2, :].rearrange("p h t -> p (h t)"), bank[6 + n][:], ACT.Square).then_inc(S("sqh_ready"), 1)
            take2([("xk", 2), ("xk", 3)])
            for n in range(2):
                act.wait_ge(S("ssh_ready"), base("ssh_ready") + n + 1)
                act.activation(rsh[:, n * 512:(n + 1) * 512], bank[4 + n][:], ACT.Sqrt, scale=1.0 / P, bias=eps).then_inc(S("stdh_ready"), 1)
            take2([("xk", i) for i in range(4, 8)])
            take2([("xv", i) for i in range(4)])
            act.wait_ge(S("conv_centred"), 1)
            act.activation(sqc, cv, ACT.Square).then_inc(S("sqc_ready"), 1)
            take2([("xv", i) for i in range(4, 6)])
            act.wait_ge(S("varc_ready"), base("varc_ready") + 1)
            act.activation(rstdc, bank[7][:, 0:T], ACT.Sqrt, scale=1.0 / CC, bias=eps).then_inc(S("stdc_ready"), 1)
            take2([("xv", i) for i in range(6, 8)])
            act.wait_ge(S("conv_normed"), 1)
            for i in range(4):
                act.activation(cv[:, i, :], cv[:, i, :], ACT.Silu, scale=v("conv_ln_g", i), bias=v("conv_ln_b", i)).then_inc(S("conv_act"), 1)
            for k in range(KT):
                act.wait_ge(S("x3_ready"), base("x3_ready") + k + 1)
                act.activation(sqn[:, k, :], Xv[:, k, :], ACT.Square).then_inc(S("sqn_ready"), 1)
            act.wait_ge(S("ssn_ready"), base("ssn_ready") + 1)
            act.activation(rsn, bank[6][:, 0:T], ACT.Sqrt, scale=1.0 / D, bias=eps).then_inc(S("stdn_ready"), 1)
            take2([("xq", i) for i in range(8)])
            for h in range(4):
                act.wait_ge(S("xmax_ready"), base("xmax_ready") + h + 1)
                for qt in range(TT):
                    c = 2 * h + qt
                    ins = act.activation(xP[:, h, qt, :], bank[4 + h % 2][:, qt * T:(qt + 1) * T], ACT.Exp, scale=1.0 / 16.0,
                                         bias=xnmx[:, c:c + 1], accum_out=xrs[:, c:c + 1])
                ins.then_inc(S("xexp_ready"), 1)
            for h in range(4):
                act.wait_ge(S("xPT_mm"), h + 1)
                act.activation(xPT[:, h, :, :].rearrange("p k q -> p (k q)"), bank[6 + h % 2][:], ACT.Copy).then_inc(S("xPT_ready"), 1)
            for k in range(KT):
                act.wait_ge(S("x4_ready"), base("x4_ready") + k + 1)
                act.activation(sq5[:, k, :], Xv[:, k, :], ACT.Square).then_inc(S("sq5_ready"), 1)
            act.wait_ge(S("ss5_mm"), base("ss5_mm") + 1)
            act.activation(rs5, bank[6][:, 0:T], ACT.Sqrt, scale=1.0 / D, bias=eps).then_inc(S("std5_ready"), 1)
            def take_rows(rows, turned, done, n, b):
                act.wait_ge(S(turned), n + 1)
                act.activation(rows[:, n // 2, (n % 2) * 512:(n % 2 + 1) * 512], bank[b][:], ACT.Copy).then_inc(S(done), 1)

            for n in range(4):
                take_rows(h_tok, "h_turned", "h_tok_ready", n, n)
            for n in range(2):
                take_rows(x_tok, "x_turned", "x_tok_ready", n, 4 + n)
            act.wait_ge(S("shifted5"), 2)
            act.activation(gex, gex, ACT.Exp)
            act.activation(e21, e21, ACT.Exp).then_inc(S("exp5_ready"), 1)
            for n in range(2, 4):
                take_rows(x_tok, "x_turned", "x_tok_ready", n, 4 + n % 2)
            act.wait_ge(S("rounds_ready"), 1)
            n = act.value_load(rounds[0:1, :], min_val=1, max_val=4)

            def silu_of(q):
                act.wait_ge(S("gate_mm"), q + 1)
                nc.scalar.activation(silu, bank[4][:], ACT.Silu).then_inc(S("silu_ready"), 1)

            def take_gathered(q):
                act.wait_ge(S("gather_mm"), q + 1)
                for b in range(2):
                    ins = nc.scalar.activation(hg[:, 4 * b:4 * b + 4, :].rearrange("p k n -> p (k n)"), bank[6 + b][:], ACT.Copy)
                ins.then_inc(S("hg_ready"), 1)

            def take_y(q):
                act.wait_ge(S("down_mm"), q + 1)
                for b in range(2):
                    ins = nc.scalar.activation(y_slot[:, 512 * b:512 * (b + 1)], bank[6 + b][:], ACT.Copy)
                ins.then_inc(S("y_slot_ready"), 1)

            with act.Fori(0, n) as r:
                take_gathered(r * 16)
                with act.Fori(0, EXPERTS // 2 - 1) as i:
                    silu_of(r * 16 + i)
                    take_gathered(r * 16 + i + 1)
                    take_y(r * 16 + i)
                silu_of(r * 16 + 15)
                take_y(r * 16 + 15)
            for tt in range(TT):
                act.wait_ge(S("x5_ready"), 2 * tt + 2)
                act.activation(y_slot, x5[:, tt, :], ACT.Square, accum_out=ss5[:, tt:tt + 1]).then_inc(S("ss5_ready"), 1)
                act.wait_ge(S("ss5_ready"), tt + 1)
                act.activation(ss5[:, tt:tt + 1], ss5[:, tt:tt + 1], ACT.Sqrt, scale=1.0 / D, bias=eps).then_inc(S("std6_ready"), 1)

        @block.tensor
        def _(pe):
            pair = [0]
            at = [0]

            def take():
                n = at[0]
                at[0] += 1
                if n % 2 == 0:
                    pair_landed(pe, n // 2)
                return unit(n)

            cs = csT.rearrange("p (k two) -> p k two", two=2)
            pe.wait_ge(S("cs_ready"), 1)
            for n in range(16):
                w = take()
                for k in range(KT):
                    last = nc.tensor.matmul(bank[n // 4][0:2, (n % 4) * P:(n % 4 + 1) * P], cs[:, k, :], w[:, k, :],
                                            start=(k == 0), stop=(k == KT - 1))
                last.then_inc(S("first_unit_done"), 1)
                if n == 9:
                    pe.wait_ge(S("const_in"), 16)
                    pe.wait_ge(S("sq1_ready"), base("sq1_ready") + 2)
                    for k in range(KT):
                        last = nc.tensor.matmul(bank[6][:], ones, sq[:, k, :], start=(k == 0), stop=(k == KT - 1))
                    last.then_inc(S("ss1_ready"), 1)
            pe.wait_ge(S("lprod_ready"), 1)
            nc.tensor.matmul(bank[5][:, 0:2], ones, lprod, start=True, stop=True).then_inc(S("lam_sums"), 1)
            for n in range(16):
                pe.wait_ge(S("mod_rows_taken"), n // 4 + 1)
                last = nc.tensor.transpose(bank[7][:, 2 * n:2 * n + 2], mod_rows4[0:2, n * P:(n + 1) * P], ident[0:2, 0:2])
            last.then_inc(S("mod1_ready"), 1)
            pe.wait_ge(S("lam_exp"), 1)
            aux = [0]

            def rope_mm(src2):
                b = 4 + aux[0] % 2
                if aux[0] >= 2:
                    pe.wait_ge(S("rope_taken"), aux[0] - 1)
                for j, s in enumerate(src2):
                    last = nc.tensor.matmul(bank[b][:, j * T:(j + 1) * T], swap, s, start=True, stop=True)
                last.then_inc(S("rope_ready"), 1)
                aux[0] += 1

            n_win = 0
            pe.wait_ge(S("h_x_ready"), base("h_x_ready") + KT)
            pe.wait_ge(S("h_ctx_ready"), KT)
            for what, i in W_IN_UNITS:
                w = take()
                b = bank[n_win % 4]
                if n_win >= 4:
                    pe.wait_ge(S("win_taken"), n_win - 3)
                if what in ("dk", "gk", "dq", "gq"):
                    a, n = (0, 2 * T) if what in ("dk", "gk") else (T, T)
                    for k in range(KT):
                        last = nc.tensor.matmul(b[:, 0:n], w[:, k, :], hAll[:, k, a:a + n], start=(k == 0), stop=(k == KT - 1))
                else:
                    for tt in range(4):
                        for k in range(KT):
                            last = nc.tensor.matmul(b[:, tt * P:(tt + 1) * P], hAll[:, k, tt * P:(tt + 1) * P], w[:, k, :],
                                                    start=(k == 0), stop=(k == KT - 1))
                last.then_inc(S("first_unit_done"), 1)
                n_win += 1
                if n_win == 7:
                    pe.wait_ge(S("win_taken"), 5)
                    for j in range(2):
                        rope_mm([dkT[:, 2 * j, T:], dkT[:, 2 * j + 1, T:]])
                    pe.wait_ge(S("sqg_ready"), base("sqg_ready") + 1)
                    nc.tensor.matmul(bank[6][:], halves, sq[:, 0, :], start=True, stop=True).then_inc(S("ssg_ready"), 1)
                if n_win == 11:
                    pe.wait_ge(S("win_taken"), 9)
                    for j in range(2):
                        rope_mm([dqT[:, 2 * j, :], dqT[:, 2 * j + 1, :]])
                if n_win in (14, 15):
                    g = n_win - 14
                    pe.wait_ge(S("sqg_ready"), base("sqg_ready") + 3 + 2 * g)
                    pe.wait_ge(S("stdg_ready"), base("stdg_ready") + 1 + g)
                    nc.tensor.matmul(bank[6][:], halves, sq[:, 2 + g, :], start=True, stop=True).then_inc(S("ssg_ready"), 1)
                if n_win == 16:
                    pe.wait_ge(S("gk_normed"), 1)
                    rope_mm([gkT[:, T:]])
            for j in range(2):
                pe.wait_ge(S("gq_normed"), j + 1)
                rope_mm([gqT[:, 2 * j, :], gqT[:, 2 * j + 1, :]])

            def scores(i):
                t_, qt = (i % 8) // 2, i % 2
                q = dqT if i < 8 else gqT
                if i == 0:
                    pe.wait_ge(S("rope_done"), 4)
                    pe.wait_ge(S("win_taken"), 18)
                if i == 8:
                    pe.wait_ge(S("rope_done"), 7)
                for r in range(2):
                    k = dkT[:, t_, :] if i < 8 else gkT
                    if i >= 2:
                        pe.wait_ge(S("exp_ready"), base("exp_ready") + 2 * (i - 2) + r + 1)
                    a = HD * r
                    nc.tensor.matmul(bank[2 * (i % 2) + r][:], q[a:a + HD, t_, qt * P:(qt + 1) * P], k[a:a + HD, :],
                                     start=True, stop=True).then_inc(S("scores_ready"), 1)

            def transposes(i):
                pe.wait_ge(S("P_ready"), base("P_ready") + i + 1)
                if i >= 2:
                    pe.wait_ge(S("PT_taken"), i - 1 if i < 8 else i)
                for r in range(1 if i < 8 else 2):
                    for k in range(4):
                        last = nc.tensor.transpose(bank[PT_bank(i, r)][:, k * P:(k + 1) * P], Pb[:, i % 3, r, k * P:(k + 1) * P], ident)
                last.then_inc(S("PT_ready"), 1)

            def pv(i):
                t_ = (i % 8) // 2
                pe.wait_ge(S("PT_taken"), i + 1)
                if i >= 2:
                    pe.wait_ge(S("o_taken"), i - 1)
                o = bank[6 + i % 2]
                for k in range(4):
                    if i < 8:
                        last = nc.tensor.matmul(o[:, 0:P], dvs[:, k, t_ * P:(t_ + 1) * P], PTb[:, i % 2, 0, k, :], start=(k == 0), stop=(k == 3))
                if i >= 8:
                    for r in range(2):
                        for k in range(4):
                            last = nc.tensor.matmul(o[HD * r:HD * (r + 1), 0:P], gvs[:, k, HD * r:HD * (r + 1)], PTb[:, i % 2, r, k, :],
                                                    start=(k == 0), stop=(k == 3))
                last.then_inc(S("pv_ready"), 1)

            for i in range(19):
                if i < 16:
                    scores(i)
                if 2 <= i < 18:
                    transposes(i - 2)
                if i == 17:
                    pe.wait_ge(S("exp_ready"), base("exp_ready") + 30)
                    for n in range(2):
                        pe.wait_ge(S("sqo_ready"), base("sqo_ready") + n + 1)
                        nc.tensor.matmul(bank[n][:], ones, sq[:, n, :], start=True, stop=True).then_inc(S("sso_ready"), 1)
                if i == 18:
                    pe.wait_ge(S("mod_pair_done"), 16)
                    pe.wait_ge(S("exp_ready"), base("exp_ready") + 32)
                    for n in range(32):
                        last = nc.tensor.matmul(bank[3][:, n:n + 1], mod_acc[:, n, :], ones[:, 0:1], start=True, stop=True)
                    last.then_inc(S("mod2_ready"), 1)
                if i >= 3:
                    pv(i - 3)
            pe.wait_ge(S("o_taken"), 16)
            pe.wait_ge(S("od_normed"), 2)
            for n in range(8):
                w = take()
                b = bank[2 + n % 4]
                if n == 1:
                    pe.wait_ge(S("mod_taken"), 1)
                if n >= 4:
                    pe.wait_ge(S("x1_ready"), base("x1_ready") + n - 3)
                for k in range(KT):
                    last = nc.tensor.matmul(b[:, 0:T], w[:, k, :], oT[:, k, :], start=(k == 0), stop=(k == KT - 1))
                last.then_inc(S("first_unit_done"), 1)
            for k in range(KT):
                pe.wait_ge(S("sq2_ready"), base("sq2_ready") + k + 1)
                last = nc.tensor.matmul(bank[6][:, 0:T], ones, sq[:, k, 0:T], start=(k == 0), stop=(k == KT - 1))
            last.then_inc(S("ss2_ready"), 1)
            pe.wait_ge(S("subkeys_in"), 16)
            subkeys = three(work[:, 0:2048], 16)

            def key_scores(n):
                pe.wait_ge(S("qh_ready"), n + 1)
                if n >= 2:
                    pe.wait_ge(S("sc_ready"), n - 1)
                for tt in range(TT):
                    last = nc.tensor.matmul(bank[2 + n % 2][:, tt * P:(tt + 1) * P], qh[:, n % 2, tt * P:(tt + 1) * P],
                                            subkeys[:, n, :], start=True, stop=True)
                last.then_inc(S("keys_scored"), 1)

            for n in range(16):
                w = take()
                if n >= 2:
                    pe.wait_ge(S("qh_ready"), n - 1)
                for k in range(KT):
                    if n == 0:
                        pe.wait_ge(S("h2_ready"), k + 1)
                    last = nc.tensor.matmul(bank[n % 2][:, 0:T], w[:, k, :], Hv[:, k, :], start=(k == 0), stop=(k == KT - 1))
                last.then_inc(S("first_unit_done"), 1)
                if n >= 1:
                    key_scores(n - 1)
            key_scores(15)
            pe.wait_ge(S("ids_ready"), 1)
            for tt in range(TT):
                for i, a in enumerate((gate[:, tt, :, :].rearrange("p h n -> p (h n)"), ids[:, 0, tt, :], ids[:, 1, tt, :])):
                    last = nc.tensor.transpose(bank[4 + tt][:, i * P:(i + 1) * P], a, ident)
                last.then_inc(S("GIJ_turned"), 1)
            pe.wait_ge(S("zeros_ready"), 1)
            for b in range(4):
                nc.tensor.matmul(bank[b][:], zeros[:, 0:P], zeros, start=True, stop=False, skip_group_check=True)
            pe.wait_ge(S("GIJ_ready"), 2)
            pe.sem_inc(S("gates_mm"), 8)
            with pe.Fori(0, T // 16) as i:
                g = i * 4
                for q in range(16):
                    if q % 4 == 0:
                        pe.wait_ge(S("gates_taken"), g + (q // 4 + 1))
                    pe.wait_ge(S("left_ready"), g * 4 + (q + 1))
                    if q % 4 == 0:
                        pe.wait_ge(S("right_ready"), g + (q // 4 + 1))
                    if q % 8 in POOL_TOKENS:
                        pe.wait_ge(S("pool_rows_ready"), i * 6 + (q // 8 * 3 + POOL_TOKENS.index(q % 8) + 4))
                    nc.tensor.matmul(bank[4 + q // 4][:, (q % 4) * P:(q % 4 + 1) * P], left[:, q % 8, :], right[:, q % 8, :],
                                     start=True, stop=True).then_inc(S("gates_mm"), 1)

            def ux(q, j, first=False):
                pe.wait_ge(S("u_hi_ready"), j + 1)
                if not first:
                    pe.wait_ge(S("gelu_ready"), j - 1)
                hi, lo, out = three(u_hi, KT), three(peer_unit(q, 0, ring_parts), KT), bank[4 + q % 2][:, 0:T]
                for k in range(KT):
                    nc.tensor.matmul(out, hi[:, k, :], x_hi[:, k, :], start=(k == 0), stop=False)
                    nc.tensor.matmul(out, hi[:, k, :], x_lo[:, k, :], start=False, stop=False)
                pe.wait_ge(S("u_lo_ready"), j + 1)
                for k in range(KT):
                    last = nc.tensor.matmul(out, lo[:, k, :], x_hi[:, k, :], start=False, stop=(k == KT - 1))
                last.then_inc(S("ux_ready"), 1)

            def wv(q, j, stop=False):
                pe.wait_ge(S("v_hi_ready"), j + 1)
                pe.wait_ge(S("wgt_ready"), j + 1)
                lo = peer_unit(q, 1, ring_parts)
                for b_ in ((v_hi, wgt_hi), (v_hi, wgt_lo), (lo, wgt_hi)):
                    if b_[0] is lo:
                        pe.wait_ge(S("v_lo_ready"), j + 1)
                    for k in range(KT):
                        last = nc.tensor.matmul(bank[k // 2][:, (k % 2) * T:(k % 2 + 1) * T], b_[0][:, k * P:(k + 1) * P],
                                                b_[1][:, q % 2, :], start=False, stop=stop and b_[0] is lo, skip_group_check=True)
                last.then_inc(S("peer_pair_done"), 1)

            pe.wait_ge(S("x_lo_ready"), 1)
            ux(0, 0, True)
            ux(1, 1, True)
            wv(0, 0)
            with pe.Fori(0, PKEYS // RING - 1) as i:
                for q in range(RING):
                    ux((q + 2) % RING, i * RING + (q + 2))
                    wv((q + 1) % RING, i * RING + (q + 1))
            for q in (2, 3):
                ux(q, PKEYS - RING + q)
                wv(q - 1, PKEYS - RING + q - 1)
            wv(3, PKEYS - 1, True)
            pe.wait_ge(S("fg2_ready"), 1)
            for k in range(KT):
                pe.wait_ge(S("sqx_ready"), base("sqx_ready") + k + 1)
                nc.tensor.matmul(bank[6][:, 0:T], ones, sqx[:, k, :], start=(k == 0), stop=(k == KT - 1))
                last = nc.tensor.matmul(bank[7][:, 0:T], fg2[:, k, :], sqx[:, k, :], start=(k == 0), stop=(k == KT - 1))
            last.then_inc(S("ssx_ready"), 1)
            at2 = [0]

            def take2(what, i):
                n = at2[0]
                assert SECOND[n] == (what, i)
                at2[0] += 1
                if n % 2 == 0:
                    pair_landed(pe, PAIRS1 + PAIRS_PEER + n // 2)
                if n >= 4:
                    prior = SECOND[n - 4]
                    if prior in SECOND_ACT:
                        pe.wait_ge(S("taken2"), SECOND_ACT.index(prior) + 1)
                    elif prior[0] in ("co", "ho"):
                        pe.wait_ge(S("merge_taken"), prior[1] + (1 if prior[0] == "ho" else 5))
                    elif prior[0] == "mix":
                        pe.wait_ge(S("x3_ready"), base("x3_ready") + prior[1] + 1)
                    else:
                        pe.wait_ge(S("x4_ready"), base("x4_ready") + prior[1] + 1)
                return second_unit(n)

            def project_parts(ms):
                for m in ms:
                    take2(*BETWEEN[m])
                    hi, out = three(w_hi[m % 2], KT), second_bank(*BETWEEN[m])[:, 0:T]
                    lo = three(second_unit(SECOND.index(BETWEEN[m]), ring_parts), KT)
                    pe.wait_ge(S("w2_hi_ready"), m + 1)
                    for k in range(KT):
                        nc.tensor.matmul(out, hi[:, k, :], h_hi[:, k, :], start=(k == 0), stop=False)
                        nc.tensor.matmul(out, hi[:, k, :], h_lo[:, k, :], start=False, stop=False)
                    pe.wait_ge(S("w2_lo_ready"), m + 1)
                    for k in range(KT):
                        last = nc.tensor.matmul(out, lo[:, k, :], h_hi[:, k, :], start=False, stop=(k == KT - 1))
                    last.then_inc(S("second_unit_done"), 1)

            def project(units, rhs, ready=None):
                for what, i in units:
                    w, b = three(take2(what, i), KT), second_bank(what, i)
                    if what in ("i", "xv"):
                        for tt in range(TT):
                            for k in range(KT):
                                last = nc.tensor.matmul(b[:, tt * P:(tt + 1) * P], rhs[:, k, tt * P:(tt + 1) * P], w[:, k, :],
                                                        start=(k == 0), stop=(k == KT - 1))
                    else:
                        for k in range(KT):
                            if ready and (what, i) == units[0]:
                                pe.wait_ge(S(ready), base(ready) + k + 1)
                            last = nc.tensor.matmul(b[:, 0:T], w[:, k, :], rhs[:, k, :], start=(k == 0), stop=(k == KT - 1))
                    last.then_inc(S("second_unit_done"), 1)

            project([("f", i) for i in range(4)], Hv, "H3_ready")
            pe.wait_ge(S("stdx_ready"), base("stdx_ready") + 2)
            pe.wait_ge(S("sqm_ready"), base("sqm_ready") + 1)
            for k in range(KT):
                last = nc.tensor.matmul(bank[6][:, 0:T], ones, sqm[:, k, :], start=(k == 0), stop=(k == KT - 1))
            last.then_inc(S("ssm_ready"), 1)
            project([(w, i) for w in ("q", "i") for i in range(4)], Hv)
            project([("gr", i) for i in range(4)], Hv)
            qe, ke = (x.rearrange("p (h t n) -> p h t n", h=4, t=TT) for x in (QE, KE))
            for lev in range(LEVELS + 2):
                if lev <= LEVELS:
                    pe.wait_ge(S("qke_ready"), lev + 1)
                if lev == LEVELS:
                    for h in range(4):
                        last = nc.tensor.matmul(bank[7][:, h * P:(h + 1) * P], ke[:, h, 0, :], qe[:, h, 1, :], start=True, stop=True)
                    last.then_inc(S("cross_mm"), 1)
                else:
                    n_level = min(lev, LEVELS)
                    if n_level >= 1:
                        pe.wait_ge(S("level_taken"), n_level)
                    for h in range(4):
                        for tt in range(TT):
                            i = 2 * h + tt
                            a, b = (ke[:, h, tt, :], qe[:, h, tt, :]) if lev < LEVELS else \
                                (kk[:, h, tt * P:(tt + 1) * P], qq[:, h, tt * P:(tt + 1) * P])
                            last = nc.tensor.matmul(bank[4 + i // 4][:, (i % 4) * P:(i % 4 + 1) * P], a, b, start=True, stop=True)
                    last.then_inc(S("level_mm"), 1)
                if lev == 0:
                    pe.wait_ge(S("h3_lo_ready"), 1)
                if lev <= LEVELS:
                    project_parts(range(3 * lev, 3 * lev + 3))
            pe.wait_ge(S("memn_ready"), 1)
            project([("xk", 0), ("xk", 1)], memn)
            pe.wait_ge(S("cross_ready"), 1)
            pe.wait_ge(S("level_taken"), LEVELS + 1)
            for h in range(4):
                o_ = bank[6 + h // 2][:, (h % 2) * T:(h % 2 + 1) * T]
                v0, v1 = vi[:, 0, h * P:(h + 1) * P], vi[:, 1, h * P:(h + 1) * P]
                nc.tensor.matmul(o_[:, 0:P], v0, scT[:, h, 0, :], start=True, stop=True)
                nc.tensor.matmul(o_[:, P:T], v0, cross[:, h, :], start=True, stop=False)
                last = nc.tensor.matmul(o_[:, P:T], v1, scT[:, h, 1, :], start=False, stop=True)
                if h % 2 == 1:
                    last.then_inc(S("rec_ready"), 1)
            project([("xk", 2), ("xk", 3)], memn)
            for n in range(2):
                pe.wait_ge(S("sqh_ready"), base("sqh_ready") + n + 1)
                nc.tensor.matmul(bank[4 + n][:], ones, sqh[:, 2 * n:2 * n + 2, :].rearrange("p h t -> p (h t)"),
                                 start=True, stop=True).then_inc(S("ssh_ready"), 1)
            project([("xk", i) for i in range(4, 8)], memn)
            project([("xv", i) for i in range(4)], memn)
            pe.wait_ge(S("conv_ready"), 1)
            for i in range(4):
                last = nc.tensor.matmul(bank[6][:, 0:T], ones, cv[:, i, :], start=(i == 0), stop=(i == 3))
            last.then_inc(S("meanc_ready"), 1)
            project([("xv", i) for i in range(4, 6)], memn)
            pe.wait_ge(S("sqc_ready"), base("sqc_ready") + 1)
            for i in range(4):
                last = nc.tensor.matmul(bank[7][:, 0:T], ones, sqc[:, i, :], start=(i == 0), stop=(i == 3))
            last.then_inc(S("varc_ready"), 1)
            project([("xv", i) for i in range(6, 8)], memn)
            for what, rhs in (("ho", och), ("co", cv)):
                for i in range(4):
                    pe.wait_ge(S("conv_act" if what == "co" else "och_normed"), 4)
                    w, b = three(take2(what, i), 4), second_bank(what, i)
                    for n in range(2):
                        for k in range(4):
                            last = nc.tensor.matmul(b[:, n * T:(n + 1) * T], w[:, k, n * P:(n + 1) * P], rhs[:, k, :],
                                                    start=(k == 0), stop=(k == 3))
                    last.then_inc(S("second_unit_done"), 1)
            pe.wait_ge(S("merged"), 4)
            project([("mix", i) for i in range(8)], gcs)
            for k in range(KT):
                pe.wait_ge(S("sqn_ready"), base("sqn_ready") + k + 1)
                last = nc.tensor.matmul(bank[6][:, 0:T], ones, sqn[:, k, :], start=(k == 0), stop=(k == KT - 1))
            last.then_inc(S("ssn_ready"), 1)
            project([("xq", i) for i in range(8)], Hv, "H4_ready")
            pe.wait_ge(S("taken2"), len(SECOND_ACT))
            for h in range(4):
                if h >= 2:
                    pe.wait_ge(S("xexp_ready"), base("xexp_ready") + h - 1)
                for qt in range(TT):
                    for k in range(2):
                        last = nc.tensor.matmul(bank[4 + h % 2][:, qt * T:(qt + 1) * T], xaq[:, 2 * h + k, qt * P:(qt + 1) * P],
                                                xkT[:, 2 * h + k, :], start=(k == 0), stop=(k == 1))
                last.then_inc(S("xscores_ready"), 1)
            for h in range(4):
                pe.wait_ge(S("xP_ready"), base("xP_ready") + h + 1)
                if h >= 2:
                    pe.wait_ge(S("xPT_ready"), h - 1)
                for kt in range(TT):
                    for qt in range(TT):
                        last = nc.tensor.transpose(bank[6 + h % 2][:, (2 * kt + qt) * P:(2 * kt + qt + 1) * P],
                                                   xP[:, h, qt, kt * P:(kt + 1) * P], ident)
                last.then_inc(S("xPT_mm"), 1)
            for h in range(4):
                pe.wait_ge(S("xPT_ready"), h + 1)
                if h >= 2:
                    pe.wait_ge(S("xo_taken"), h - 1)
                for d in range(2):
                    for kt in range(TT):
                        last = nc.tensor.matmul(bank[4 + h % 2][:, d * T:(d + 1) * T], xv[:, kt, (2 * h + d) * P:(2 * h + d + 1) * P],
                                                xPT[:, h, kt, :], start=(kt == 0), stop=(kt == 1))
                last.then_inc(S("xpv_ready"), 1)
            pe.wait_ge(S("xo_taken"), 4)
            project([("xo", i) for i in range(8)], xo)
            for k in range(KT):
                pe.wait_ge(S("sq5_ready"), base("sq5_ready") + k + 1)
                last = nc.tensor.matmul(bank[6][:, 0:T], ones, sq5[:, k, :], start=(k == 0), stop=(k == KT - 1))
            last.then_inc(S("ss5_mm"), 1)
            pe.wait_ge(S("x4_ready"), base("x4_ready") + 8)
            pe.wait_ge(S("H5_ready"), base("H5_ready") + KT)
            pe.wait_ge(S("router_in"), 32)
            for tt in range(TT):
                for k in range(KT):
                    last = nc.tensor.matmul(bank[7][:, 36 * tt:36 * tt + 36], Hv[:, k, tt * P:(tt + 1) * P], r_w[:, k, :],
                                            start=(k == 0), stop=(k == KT - 1))
            last.then_inc(S("logits_mm"), 1)
            for src, ready in ((Hv, "h_turned"), (Xv, "x_turned")):
                for n in range(4):
                    b = n if src is Hv else 4 + n % 2
                    if src is Xv and n >= 2:
                        pe.wait_ge(S("x_tok_ready"), n - 1)
                    for j in range(4):
                        k = 4 * (n % 2) + j
                        last = nc.tensor.transpose(bank[b][:, j * P:(j + 1) * P], src[:, k, (n // 2) * P:(n // 2 + 1) * P], ident)
                    last.then_inc(S(ready), 1)
            pe.wait_ge(S("chosen_ready"), 1)
            before = cst("before")
            nc.tensor.matmul(bank[6][:, 0:32], before, chosen[:, 0, :], start=True, stop=True)
            nc.tensor.matmul(bank[6][:, 32:64], ones, chosen[:, 0, :], start=True, stop=False)
            nc.tensor.matmul(bank[6][:, 32:64], before, chosen[:, 1, :], start=False, stop=True)
            nc.tensor.matmul(bank[6][:, 64:96], ones, chosen[:, 0, :], start=True, stop=False)
            nc.tensor.matmul(bank[6][:, 64:96], ones, chosen[:, 1, :], start=False, stop=True).then_inc(S("places_mm"), 1)
            pe.wait_ge(S("h_tok_ready"), 4)
            pe.wait_ge(S("x_tok_ready"), 4)
            pe.wait_ge(S("zeros5_ready"), 1)
            for b in range(4):
                nc.tensor.matmul(bank[b][:], zeros[:, 0:P], zeros, start=True, stop=False, skip_group_check=True)
            pe.wait_ge(S("rounds_ready"), 1)
            n = pe.value_load(rounds[0:1, :], min_val=1, max_val=4)

            def gather(q):
                pe.wait_ge(S("sel_ready"), q + 1)
                for k in range(KT):
                    for tt in range(TT):
                        last = nc.tensor.matmul(bank[6 + k // 4][:, (k % 4) * P:(k % 4 + 1) * P], h_tok[:, tt, k * P:(k + 1) * P],
                                                sel[:, tt, :], start=(tt == 0), stop=(tt == TT - 1))
                last.then_inc(S("gather_mm"), 1)

            def both(out, slots, weights, k, n):
                for a in range(2):
                    c = slice(a * CAP, (a + 1) * CAP)
                    last = nc.tensor.matmul(out[c, :], slots[:, c], weights[a], start=(k == 0), stop=(k == n - 1))
                return last

            def gate_up(q, half, parity):
                pe.wait_ge(S("hg_ready"), q + 1)
                for w, b, loaded, count, done in ((w_gate[parity], 4, f"gates_in{parity}", half, "gate_mm"), (w_up, 5, "ups_in", q, "up_mm")):
                    pe.wait_ge(S(loaded), count * 32 + 32)
                    for k in range(KT):
                        last = both(bank[b], hg[:, k, :], [x[:, k, :] for x in w], k, KT)
                    last.then_inc(S(done), 1)

            def scatter(q, stop=False):
                pe.wait_ge(S("y_slot_ready"), q + 1)
                for tt in range(TT):
                    for b in range(2):
                        last = nc.tensor.matmul(bank[2 * tt + b][:], selwT[:, tt * P:(tt + 1) * P], y_slot[:, 512 * b:512 * (b + 1)],
                                                start=False, stop=stop, skip_group_check=True)
                return last

            def turn(q):
                pe.wait_ge(S("hid_ready"), q + 1)
                for k in range(4):
                    last = nc.tensor.transpose(bank[4][:, k * P:(k + 1) * P], hid[:, k * P:(k + 1) * P], ident)
                last.then_inc(S("turn_mm"), 1)
                pe.wait_ge(S("selw_ready"), q + 1)
                for tt in range(TT):
                    last = nc.tensor.transpose(bank[5][:, tt * P:(tt + 1) * P], selw[:, tt, :], ident)
                last.then_inc(S("selT_mm"), 1)

            def down(q):
                pe.wait_ge(S("hidT_ready"), q + 1)
                pe.wait_ge(S("downs_in"), q * 32 + 32)
                for k in range(4):
                    for b in range(2):
                        last = both(bank[6 + b], hidT[:, k, :], [w[:, k, 512 * b:512 * (b + 1)] for w in w_down], k, 4)
                last.then_inc(S("down_mm"), 1)

            with pe.Fori(0, n) as r:
                q0 = r * 16
                gather(q0)
                gate_up(q0, r * 8, 0)
                gather(q0 + 1)
                turn(q0)
                pe.wait_ge(S("hg_ready"), q0 + 2)
                down(q0)
                with pe.Fori(0, EXPERTS // 4 - 1) as i:
                    for odd in (1, 0):
                        q = q0 + i * 2 + (2 - odd)
                        pe.wait_ge(S("selwT_ready"), q)
                        gate_up(q, r * 8 + i + (1 - odd), odd)
                        scatter(q - 1)
                        gather(q + 1)
                        turn(q)
                        pe.wait_ge(S("hg_ready"), q + 2)
                        down(q)
                pe.wait_ge(S("selwT_ready"), q0 + 15)
                gate_up(q0 + 15, r * 8 + 7, 1)
                scatter(q0 + 14)
                turn(q0 + 15)
                down(q0 + 15)
                pe.wait_ge(S("selwT_ready"), q0 + 16)
                scatter(q0 + 15, True).then_inc(S("round_done"), 1)


        @block.vector
        def _(dve):
            chain = [0]

            def link(ins):
                chain[0] += 1
                ins.then_inc(S("dve_own"), 1)
                dve.wait_ge(S("dve_own"), chain[0])

            dve.memset(eps, EPS).then_inc(S("eps_ready"), 1)
            dve.wait_ge(S("vec_in"), 16)
            dve.tensor_tensor(lprod, v("lam_q", 0, 2), v("lam_k", 0, 2), ALU.mult).then_inc(S("lprod_ready"), 1)
            dve.wait_ge(S("std1_ready"), base("std1_ready") + 1)
            link(dve.reciprocal(rs1, rs1))
            dve.wait_ge(S("ctx_in"), 16)
            for k in range(KT):
                dve.tensor_tensor(hAll[:, k, 0:T], ctxT[:, k, :], rs1[:, 0:T], ALU.mult).then_inc(S("normed1"), 1)
            dve.wait_ge(S("x_in"), 16)
            link(dve.tensor_tensor(hAll[:, :, T:2 * T], Xv, wide(rs1[:, T:2 * T], KT), ALU.mult))
            dve.wait_ge(S("mod1_ready"), 1)
            link(dve.tensor_tensor(mod3[:, 0:16, :], three(bank[7][:, 0:32], 16), each(v("b_mod", 0, 16), 2), ALU.add))
            link(dve.tensor_scalar(gs_x, mod3[:, 8:16, 0], 1.0, None, ALU.add))
            link(dve.tensor_scalar(gs_c, mod3[:, 8:16, 1], 1.0, None, ALU.add))
            dve.tensor_tensor(gs_x, gs_x, v("norm1_g", 0, 8), ALU.mult)
            dve.tensor_tensor(gs_c, gs_c, v("norm1_g", 0, 8), ALU.mult).then_inc(S("gs1_ready"), 1)
            dve.wait_ge(S("gs1_ready"), 1)
            for k in range(KT):
                dve.tensor_scalar(hAll[:, k, T:2 * T], hAll[:, k, T:2 * T], gs_x[:, k:k + 1], mod3[:, k, 0:1],
                                  ALU.mult, ALU.add).then_inc(S("h_x_ready"), 1)
            dve.wait_ge(S("lam_exp"), 1)
            link(dve.tensor_tensor(lam, lam_e[:, 0:1], lam_e[:, 1:2], ALU.subtract))
            link(dve.tensor_scalar(lam, lam, LAMBDA_INIT, -1.0, ALU.add, ALU.mult))
            dve.tensor_scalar(gain_dv, v("subln_g"), 1.0 - LAMBDA_INIT, None, ALU.mult)

            cs = csT.rearrange("p (k two) -> p k two", two=2)
            nmod = [0]

            def mod_pair():
                m = nmod[0]
                nmod[0] += 1
                dve.wait_ge(S(f"mod_in{m % 2}"), 16 * (m // 2 + 1))
                w = mod_in[m % 2].rearrange("p (u k n) -> p u k n", u=2, k=KT)
                acc = mod_acc[:, 2 * m:2 * m + 2, :]
                link(dve.tensor_scalar(acc, w[:, :, 0, :], cs[:, 0, 0:1], None, ALU.mult))
                for k in range(1, KT):
                    ins = dve.scalar_tensor_tensor(acc, w[:, :, k, :], cs[:, k, 0:1], acc, ALU.mult, ALU.add)
                    if k < KT - 1:
                        link(ins)
                ins.then_inc(S("mod_pair_done"), 1)

            nrope = [0]

            def rope(x, n):
                i = nrope[0]
                nrope[0] += 1
                b = three(bank[4 + i % 2][:, 0:n * T], n)
                dve.wait_ge(S("rope_ready"), i + 1)
                link(dve.tensor_tensor(rt[:, 0, 0:n, :], x, wide(cst("cos"), n), ALU.mult))
                ins = dve.tensor_tensor(rt[:, 1, 0:n, :], b, wide(cst("sin"), n), ALU.mult)
                ins.then_inc(S("rope_taken"), 1)
                dve.wait_ge(S("rope_taken"), i + 1)
                dve.tensor_tensor(x, rt[:, 0, 0:n, :], rt[:, 1, 0:n, :], ALU.add).then_inc(S("rope_done"), 1)
                dve.wait_ge(S("rope_done"), i + 1)

            for _ in range(9):
                mod_pair()
            dve.wait_ge(S("win_taken"), 5)
            for j in range(2):
                rope(dkT[:, 2 * j:2 * j + 2, T:2 * T], 2)
            mod_pair()
            dve.wait_ge(S("stdg_ready"), base("stdg_ready") + 1)
            link(dve.reciprocal(rsk, rsk))
            dve.scalar_tensor_tensor(gkT, gkT, v("gk_g"), rsk, ALU.mult, ALU.mult).then_inc(S("gk_normed"), 1)
            for _ in range(2):
                mod_pair()
            for j in range(2):
                rope(dqT[:, 2 * j:2 * j + 2, :], 2)
            for _ in range(3):
                mod_pair()
            for j in range(2):
                dve.wait_ge(S("stdg_ready"), base("stdg_ready") + 2 + j)
                link(dve.reciprocal(rsg[:, j * 512:(j + 1) * 512], rsg[:, j * 512:(j + 1) * 512]))
                dve.scalar_tensor_tensor(gqT[:, 2 * j:2 * j + 2, :], gqT[:, 2 * j:2 * j + 2, :], v("gq_g"),
                                         three(rsg[:, j * 512:(j + 1) * 512], 2), ALU.mult, ALU.mult).then_inc(S("gq_normed"), 1)
            mod_pair()
            dve.wait_ge(S("gk_normed"), 1)
            rope(gkT[:, T:].unsqueeze(1), 1)
            dve.wait_ge(S("gq_normed"), 2)
            for j in range(2):
                rope(gqT[:, 2 * j:2 * j + 2, :], 2)

            while nmod[0] < 16:
                mod_pair()

            def maxima(i):
                for r in range(2):
                    c = 2 * (i % 3) + r
                    dve.wait_ge(S("scores_ready"), base("scores_ready") + 2 * i + r + 1)
                    link(dve.reduce_max(mx[:, c:c + 1], bank[2 * (i % 2) + r][:], AX))
                    dve.tensor_scalar(nmx[:, c:c + 1], mx[:, c:c + 1], -HD ** -0.5, None, ALU.mult).then_inc(S("nmax_ready"), 1)

            def normalise(i):
                c = 2 * (i % 3)
                dve.wait_ge(S("exp_ready"), base("exp_ready") + 2 * i + 2)
                link(dve.reciprocal(rinv[:, c:c + 2], rsum[:, c:c + 2]))
                a, b = Pb[:, i % 3, 0, :], Pb[:, i % 3, 1, :]
                if i < 8:
                    dve.tensor_scalar(b, b, rinv[:, c + 1:c + 2], lam, ALU.mult, ALU.mult).then_inc(S("P2_scaled"), 1)
                    dve.wait_ge(S("P2_scaled"), i + 1)
                    dve.scalar_tensor_tensor(a, a, rinv[:, c:c + 1], b, ALU.mult, ALU.add).then_inc(S("P_ready"), 1)
                else:
                    dve.tensor_scalar(a, a, rinv[:, c:c + 1], None, ALU.mult)
                    dve.tensor_scalar(b, b, rinv[:, c + 1:c + 2], None, ALU.mult).then_inc(S("P_ready"), 1)

            def take_o(i):
                dve.wait_ge(S("pv_ready"), base("pv_ready") + i + 1)
                tile = (i % 8) // 2 + (0 if i < 8 else 4)
                dve.tensor_copy(oT[:, tile, (i % 2) * P:(i % 2 + 1) * P], bank[6 + i % 2][:, 0:P]).then_inc(S("o_taken"), 1)

            for i in range(20):
                if i < 16:
                    maxima(i)
                if 1 <= i < 17:
                    normalise(i - 1)
                if i == 18:
                    for n in range(2):
                        dve.wait_ge(S("stdo_ready"), base("stdo_ready") + n + 1)
                        r = rsg[:, n * 512:(n + 1) * 512]
                        link(dve.reciprocal(r, r))
                        dve.scalar_tensor_tensor(oT[:, 2 * n:2 * n + 2, :], oT[:, 2 * n:2 * n + 2, :], gain_dv, three(r, 2),
                                                 ALU.mult, ALU.mult).then_inc(S("od_normed"), 1)
                if i == 19:
                    dve.wait_ge(S("mod2_ready"), 1)
                    link(dve.tensor_tensor(mod3[:, 16:48, 0], bank[3][:, 0:32], v("b_mod", 16, 32), ALU.add))
                    link(dve.tensor_scalar(gs2, mod3[:, 32:40, 0], 1.0, None, ALU.add))
                    dve.tensor_tensor(gs2, gs2, v("norm2_g", 0, 8), ALU.mult).then_inc(S("mod_taken"), 1)
                if i >= 4:
                    take_o(i - 4)
            for n in range(8):
                first_done(dve, "out", n)
                dve.scalar_tensor_tensor(Xv[:, n, :], bank[2 + n % 4][:, 0:T], mod3[:, 16 + n, 0:1], Xv[:, n, :],
                                         ALU.mult, ALU.add).then_inc(S("x1_ready"), 1)
            dve.wait_ge(S("std2_ready"), base("std2_ready") + 1)
            dve.wait_ge(S("mod_taken"), 1)
            dve.wait_ge(S("x1_ready"), base("x1_ready") + 8)
            link(dve.reciprocal(rs1[:, 0:T], rs1[:, 0:T]))
            for k in range(KT):
                dve.scalar_tensor_tensor(Hv[:, k, :], Xv[:, k, :], gs2[:, k:k + 1], rs1[:, 0:T], ALU.mult, ALU.mult).then_inc(S("h2_scaled"), 1)
            dve.memset(zeros, 0.0).then_inc(S("zeros_ready"), 1)

            def top16(values, spare, out_v, out_i):
                for tt in range(TT):
                    ins = dve.max(out_v[tt][:, 0:8], values[tt])
                link(ins)
                for tt in range(TT):
                    dve.max_index(out_i[tt][:, 0:8], out_v[tt][:, 0:8], values[tt])
                for tt in range(TT):
                    ins = dve.match_replace(spare[tt], out_v[tt][:, 0:8], values[tt], -3.0e38)
                link(ins)
                for tt in range(TT):
                    ins = dve.max(out_v[tt][:, 8:16], spare[tt])
                link(ins)
                for tt in range(TT):
                    ins = dve.max_index(out_i[tt][:, 8:16], out_v[tt][:, 8:16], spare[tt])
                return ins

            for n in range(16):
                dve.wait_ge(S("sc_ready"), n + 1)
                top16([sc[:, n % 2, tt, :] for tt in range(TT)], [sc2[:, n % 2, tt, :] for tt in range(TT)],
                      [sv[:, tt, n, :] for tt in range(TT)], [si[:, tt, n, :] for tt in range(TT)]).then_inc(S("sc_used"), 1)
                if n % 2 == 0:
                    continue
                h = n // 2
                dve.wait_ge(S("sc_used"), n + 1)
                for tt in range(TT):
                    ins = dve.tensor_tensor(three(cand[:, h % 2, tt, :], PTOP), each(sv[:, tt, n - 1, :], PTOP),
                                            wide(sv[:, tt, n, :], PTOP), ALU.add)
                link(ins)
                link(top16([cand[:, h % 2, tt, :] for tt in range(TT)], [cand2[:, h % 2, tt, :] for tt in range(TT)],
                           [best[:, tt, h, :] for tt in range(TT)], [pos[:, tt, h, :] for tt in range(TT)]))
            dve.tensor_tensor(gate, best, best[:, :, :, 0:1].broadcast_to([P, TT, PH, PTOP]), ALU.subtract).then_inc(S("best_shifted"), 1)
            posf = pos.rearrange("p t h n -> p t (h n)")
            dve.tensor_scalar(digit_u[:, 0, :, :], posf, 4, None, ALU.logical_shift_right)
            link(dve.tensor_scalar(digit_u[:, 1, :, :], posf, 15, None, ALU.bitwise_and))
            dve.tensor_copy(digit.rearrange("p d t k -> p (d t k)"), digit_u.rearrange("p d t k -> p (d t k)"))
            link(dve.tensor_copy(sif.rearrange("p t h n -> p (t h n)"), si.rearrange("p t h n -> p (t h n)")))
            for d in range(2):
                place_, picked = digit[:, d, :, :].rearrange("p t (h n) -> p t h n", h=PH), pick
                key = sif.rearrange("p t (h d) a -> p t h d a", d=2)[:, :, :, d, :]
                for a in range(PTOP):
                    ins = dve.scalar_tensor_tensor(picked[:, :, :, :, a], place_, float(a), key[:, :, :, a:a + 1].broadcast_to([P, TT, PH, PTOP]),
                                                   ALU.is_equal, ALU.mult)
                link(ins)
                link(dve.reduce_sum(ids[:, d, :, :].rearrange("p t (h n) -> p t h n", h=PH), picked, AX))
            dve.wait_ge(S("gate_exp"), 1)
            gs = gsum.rearrange("p (t h) -> p t h", t=TT)
            gr = grec.rearrange("p (t h) -> p t h", t=TT)
            link(dve.reduce_sum(gs, gate, AX))
            link(dve.reciprocal(grec, gsum))
            dve.tensor_tensor(gate, gate, gr.unsqueeze(3).broadcast_to([P, TT, PH, PTOP]), ALU.mult).then_inc(S("ids_ready"), 1)
            dve.wait_ge(S("GIJ_ready"), 2)
            with dve.Fori(0, T // 8) as i:
                t0 = i * 8
                for q in range(8):
                    if q % 4 == 0:
                        dve.wait_ge(S("gates_mm"), t0 + (q + 4))
                        n = 3 - q // 4
                        nc.vector.tensor_tensor(right[:, q:q + n, :], wide(cst("iota"), n), each(GIJ[:, 2, bass.ds(t0 + q, n)], P),
                                                ALU.is_equal).then_inc(S("right_ready"), 1)
                    nc.vector.tensor_scalar(left[:, q, :], cst("iota"), GIJ[:, 1, bass.ds(t0 + q, 1)], GIJ[:, 0, bass.ds(t0 + q, 1)],
                                            ALU.is_equal, ALU.mult).then_inc(S("left_ready"), 1)

            dve.wait_ge(S("x_hi_ready"), 1)
            dve.tensor_tensor(x_lo, Hv, x_hi, ALU.subtract).then_inc(S("x_lo_ready"), 1)

            def rest_u(q, j):
                dve.wait_ge(S("u_hi_ready"), j + 1)
                nc.vector.tensor_tensor(peer_unit(q, 0, ring_parts), peer_unit(q, 0), u_hi, ALU.subtract).then_inc(S("u_lo_ready"), 1)

            def rest_v(q, j):
                dve.wait_ge(S("v_hi_ready"), j + 1)
                nc.vector.tensor_tensor(peer_unit(q, 1, ring_parts), peer_unit(q, 1), v_hi, ALU.subtract).then_inc(S("v_lo_ready"), 1)

            def weigh(q, j, first=False):
                w = act_e[:, q % 2, :]
                dve.wait_ge(S("gelu_ready"), j + 1)
                nc.vector.tensor_tensor(w.unsqueeze(1), w.unsqueeze(1), G[:, bass.ds(j, 1), :], ALU.mult).then_inc(S("weighed"), 1)
                if not first:
                    dve.wait_ge(S("peer_pair_done"), j - 1)
                dve.wait_ge(S("weighed"), j + 1)
                nc.vector.tensor_copy(wgt_hi[:, q % 2, :], w).then_inc(S("wgt_hi_ready"), 1)
                dve.wait_ge(S("wgt_hi_ready"), j + 1)
                nc.vector.tensor_tensor(wgt_lo[:, q % 2, :], w, wgt_hi[:, q % 2, :], ALU.subtract).then_inc(S("wgt_ready"), 1)

            rest_u(0, 0)
            rest_u(1, 1)
            weigh(0, 0, True)
            rest_v(0, 0)
            rest_u(2, 2)
            weigh(1, 1, True)
            rest_v(1, 1)
            with dve.Fori(0, PKEYS // RING - 1) as i:
                for q in range(1, RING + 1):
                    rest_u((q + 2) % RING, i * RING + (q + 2))
                    weigh((q + 1) % RING, i * RING + (q + 1))
                    rest_v((q + 1) % RING, i * RING + (q + 1))
            rest_u(3, PKEYS - 1)
            for q in (2, 3):
                weigh(q, PKEYS - RING + q)
                rest_v(q, PKEYS - RING + q)
            dve.wait_ge(S("ux_ready"), PKEYS)
            link(dve.tensor_tensor(gain2, v("final_norm_g", 0, 8), v("final_norm_g", 0, 8), ALU.mult))
            dve.tensor_copy(fg2, each(gain2, P)).then_inc(S("fg2_ready"), 1)
            dve.wait_ge(S("peer_pair_done"), PKEYS)
            for n in range(8):
                dve.scalar_tensor_tensor(Xv[:, n, :], bank[n // 2][:, (n % 2) * T:(n % 2 + 1) * T], mod3[:, 40 + n, 0:1], Xv[:, n, :],
                                         ALU.mult, ALU.add).then_inc(S("x2_ready"), 1)
            dve.wait_ge(S("stdx_ready"), base("stdx_ready") + 1)
            dve.wait_ge(S("x2_ready"), base("x2_ready") + 8)
            link(dve.reciprocal(rsx[:, 0:T], rsx[:, 0:T]))
            link(dve.scalar_tensor_tensor(rsx[:, T:2 * T], bank[7][:, 0:T], 1.0 / D, rsx[:, 0:T], ALU.mult, ALU.mult))
            dve.tensor_tensor(rsx[:, T:2 * T], rsx[:, T:2 * T], rsx[:, 0:T], ALU.mult).then_inc(S("ms_mix_ready"), 1)
            dve.tensor_tensor(fg_mix, v("final_norm_g", 0, 8), v("norm_mix_g", 0, 8), ALU.mult).then_inc(S("fg_mix_ready"), 1)
            dve.tensor_tensor(lbd, v("lb", 0, 4), v("lb", 4, 4), ALU.subtract).then_inc(S("lbd_ready"), 1)
            dve.wait_ge(S("stdx_ready"), base("stdx_ready") + 2)
            dve.wait_ge(S("fg_mix_ready"), 1)
            link(dve.reciprocal(rsx[:, T:2 * T], rsx[:, T:2 * T]))
            link(dve.tensor_tensor(rsx[:, T:2 * T], rsx[:, T:2 * T], rsx[:, 0:T], ALU.mult))
            for k in range(KT):
                dve.scalar_tensor_tensor(Hv[:, k, :], Xv[:, k, :], fg_mix[:, k:k + 1], rsx[:, T:2 * T], ALU.mult, ALU.mult).then_inc(S("H3_ready"), 1)
            dve.wait_ge(S("H3_ready"), base("H3_ready") + KT)
            for k in range(KT):
                dve.scalar_tensor_tensor(Xv[:, k, :], Xv[:, k, :], v("final_norm_g", k), rsx[:, 0:T], ALU.mult, ALU.mult).then_inc(S("x2n_ready"), 1)
            dve.wait_ge(S("lb_ready"), 1)
            link(dve.tensor_scalar(lb1, lb, -1.0, 1.0, ALU.mult, ALU.add))
            for i in range(4):
                ins = dve.tensor_scalar(ff[:, i, :], ff[:, i, :], lb1[:, i:i + 1], lb[:, i:i + 1], ALU.mult, ALU.add)
            ins.then_inc(S("f_ready"), 1)
            dve.wait_ge(S("f_ready"), 1)
            dve.tensor_scalar(kk, ff, -1.0, 1.0, ALU.mult, ALU.add).then_inc(S("kk_ready"), 1)
            dve.wait_ge(S("stdm_ready"), base("stdm_ready") + 1)
            link(dve.reciprocal(rsm, rsm))
            for k in range(KT):
                ins = dve.scalar_tensor_tensor(memn[:, k, :], memn[:, k, :], v("norm_mem_g", k), rsm, ALU.mult, ALU.mult)
            ins.then_inc(S("memn_ready"), 1)
            dve.wait_ge(S("logf_ready"), 1)
            for i in range(4 * TT):
                ins = dve.tensor_tensor_scan(cum[:, i * P:(i + 1) * P], ones, DE[:, i * P:(i + 1) * P], 0.0, ALU.mult, ALU.add)
            link(ins)
            dve.memset(QE, 0.0)
            dve.memset(KE, 0.0)
            link(dve.memset(scT, 0.0))
            dve.wait_ge(S("masks_in"), 16)
            dve.wait_ge(S("kk_ready"), 1)
            dve.wait_ge(S("taken2"), 8)
            kkf, qqf = (x.rearrange("p c t -> p (c t)") for x in (kk, qq))
            sc8 = scT.rearrange("p h t n -> p (h t) n")

            dve.wait_ge(S("h3_hi_ready"), 1)
            dve.tensor_tensor(h_lo, Hv, h_hi, ALU.subtract).then_inc(S("h3_lo_ready"), 1)

            def rest2(m):
                n = SECOND.index(BETWEEN[m])
                dve.wait_ge(S("w2_hi_ready"), m + 1)
                dve.tensor_tensor(second_unit(n, ring_parts), second_unit(n), w_hi[m % 2], ALU.subtract).then_inc(S("w2_lo_ready"), 1)

            def take_level(n, mask):
                dve.wait_ge(S("level_mm"), n + 1)
                for b in range(2):
                    ins = dve.copy_predicated(sc8[:, 4 * b:4 * b + 4, :], wide(mask, 4).bitcast(U32), three(bank[4 + b][:], 4))
                ins.then_inc(S("level_taken"), 1)

            for lev in range(LEVELS + 1):
                half = 1 << lev
                a, b = ([x.rearrange("p (m z n) -> p m z n", z=2, n=half)[:, :, z, :] for x in (cum, DE, QE, KE, kkf, qqf)]
                        for z in range(2))
                cum0, D0, _, K0, k0, _ = a
                cum1, D1, Q1, _, _, q1 = b
                ref = cum0[:, :, half - 1:half].broadcast_to([P, 4 * T // (2 * half), half])
                if lev >= 1:
                    dve.wait_ge(S("qke_ready"), lev)
                dve.tensor_tensor(D0, ref, cum0, ALU.subtract)
                if lev < LEVELS:
                    ins = dve.tensor_tensor(D1, cum1, ref, ALU.subtract)
                else:
                    ins = dve.tensor_copy(D1, cum1)
                ins.then_inc(S("dist_ready"), 1)
                if lev >= 1:
                    rest2(3 * lev - 2)
                    take_level(lev - 1, masks[:, lev - 1, :])
                    rest2(3 * lev - 1)
                dve.wait_ge(S("decay_ready"), lev + 1)
                dve.tensor_tensor(K0, k0, D0, ALU.mult)
                dve.tensor_tensor(Q1, q1, D1, ALU.mult).then_inc(S("qke_ready"), 1)
                rest2(3 * lev)
                if lev == 4:
                    dve.wait_ge(S("taken2"), SECOND_ACT.index(("cg", 3)) + 1)
                    dve.memset(up[:, :, 0:CONV_K - 1], 0.0)
                    dve.tensor_tensor(up[:, :, CONV_K - 1:], caT, sgate, ALU.mult).then_inc(S("up_ready"), 1)
            rest2(3 * LEVELS + 1)
            rest2(3 * LEVELS + 2)
            take_level(LEVELS, ident)
            dve.wait_ge(S("up_ready"), 1)
            convolve(dve, range(CONV_DVE), "taps")
            dve.wait_ge(S("taps"), CONV_DVE * CONV_K)
            dve.wait_ge(S("pool_taps"), (4 - CONV_DVE) * (2 * CONV_K - 1))
            dve.tensor_copy(mean[:, 0:1], cv[:, 0, 0:1]).then_inc(S("conv_ready"), 1)
            for n in range(2):
                dve.wait_ge(S("stdh_ready"), base("stdh_ready") + n + 1)
                link(dve.reciprocal(rsh[:, n * 512:(n + 1) * 512], rsh[:, n * 512:(n + 1) * 512]))
                o_ = och[:, 2 * n:2 * n + 2, :]
                link(dve.scalar_tensor_tensor(o_, o_, v("onorm_g"), three(rsh[:, n * 512:(n + 1) * 512], 2), ALU.mult, ALU.mult))
                ins = dve.tensor_tensor(o_, o_, gg[:, 2 * n:2 * n + 2, :], ALU.mult)
                ins.then_inc(S("och_normed"), 2)
            dve.wait_ge(S("meanc_ready"), base("meanc_ready") + 1)
            link(dve.tensor_scalar(mean, bank[6][:, 0:T], 1.0 / CC, None, ALU.mult))
            dve.tensor_tensor(cv, cv, wide(mean, 4), ALU.subtract).then_inc(S("conv_centred"), 1)
            dve.wait_ge(S("stdc_ready"), base("stdc_ready") + 1)
            link(dve.reciprocal(rstdc, rstdc))
            dve.wait_ge(S("conv_centred"), 1)
            dve.tensor_tensor(cv, cv, wide(rstdc, 4), ALU.mult).then_inc(S("conv_normed"), 1)
            for i in range(4):
                second_done(dve, "ho", i)
                dve.tensor_tensor(grs[:, 2 * i:2 * i + 2, :], grs[:, 2 * i:2 * i + 2, :], three(second_bank("ho", i)[:], 2), ALU.mult).then_inc(S("merge_taken"), 1)
            for i in range(4):
                second_done(dve, "co", i)
                dve.tensor_tensor(gcs[:, 2 * i:2 * i + 2, :], gcs[:, 2 * i:2 * i + 2, :], three(second_bank("co", i)[:], 2), ALU.mult).then_inc(S("merge_taken"), 1)
                dve.wait_ge(S("merge_taken"), 5 + i)
                dve.tensor_tensor(gcs[:, 2 * i:2 * i + 2, :], gcs[:, 2 * i:2 * i + 2, :], grs[:, 2 * i:2 * i + 2, :], ALU.add).then_inc(S("merged"), 1)
            dve.wait_ge(S("x2n_ready"), base("x2n_ready") + KT)
            for i in range(8):
                second_done(dve, "mix", i)
                dve.tensor_tensor(Xv[:, i, :], second_bank("mix", i)[:, 0:T], Xv[:, i, :], ALU.add).then_inc(S("x3_ready"), 1)
            dve.wait_ge(S("stdn_ready"), base("stdn_ready") + 1)
            link(dve.reciprocal(rsn, rsn))
            dve.wait_ge(S("x3_ready"), base("x3_ready") + 8)
            for k in range(KT):
                dve.scalar_tensor_tensor(Hv[:, k, :], Xv[:, k, :], v("norm_xa_g", k), rsn, ALU.mult, ALU.mult).then_inc(S("H4_ready"), 1)
            for h in range(4):
                c = slice(2 * h, 2 * h + 2)
                dve.wait_ge(S("xscores_ready"), base("xscores_ready") + h + 1)
                link(dve.reduce_max(xmx[:, c], three(bank[4 + h % 2][:], 2), AX))
                dve.tensor_scalar(xnmx[:, c], xmx[:, c], -1.0 / 16.0, None, ALU.mult).then_inc(S("xmax_ready"), 1)
            for h in range(4):
                c = slice(2 * h, 2 * h + 2)
                dve.wait_ge(S("xexp_ready"), base("xexp_ready") + h + 1)
                link(dve.reciprocal(xri[:, c], xrs[:, c]))
                dve.tensor_tensor(xP[:, h, :, :], xP[:, h, :, :], each(xri[:, c], T), ALU.mult).then_inc(S("xP_ready"), 1)
            for h in range(4):
                dve.wait_ge(S("xpv_ready"), base("xpv_ready") + h + 1)
                dve.tensor_copy(xo[:, 2 * h:2 * h + 2, :], three(bank[4 + h % 2][:], 2)).then_inc(S("xo_taken"), 1)
            for i in range(8):
                second_done(dve, "xo", i)
                dve.tensor_tensor(Xv[:, i, :], second_bank("xo", i)[:, 0:T], Xv[:, i, :], ALU.add).then_inc(S("x4_ready"), 1)
            dve.memset(zeros, 0.0).then_inc(S("zeros5_ready"), 1)
            dve.wait_ge(S("std5_ready"), base("std5_ready") + 1)
            link(dve.reciprocal(rs5, rs5))
            dve.wait_ge(S("x4_ready"), base("x4_ready") + 8)
            for k in range(KT):
                dve.scalar_tensor_tensor(Hv[:, k, :], Xv[:, k, :], v("norm_ffn_g", k), rs5, ALU.mult, ALU.mult).then_inc(S("H5_ready"), 1)
            link(dve.memset(g8, -3.0e38))
            dve.wait_ge(S("logits_mm"), 1)
            dve.wait_ge(S("router_in"), 32)
            link(dve.tensor_tensor(logit, three(bank[7][:, 0:72], TT), wide(r_b, TT), ALU.add))
            link(dve.tensor_copy(g8[:, :, 0:GROUPS], logit[:, :, 0:GROUPS]))
            for tt in range(TT):
                ins = dve.max(gm8[:, tt, :], g8[:, tt, :])
            link(ins)
            for tt in range(TT):
                dve.max_index(gi8[:, tt, :], gm8[:, tt, :], g8[:, tt, :])
            link(dve.tensor_tensor(gex, logit[:, :, 0:GROUPS], gm8[:, :, 0:1].broadcast_to([P, TT, GROUPS]), ALU.subtract))
            ins = dve.tensor_copy(gif, gi8[:, :, 0:1])
            ins.then_inc(S("shifted5"), 1)
            dve.wait_ge(S("shifted5"), 1)
            link(dve.tensor_tensor(grp, wide(cst("iota")[:, 0:GROUPS], TT), gif.broadcast_to([P, TT, GROUPS]), ALU.is_equal))
            el = logit[:, :, GROUPS:].rearrange("p t (g e) -> p t g e", g=GROUPS)
            link(dve.tensor_tensor(prod, el, grp.unsqueeze(3).broadcast_to([P, TT, GROUPS, PER_GROUP]), ALU.mult))
            for tt in range(TT):
                ins = dve.reduce_sum(i8[:, tt, :], prod[:, tt, :, :].rearrange("p g e -> p e g"), AX)
            link(ins)
            for tt in range(TT):
                ins = dve.max(em8[:, tt, :], i8[:, tt, :])
            link(ins)
            for tt in range(TT):
                ins = dve.max_index(ei8[:, tt, :], em8[:, tt, :], i8[:, tt, :])
            link(ins)
            dve.tensor_tensor(e21.unsqueeze(2), em8[:, :, 1:2], em8[:, :, 0:1], ALU.subtract).then_inc(S("shifted5"), 1)
            link(dve.tensor_copy(eif, ei8[:, :, 0:2]))
            dve.scalar_tensor_tensor(eid, gif.broadcast_to([P, TT, TOP_K]), float(PER_GROUP), eif, ALU.mult, ALU.add).then_inc(S("eid_ready"), 1)
            dve.wait_ge(S("exp5_ready"), 1)
            dve.wait_ge(S("eid_ready"), 1)
            link(dve.reduce_sum(gsm, gex, AX))
            link(dve.scalar_tensor_tensor(den, e21, 1.0, gsm, ALU.add, ALU.mult))
            link(dve.reciprocal(w12[:, :, 0], den))
            link(dve.tensor_tensor(w12[:, :, 1], w12[:, :, 0], e21, ALU.mult))
            for tt in range(TT):
                ins = dve.tensor_scalar(chosen[:, tt, :], cst("iota")[:, 0:EXPERTS], eid[:, tt, 0:1], None, ALU.is_equal)
                dve.tensor_scalar(weight[:, tt, :], cst("iota")[:, 0:EXPERTS], eid[:, tt, 0:1], w12[:, tt, 0:1], ALU.is_equal, ALU.mult)
            oh, ohw = three(scr[:, 0:64], TT), three(scr[:, 72:136], TT)
            for tt in range(TT):
                dve.tensor_scalar(oh[:, tt, :], cst("iota")[:, 0:EXPERTS], eid[:, tt, 1:2], None, ALU.is_equal)
                ins = dve.tensor_scalar(ohw[:, tt, :], cst("iota")[:, 0:EXPERTS], eid[:, tt, 1:2], w12[:, tt, 1:2], ALU.is_equal, ALU.mult)
            link(ins)
            dve.tensor_tensor(chosen, chosen, oh, ALU.add).then_inc(S("chosen_ready"), 1)
            dve.tensor_tensor(weight, weight, ohw, ALU.add).then_inc(S("weight_ready"), 1)
            dve.wait_ge(S("places_mm"), 1)
            dve.tensor_scalar(cmp4, cst("iota")[:, 0:4], float(CAP), None, ALU.mult)
            dve.tensor_copy(place, three(bank[6][:, 0:64], TT))
            link(dve.reduce_max(most, bank[6][:, 64:96], AX))
            link(dve.tensor_scalar(cmp4, cmp4, most, None, ALU.is_lt))
            link(dve.reduce_sum(rnd, cmp4, AX))
            dve.tensor_copy(rounds, rnd).then_inc(S("rounds_ready"), 1)
            dve.wait_ge(S("rounds_ready"), 1)
            dve.wait_ge(S("weight_ready"), 1)
            n = dve.value_load(rounds[0:1, :], min_val=1, max_val=4)
            iota_cap = cst("iota")[:, 0:CAP]

            def one_hot(out, scale, p):
                for tt in range(TT):
                    for a in range(2):
                        e = slice(2 * p + a, 2 * p + a + 1) if isinstance(p, int) else bass.ds(p * 2 + a, 1)
                        ins = nc.vector.tensor_scalar(out[:, tt, a * CAP:(a + 1) * CAP], iota_cap, place[:, tt, e], scale[:, tt, e],
                                                      ALU.is_equal, ALU.mult)
                return ins

            def select(q, p):
                dve.wait_ge(S("gather_mm"), q)
                one_hot(sel, chosen, p).then_inc(S("sel_ready"), 1)

            def middle(q, p):
                one_hot(selw, weight, p).then_inc(S("selw_ready"), 1)
                dve.wait_ge(S("silu_ready"), q + 1)
                dve.wait_ge(S("up_mm"), q + 1)
                nc.vector.tensor_tensor(hid, silu, bank[5][:], ALU.mult).then_inc(S("hid_ready"), 1)
                dve.wait_ge(S("turn_mm"), q + 1)
                nc.vector.tensor_copy(hidT.rearrange("p k n -> p (k n)"), bank[4][:]).then_inc(S("hidT_ready"), 1)
                dve.wait_ge(S("selT_mm"), q + 1)
                nc.vector.tensor_copy(selwT, bank[5][:, 0:T]).then_inc(S("selwT_ready"), 1)

            with dve.Fori(0, n) as r:
                q0 = r * 16
                one_hot(sel, chosen, 0).then_inc(S("sel_ready"), 1)
                with dve.Fori(0, EXPERTS // 2 - 1) as i:
                    select(q0 + i + 1, i + 1)
                    middle(q0 + i, i)
                middle(q0 + 15, 15)
                nc.vector.tensor_scalar(place, place, -float(CAP), None, ALU.add).then_inc(S("place_moved"), 1)
                dve.wait_ge(S("place_moved"), r + 1)
            dve.wait_ge(S("round_done"), n)
            for m in range(4):
                h_ = slice((m % 2) * 512, (m % 2 + 1) * 512)
                dve.tensor_tensor(x5[:, m // 2, h_], bank[m][:], x_tok[:, m // 2, h_], ALU.add).then_inc(S("x5_ready"), 1)
            dve.wait_ge(S("final_in"), 16)
            for tt in range(TT):
                dve.wait_ge(S("std6_ready"), base("std6_ready") + tt + 1)
                link(dve.reciprocal(ri5[:, tt:tt + 1], ss5[:, tt:tt + 1]))
                dve.scalar_tensor_tensor(x5[:, tt, :], x5[:, tt, :], ri5[:, tt:tt + 1], fin_g, ALU.mult, ALU.mult).then_inc(S("out_ready"), 1)


def lay_out(inputs):
    g = {k: np.asarray(a) for k, a in inputs.items()}

    def features(a):
        a = a.T
        return np.ascontiguousarray(a.reshape(-1, P, a.shape[1]).transpose(1, 0, 2)).reshape(P, -1)

    def tiles(w, width=P):
        k, n = w.shape
        return np.ascontiguousarray(w.reshape(k // P, P, n // width, width).transpose(2, 1, 0, 3)).reshape(n // width, P, -1)

    def rows(w):
        e, k, n = w.shape
        return np.ascontiguousarray(w.reshape(e, k // P, P, n).transpose(0, 2, 1, 3)).reshape(e, P, -1)

    def col(a):
        return a.reshape(-1, P).T

    o = {}
    o["xT"], o["ctxT"], o["memT"] = features(g["x"][0]), features(g["ctx"][0]), features(g["mem_2"][0])
    o["cT"] = np.ascontiguousarray(np.stack([col(g["c"][0]), col(g["c_ctx"])], 2)).reshape(P, 16)
    vec = {"b_mod": col(g["b_mod"][0])}
    for n in ("norm1_g", "norm2_g"):
        vec[n] = col(g[n][0])
    vec["final_norm_g"] = col(g["final_norm_g"])
    for n in ("norm_mix_g", "norm_xa_g", "norm_mem_g", "norm_ffn_g", "conv_b", "conv_ln_g", "conv_ln_b"):
        vec[n] = col(g[n + "_2"][0])
    vec["lb"] = np.concatenate([col(g["hgrn_lb_logits_2"][0]), col(g["hgrn_lb_logits_2"][1])], 1)
    vec["onorm_g"], vec["subln_g"] = col(g["hgrn_onorm_g_2"][0]), col(g["diff_subln_g"][0])
    vec["gq_g"] = np.tile(g["gqa_q_norm_g"][0], 2)[:, None]
    vec["gk_g"] = np.tile(g["gqa_k_norm_g"][0], 2)[:, None]
    for n, k in (("lam_q", "q"), ("lam_k", "k")):
        vec[n] = np.zeros((P, 2), np.float32)
        vec[n][:HD, 0], vec[n][:HD, 1] = g[f"diff_l{k}1"][0], g[f"diff_l{k}2"][0]
    vec["conv_w"] = np.ascontiguousarray(g["conv_w_2"][0].reshape(CONV_K, 4, P).transpose(2, 1, 0)).reshape(P, -1)
    o["vec"] = np.concatenate([vec[n] for n in VEC], 1)
    heads = [0, 4, 1, 5, 2, 6, 3, 7]
    w_in = tiles(g["w_in"][0])
    gq = g["w_in"][0][:, 1536:2048].reshape(D, 8, HD)[:, heads].reshape(D, 512)
    first = {"mod": tiles(g["w_mod"][0]), "dq": w_in[0:4], "dk": w_in[4:8], "dv": w_in[8:12], "gq": tiles(gq),
             "gk": w_in[16:17], "gv": w_in[17:18]}
    w_out = g["w_out"][0]
    w_out = np.concatenate([w_out[:512], w_out[512:].reshape(8, HD, D)[heads].reshape(512, D)])
    first["out"], first["wq"] = tiles(w_out), tiles(g["peer_wq"][0])
    o["first"] = pairs([first[what][i] for what, i in FIRST])
    o["mod_rest"] = pairs(list(first["mod"][16:16 + MOD_REST]))
    o["subkeys"] = np.ascontiguousarray(g["peer_subkeys"][0].reshape(16, PKEYS, P).transpose(2, 0, 1)).reshape(P, 2048)
    u = g["peer_u"][0].reshape(PKEYS, PKEYS, KT, P).transpose(1, 3, 2, 0).reshape(PKEYS, P, 1, UNIT)
    w = g["peer_v"][0].reshape(PKEYS, PKEYS, 1, D).transpose(1, 0, 2, 3)
    o["peer"] = np.concatenate([u, w], 2).reshape(PKEYS, P, 2 * UNIT)
    s, at = g["w_in_2"][0], 0
    second = {}
    for n, w in (("ca", 512), ("cg", 512), ("q", 512), ("f", 512), ("i", 512), ("g", 512), ("gc", 1024), ("gr", 1024)):
        second[n] = tiles(s[:, at:at + w])
        at += w
    second["co"], second["ho"] = tiles(g["conv_w_out_2"][0], 256), tiles(g["hgrn_w_out_2"][0], 256)
    for n, k in (("mix", "w_mix_out_2"), ("xq", "xa_w_q_2"), ("xk", "xa_w_k_2"), ("xv", "xa_w_v_2"), ("xo", "xa_w_o_2")):
        second[n] = tiles(g[k][0])
    o["second"] = pairs([second[what][i] for what, i in SECOND])
    o["moe_gate"] = rows(g["moe_w_gate_2"][0])
    o["moe_up"] = rows(g["moe_w_up_2"][0])
    o["moe_down"] = rows(g["moe_w_down_2"][0])
    o["router_w"] = np.ascontiguousarray(np.concatenate([g["router_group_w_2"][0], g["router_expert_w_2"][0]], 1)
                                         .reshape(KT, P, 36).transpose(1, 0, 2)).reshape(P, -1)
    o["router_b"] = np.concatenate([g["router_group_b_2"][0], g["router_expert_b_2"][0]])[None]
    o["final_g"] = g["final_norm_g_2"][None]
    c = {"ident": np.eye(P), "ones": np.ones((P, P)), "halves": np.kron(np.eye(2), np.ones((HD, HD)))}
    r = np.arange(P)
    swap = np.zeros((P, P))
    first_half = r % 32 < 16
    swap[r[first_half] + 16, r[first_half]] = -1.0
    swap[r[~first_half] - 16, r[~first_half]] = 1.0
    c["swap"] = swap
    freq = (np.float32(10000.0) ** (-np.arange(16, dtype=np.float32) / np.float32(16))).astype(np.float32)
    tok = np.arange(T)
    grid = np.where(((r // 32) % 2 == 0)[:, None], (tok // 64)[None], (tok % 64)[None]).astype(np.float32)
    ang = (grid * freq[r % 16][:, None]).astype(np.float32)
    c["cos"], c["sin"] = np.cos(ang), np.sin(ang)
    c["iota"] = np.tile(np.arange(P), (P, 1))
    c["before"] = (r[:, None] < r[None]) * 1.0
    o["const"] = np.concatenate([c[n] for n in CONST], 1).astype(np.float32)
    masks = []
    for lev in range(LEVELS):
        half = 1 << lev
        same = (r[:, None] // (2 * half)) == (r[None] // (2 * half))
        masks.append(same & (r[:, None] % (2 * half) < half) & (r[None] % (2 * half) >= half))
    o["masks"] = np.concatenate(masks, 1).astype(np.float32)
    return o


def pairs(units):
    a = np.stack(units).reshape(len(units) // 2, 2, P, UNIT).transpose(0, 2, 1, 3)
    return np.ascontiguousarray(a).reshape(len(units) // 2, P, 2 * UNIT)


def kernel(**inputs):
    import concourse.bacc as bacc
    from concourse.bass_utils import run_bass_kernel_spmd
    nc = bacc.Bacc("TRN2", target_bir_lowering=False, num_devices=1)
    arrays, dram = {}, {}
    for name, a in lay_out(inputs).items():
        arrays[f"in_{name}_dram"] = a
        dram[name] = nc.dram_tensor(f"in_{name}_dram", a.shape, F32, kind="ExternalInput").ap()
    dram["out"] = nc.dram_tensor("out_dram", (T, D), F32, kind="ExternalOutput").ap()
    build(nc, dram)
    r = run_bass_kernel_spmd(nc, [arrays], core_ids=[0])
    return r.results[0]["out_dram"].reshape(1, T, D)
```
